# Optimizing a Trainium2 kernel written in Bass

```python
import jax, jax.numpy as jnp
from jax import lax
import numpy as np

D_MODEL = 1024
BATCH = 1
SEQ = 256
DEPTH = 2
DEC_BATCH = 8
DEC_SEQ = 16
PAST_LEN = 256

CHUNK = 64
R_HEADS = 8
R_DK = 128
R_DV = 256
A_HEADS = 8
A_DH = 128
BAND_CHUNKS = 8
BAND_ROWS = BAND_CHUNKS * CHUNK
REL_CLIP = 128
D_FF = 4 * D_MODEL
ROPE_BASE = 10000.0
EPS = 1e-6
NEG_INF = -1e30
R_QK = R_HEADS * R_DK
R_V = R_HEADS * R_DV
A_W = A_HEADS * A_DH
IN_SPLITS = (R_QK, R_QK, R_V, R_V, A_W, A_W, A_W, D_MODEL, D_MODEL)
D_IN = R_QK * 2 + R_V * 2 + A_W * 3 + D_MODEL * 2

kernel_name = "hybrid_retention_chunkband_stream_step"

def rmsnorm(x, g):
    xf = x.astype(jnp.float32)
    y = xf * lax.rsqrt(jnp.mean(xf * xf, axis=-1, keepdims=True) + EPS)
    return (y * g.astype(jnp.float32)).astype(x.dtype)

def rotary(x, pos):
    half = x.shape[-1] // 2
    inv = ROPE_BASE ** (-jnp.arange(half, dtype=jnp.float32) / half)
    ang = pos.astype(jnp.float32)[:, None] * inv[None, :]
    cos = jnp.cos(ang)[None, :, None, :]
    sin = jnp.sin(ang)[None, :, None, :]
    xf = x.astype(jnp.float32)
    x1, x2 = xf[..., :half], xf[..., half:]
    return jnp.concatenate([x1 * cos - x2 * sin, x1 * sin + x2 * cos], axis=-1).astype(x.dtype)

def log_gamma():
    return jnp.log(1.0 - 2.0 ** (-5.0 - jnp.arange(R_HEADS, dtype=jnp.float32)))

def retention_chunk(q, k, v, S):
    q = q.astype(jnp.float32)
    k = k.astype(jnp.float32)
    v = v.astype(jnp.float32)
    S = S.astype(jnp.float32)
    T = q.shape[1]
    lg = log_gamma()
    idx = jnp.arange(T, dtype=jnp.float32)
    dist = idx[:, None] - idx[None, :]
    causal = dist >= 0
    dmask = jnp.where(causal[None], jnp.exp(lg[:, None, None] * jnp.where(causal, dist, 0.0)[None]), 0.0)
    scores = jnp.einsum('bihd,bjhd->bhij', q, k) * dmask[None]
    o = jnp.einsum('bhij,bjhv->bihv', scores, v)
    cross = jnp.exp(lg[None, :] * (idx[:, None] + 1.0))
    o = o + jnp.einsum('bihd,bhdv->bihv', q, S) * cross[None, :, :, None]
    kdec = k * jnp.exp(lg[None, :] * (T - 1.0 - idx[:, None]))[None, :, :, None]
    S_new = S * jnp.exp(lg * T)[None, :, None, None] + jnp.einsum('bjhd,bjhv->bhdv', kdec, v)
    return o, S_new

def retention_prompt(q, k, v):
    B, T = q.shape[:2]
    nc = T // CHUNK

    def to_chunks(a):
        return jnp.moveaxis(a.reshape(B, nc, CHUNK, *a.shape[2:]), 1, 0)

    def step(S, qkv):
        qc, kc, vc = qkv
        o, S = retention_chunk(qc, kc, vc, S)
        return S, o

    S0 = jnp.zeros((B, R_HEADS, R_DK, R_DV), jnp.float32)
    S, o = lax.scan(step, S0, (to_chunks(q), to_chunks(k), to_chunks(v)))
    o = jnp.moveaxis(o, 0, 1).reshape(B, T, R_HEADS, R_DV)
    return o, S

def retention_out(o, z, gn_g):
    B, T = o.shape[:2]
    of = o.astype(jnp.float32)
    of = of * lax.rsqrt(jnp.mean(of * of, axis=-1, keepdims=True) + EPS)
    of = of.reshape(B, T, R_V) * gn_g.astype(jnp.float32)
    return (jax.nn.silu(z.astype(jnp.float32)) * of).astype(z.dtype)

def rel_bias_lookup(rel_bias, qpos, kpos):
    d = jnp.clip(qpos[:, None] - kpos[None, :], -REL_CLIP, REL_CLIP) + REL_CLIP
    return rel_bias[:, d].astype(jnp.float32)

def band_attend(q, k, v, bias, valid):
    s = jnp.einsum('bqhd,bkhd->bhqk', q.astype(jnp.float32), k.astype(jnp.float32)) * (A_DH ** -0.5)
    s = jnp.where(valid[None, None, None, :], s + bias[None], NEG_INF)
    p = jax.nn.softmax(s, axis=-1)
    return jnp.einsum('bhqk,bkhd->bqhd', p, v.astype(jnp.float32)).astype(q.dtype)

def att_mix_prompt(q, k, v, rbias):
    B, T = q.shape[:2]
    nc = T // CHUNK
    band = BAND_ROWS + CHUNK
    kp = jnp.pad(k, ((0, 0), (BAND_ROWS, 0), (0, 0), (0, 0)))
    vp = jnp.pad(v, ((0, 0), (BAND_ROWS, 0), (0, 0), (0, 0)))
    qc = jnp.moveaxis(q.reshape(B, nc, CHUNK, A_HEADS, A_DH), 1, 0)
    r_q = jnp.arange(CHUNK, dtype=jnp.int32)
    r_k = jnp.arange(band, dtype=jnp.int32)
    bias = rel_bias_lookup(rbias, r_q + BAND_ROWS, r_k)

    def one(args):
        ci, qi = args
        start = ci * CHUNK
        kb = lax.dynamic_slice_in_dim(kp, start, band, axis=1)
        vb = lax.dynamic_slice_in_dim(vp, start, band, axis=1)
        valid = (start - BAND_ROWS + r_k) >= 0
        return band_attend(qi, kb, vb, bias, valid)

    o = lax.map(one, (jnp.arange(nc, dtype=jnp.int32), qc))
    o = jnp.moveaxis(o, 0, 1).reshape(B, T, A_W)
    keep = min(BAND_ROWS, T)
    return o, k[:, T - keep:], v[:, T - keep:]

def att_mix_sample(q, k, v, rbias, ck, cv):
    B, T = q.shape[:2]
    pk = ck.shape[1]
    kall = jnp.concatenate([ck.astype(k.dtype), k], axis=1)
    vall = jnp.concatenate([cv.astype(v.dtype), v], axis=1)
    qpos = PAST_LEN + jnp.arange(T, dtype=jnp.int32)
    kpos = jnp.concatenate([PAST_LEN - pk + jnp.arange(pk, dtype=jnp.int32), qpos])
    bias = rel_bias_lookup(rbias, qpos, kpos)
    valid = jnp.ones((pk + T,), dtype=bool)
    o = band_attend(q, kall, vall, bias, valid).reshape(B, T, A_W)
    return o, k, v

def trunk_layer(x, c, pos, lp, ret_mix, att_mix):
    (w_ada, b_ada, g_mix, g_ffn, w_in, gn_g, qn_g, kn_g, rbias,
     w_br_ret, w_br_att, w_out, w_up, w_down) = lp
    mods = jax.nn.silu(c) @ w_ada + b_ada
    sh1, sc1, gt1, sh2, sc2, gt2 = [t[:, None, :] for t in jnp.split(mods, 6, axis=-1)]
    B, T = x.shape[:2]
    h = rmsnorm(x, g_mix) * (1.0 + sc1) + sh1
    u = h @ w_in
    q_r, k_r, v_r, z_r, q_a, k_a, v_a, m_r, m_a = jnp.split(u, list(np.cumsum(IN_SPLITS)[:-1]), axis=-1)
    qr = rotary(q_r.reshape(B, T, R_HEADS, R_DK), pos) * (R_DK ** -0.5)
    kr = rotary(k_r.reshape(B, T, R_HEADS, R_DK), pos)
    vr = v_r.reshape(B, T, R_HEADS, R_DV)
    o_r, s_new = ret_mix(qr, kr, vr)
    y_r = retention_out(o_r, z_r, gn_g)
    qa = rmsnorm(q_a.reshape(B, T, A_HEADS, A_DH), qn_g)
    ka = rmsnorm(k_a.reshape(B, T, A_HEADS, A_DH), kn_g)
    va = v_a.reshape(B, T, A_HEADS, A_DH)
    y_a, k_rows, v_rows = att_mix(qa, ka, va, rbias)
    mixed = jax.nn.sigmoid(m_r) * (y_r @ w_br_ret) + jax.nn.sigmoid(m_a) * (y_a @ w_br_att)
    x = x + gt1 * (mixed @ w_out)
    h2 = rmsnorm(x, g_ffn) * (1.0 + sc2) + sh2
    x = x + gt2 * (jnp.square(jax.nn.relu(h2 @ w_up)) @ w_down)
    return x, s_new.astype(x.dtype), k_rows, v_rows

def setup_inputs(seed: int = 0) -> dict:
    key = jax.random.key(seed)
    ks = jax.random.split(key, 24)
    past_keep = min(BAND_ROWS, PAST_LEN)
    n = jax.random.normal
    f = jnp.float32
    return {
        "x_prompt": n(ks[0], (BATCH, SEQ, D_MODEL), f),
        "x_sample": n(ks[1], (DEC_BATCH, DEC_SEQ, D_MODEL), f),
        "state_ret": n(ks[2], (DEPTH, DEC_BATCH, R_HEADS, R_DK, R_DV), f),
        "cache_attn_k": n(ks[3], (DEPTH, DEC_BATCH, past_keep, A_HEADS, A_DH), f),
        "cache_attn_v": n(ks[4], (DEPTH, DEC_BATCH, past_keep, A_HEADS, A_DH), f),
        "c_prompt": n(ks[5], (BATCH, D_MODEL), f),
        "c_sample": n(ks[6], (DEC_BATCH, D_MODEL), f),
        "w_ada": n(ks[7], (DEPTH, D_MODEL, 6 * D_MODEL), f) * (0.3 * D_MODEL ** -0.5),
        "b_ada": n(ks[8], (DEPTH, 6 * D_MODEL), f) * 0.02,
        "norm_mix_g": 1.0 + 0.02 * n(ks[9], (DEPTH, D_MODEL), f),
        "norm_ffn_g": 1.0 + 0.02 * n(ks[10], (DEPTH, D_MODEL), f),
        "w_in": n(ks[11], (DEPTH, D_MODEL, D_IN), f) * D_MODEL ** -0.5,
        "ret_gn_g": 1.0 + 0.02 * n(ks[12], (DEPTH, R_V), f),
        "q_norm_g": 1.0 + 0.02 * n(ks[13], (DEPTH, A_DH), f),
        "k_norm_g": 1.0 + 0.02 * n(ks[14], (DEPTH, A_DH), f),
        "rel_bias": 0.5 * n(ks[15], (DEPTH, A_HEADS, 2 * REL_CLIP + 1), f),
        "w_br_ret": n(ks[16], (DEPTH, R_V, D_MODEL), f) * R_V ** -0.5,
        "w_br_att": n(ks[17], (DEPTH, A_W, D_MODEL), f) * A_W ** -0.5,
        "w_out": n(ks[18], (DEPTH, D_MODEL, D_MODEL), f) * D_MODEL ** -0.5,
        "w_up": n(ks[19], (DEPTH, D_MODEL, D_FF), f) * D_MODEL ** -0.5,
        "w_down": n(ks[20], (DEPTH, D_FF, D_MODEL), f) * D_FF ** -0.5,
    }

def reference(x_prompt, x_sample, state_ret, cache_attn_k, cache_attn_v, c_prompt, c_sample,
              w_ada, b_ada, norm_mix_g, norm_ffn_g, w_in, ret_gn_g, q_norm_g, k_norm_g, rel_bias,
              w_br_ret, w_br_att, w_out, w_up, w_down):
    pos_p = jnp.arange(x_prompt.shape[1], dtype=jnp.int32)
    pos_s = PAST_LEN + jnp.arange(x_sample.shape[1], dtype=jnp.int32)
    xp, xs = x_prompt, x_sample
    rs_p, kp_l, vp_l, rs_s, ks_l, vs_l = [], [], [], [], [], []
    for l in range(DEPTH):
        lp = (w_ada[l], b_ada[l], norm_mix_g[l], norm_ffn_g[l], w_in[l], ret_gn_g[l],
              q_norm_g[l], k_norm_g[l], rel_bias[l], w_br_ret[l], w_br_att[l], w_out[l],
              w_up[l], w_down[l])
        xp, s_p, k_p, v_p = trunk_layer(xp, c_prompt, pos_p, lp, retention_prompt, att_mix_prompt)
        s_in = state_ret[l]
        ck, cv = cache_attn_k[l], cache_attn_v[l]
        xs, s_s, k_s, v_s = trunk_layer(
            xs, c_sample, pos_s, lp,
            lambda q, k, v: retention_chunk(q, k, v, s_in),
            lambda q, k, v, rb: att_mix_sample(q, k, v, rb, ck, cv))
        rs_p.append(s_p); kp_l.append(k_p); vp_l.append(v_p)
        rs_s.append(s_s); ks_l.append(k_s); vs_l.append(v_s)
    ret_state_prompt = jnp.stack(rs_p, axis=0)
    att_k_prompt = jnp.stack(kp_l, axis=0)
    att_v_prompt = jnp.stack(vp_l, axis=0)
    ret_state_sample = jnp.stack(rs_s, axis=0)
    att_k_sample = jnp.stack(ks_l, axis=0)
    att_v_sample = jnp.stack(vs_l, axis=0)
    return (xp, xs, ret_state_prompt, att_k_prompt, att_v_prompt, ret_state_sample, att_k_sample, att_v_sample)


_drawn_inputs = setup_inputs


def setup_inputs(seed=0):
    import zlib

    import numpy as np

    out = dict(_drawn_inputs(seed))
    spreads = {}
    factors = {'cache_attn_k': 4.889,
     'cache_attn_v': 3.839,
     'norm_ffn_g': 7.393,
     'ret_gn_g': 8.0,
     'q_norm_g': 8.0,
     'k_norm_g': 2.911,
     'rel_bias': 5.593}
    for name, (base, spread) in spreads.items():
        noise = np.random.default_rng([zlib.crc32(name.encode()), seed]).standard_normal(out[name].shape)
        drawn = base * np.exp(spread * noise) if base else spread * noise
        out[name] = __import__('jax').numpy.asarray(drawn.astype(out[name].dtype))
    for name, factor in factors.items():
        out[name] = (out[name] * factor).astype(out[name].dtype)
    return out
```

```python
from contextlib import ExitStack, contextmanager

import numpy as np
import concourse.bass as bass
from concourse import mybir
from concourse.alu_op_type import AluOpType as ALU

F32 = mybir.dt.float32
F32R = mybir.dt.float32r
ACT = mybir.ActivationFunctionType
AXX = mybir.AxisListType.X

P = 128
DM, DEPTH, HEADS, DH, DV, FF = 1024, 2, 8, 128, 256, 4096
SEQ, SB, ST, PAST, CHUNK, CLIP = 256, 8, 16, 256, 64, 128
TOK = SEQ + SB * ST
NT, KT = TOK // P, DM // P
PR = SEQ
NSEQ = 1 + SB
RQK, RV, AW = HEADS * DH, HEADS * DV, HEADS * DH
D_IN = 2 * RQK + 2 * RV + 3 * AW + 2 * DM
C_QR, C_KR, C_VR, C_ZR = 0, RQK, 2 * RQK, 2 * RQK + RV
C_QA = C_ZR + RV
C_KA, C_VA, C_MR, C_MA = C_QA + AW, C_QA + 2 * AW, C_QA + 3 * AW, C_QA + 3 * AW + DM
EPS, NEG = 1e-6, -1e30
BK, BC = 4, 256
RAW, SPLIT = 4, 2
W_DEC = 592
DC_K, DC_SEQ, DC_S, DC_ROW = 512, 514, 522, 528
B_Q0, B_Q1, B_C, B_N, W_BIAS = 0, 128, 384, 640, 768
BAND = 400
BAND_TOP = PAST + ST - 1
ADA_C, ADA_STEPS = 512, 12
H0, M0, F0 = 4, 4, 30


def tables():
    half = DH // 2
    inv = np.float32(10000.0) ** (-np.arange(half, dtype=np.float32) / np.float32(half))
    pos = np.concatenate([np.arange(SEQ), np.tile(PAST + np.arange(ST), SB)]).astype(np.float32)
    ang = (pos[:, None] * inv[None, :]).astype(np.float32)
    cos = np.cos(ang).reshape(NT, P, half)
    sin = np.sin(ang).reshape(NT, P, half)
    rope = np.stack([cos, -sin, sin], axis=2).transpose(1, 0, 2, 3)
    dec = np.zeros((HEADS, P, W_DEC), np.float64)
    p = np.arange(P)[:, None]
    i = np.arange(SEQ)[None, :]
    for h in range(HEADS):
        lg = np.float64(np.log(np.float32(1.0 - 2.0 ** (-5.0 - h))))
        s = DH ** -0.5
        dec[h, :, 0:256] = np.where(i >= p, np.exp(lg * np.maximum(i - p, 0)), 0) * s
        dec[h, :, 256:384] = dec[h, :, 0:128]
        q = np.arange(P)[None, :]
        same = (q // ST == p // ST) & (q >= p)
        dec[h, :, 384:512] = np.where(same, np.exp(lg * np.maximum(q - p, 0)), 0) * s
        dec[h, :, DC_K] = np.exp(lg * (SEQ - 1 - p[:, 0]))
        dec[h, :, DC_K + 1] = np.exp(lg * (SEQ - 1 - P - p[:, 0]))
        for b in range(SB):
            dec[h, :, DC_SEQ + b] = np.where(p[:, 0] // ST == b, np.exp(lg * (ST - 1 - p[:, 0] % ST)), 0)
        dec[h, :, DC_S] = np.exp(lg * ST)
        dec[h, :, DC_ROW:DC_ROW + 64] = np.tile(np.exp(lg * (np.arange(ST) + 1)), 4)[None, :] * s
    return np.ascontiguousarray(rope, np.float32), dec.astype(np.float32)


def plan(groups):
    uses, ready, out = [0] * 4, 0, []
    for banks, last in groups:
        entries = []
        for n, b in enumerate(banks):
            if n < len(banks) - 1:
                ready += 1
                entries.append((b, uses[b], "ready", ready))
            else:
                entries.append((b, uses[b], "block", last + 1 + SPLIT))
            uses[b] += 1
        out.append(entries)
    return out, uses, ready


class Stage:
    def __init__(self, turns, blocks, groups, **more):
        self.turns, self.blocks = turns, blocks
        self.groups, self.uses, self.ready = plan(groups)
        self.adds = {"blk": blocks, "round": blocks // RAW, "ready": self.ready, **more,
                     **{f"bank{b}": self.uses[b] for b in range(4)}}


S_V = Stage(2, 4, [((0, 1, 2), 1), ((3, 0, 1), 3)])
S_HEAD = Stage(HEADS, 8, [((0, 1, 2), 1), ((3, 0, 1), 3), ((2, 3, 0), 5), ((1, 2), 7)], head=1, ada=1)
S_MERGE = Stage(2, 20, [g for c in (0, 10) for g in (((0, 1), c + 1), ((2, 3), c + 5), ((0, 1), c + 7), ((2, 3), c + 9))], mix=4)
S_OUT = Stage(2, 4, [((0, 1), 1), ((2, 3), 3)], res=4)
S_UP = Stage(8, 4, [((0, 1), 1), ((2, 3), 3)], ff=4)
S_DOWN = Stage(4, 8, [((0, 1), 7)], res=2)


class Counts:

    NAMES = ("blk", "round", "ready", "bank0", "bank1", "bank2", "bank3", "head", "norm", "ada", "mix", "ff",
             "res", "own")

    def __init__(self, eng, own, names):
        self.eng, self.own_sem = eng, own
        self.regs = {}
        for n in self.NAMES:
            if n in names:
                self.regs[n] = eng.alloc_register(f"count_{n}")
                eng.reg_mov(self.regs[n], 0)

    @contextmanager
    def turn(self, adds, use=None):
        names = [n for n in self.regs if (use is None and adds.get(n)) or n == "own" or (use and n in use)]
        self.now = {n: self.eng.snap(self.regs[n]) for n in names}
        self.mine = 0
        yield self
        for n, r in self.regs.items():
            k = self.mine if n == "own" else adds.get(n, 0)
            if k:
                self.eng.reg_add(r, r, k)

    def __getattr__(self, n):
        return self.now[n]

    def op(self, ins):
        self.mine += 1
        return ins.then_inc(self.own_sem, 1)

    def settle(self):
        self.eng.wait_ge(self.own_sem, self.now["own"] + self.mine)


def trunk(nc, x_prompt, x_sample, state_ret, cache_attn_k, cache_attn_v, c_prompt, c_sample, w_ada,
          b_ada, norm_mix_g, norm_ffn_g, w_in, ret_gn_g, q_norm_g, k_norm_g, rel_bias, w_br_ret,
          w_br_att, w_out, w_up, w_down, rope, decay, y_prompt, y_sample, st_prompt, k_prompt,
          v_prompt, st_sample, k_sample, v_sample):
    ctx = ExitStack()

    def sem(name):
        return ctx.enter_context(nc.semaphore(name))

    def sb(name, shape, dt=F32, stack=ctx):
        return stack.enter_context(nc.sbuf_tensor(name, shape, dt))

    raw = sb("raw", [P, RAW, BK, BC])
    whi = sb("whi", [P, SPLIT, BK, BC], F32R)
    wlo = sb("wlo", [P, SPLIT, BK, BC], F32R)
    xT = sb("xT", [P, KT, TOK])
    hhi = sb("hhi", [P, KT, TOK], F32R)
    hlo = sb("hlo", [P, KT, TOK], F32R)
    ada_w = sb("ada_w", [P, 2, 2, ADA_C])
    ada_b = sb("ada_b", [1, ADA_C])
    ada_s = sb("ada_s", [P, P])
    modT = sb("modT", [P, 6 * KT, NSEQ])
    modA = sb("modA", [P, KT, NSEQ])
    cT = sb("cT", [P, KT, 32])
    gT = sb("gT", [P, 64])
    gqk = sb("gqk", [P, DEPTH, 2 * DH])
    rope_t = sb("rope_t", [P, NT, 3, DH // 2])
    ident = sb("ident", [P, P])
    ones = sb("ones", [P, P])
    eps_t = sb("eps_t", [P, 1])
    mhalf = sb("mhalf", [P, 8])
    qa_par = sb("qa_par", [P, 2, P])
    qr_par = sb("qr_par", [P, 2, P])
    p_par = sb("p_par", [P, 2, 2, P])
    gcol = sb("gcol", [P, 2])
    small = sb("small", [P, 64])
    qk_ms, qk_rs = small[:, 0:6], small[:, 8:14]
    negmax, rowsum, rinv = small[:, 16:19], small[:, 20:23], small[:, 24:27]
    o_ms, o_rs, qk_ss, o_ss = small[:, 28:31], small[:, 32:35], small[:, 36:42], small[:, 44:47]

    ystack = ExitStack()
    y_ret = sb("y_ret", [P, 2 * HEADS, TOK], stack=ystack)
    y_att = sb("y_att", [P, HEADS, TOK], stack=ystack)
    hstack = ExitStack()
    vaT = sb("va_tok", [P, NT, AW], stack=hstack)
    kc = sb("kc", [P, 2, 2, 4, DH], stack=hstack)
    kcT = sb("kcT", [P, 4, PAST], stack=hstack)
    vc = sb("vc", [P, 2, SB, DH], stack=hstack)
    st = sb("st", [P, SB, DV], stack=hstack)
    bias = sb("bias", [P, W_BIAS], stack=hstack)
    dec = sb("dec", [P, W_DEC], stack=hstack)
    qkA = sb("qkA", [P, NT, 2 * DH], stack=hstack)
    qkZ = sb("qkZ", [P, 2 * TOK], stack=hstack)
    qkR = sb("qkR", [P, NT, 2 * DH], stack=hstack)
    tmp = sb("tmp", [P, NT * 2 * DH], stack=hstack)
    vR = sb("vR", [P, NT, DV], stack=hstack)
    qaT = sb("qaT", [P, TOK], stack=hstack)
    kaT = sb("kaT", [P, TOK], stack=hstack)
    qrT = sb("qrT", [P, SEQ + P], stack=hstack)
    krT = sb("krT", [P, TOK], stack=hstack)
    prob = sb("prob", [P, W_BIAS], stack=hstack)
    pT = sb("pT", [P, 512], stack=hstack)
    sdT = sb("sdT", [P, 512], stack=hstack)
    kdec = sb("kdec", [P, 2, DH], stack=hstack)
    oa = sb("oa", [P, NT, DH], stack=hstack)
    stp = sb("stp", [P, DV], stack=hstack)
    kdm = kcT[:, :, :].rearrange("p a b -> p (a b)").rearrange("p (b d) -> p b d", b=SB)
    rraw = qkZ[:, :].rearrange("p (t c) -> p t c", t=NT)
    zs = qkZ[:, :].rearrange("p (n t) -> p n t", n=2)
    onorm = prob[:, :].rearrange("p (t v) -> p t v", t=NT)
    hstack.close()
    nstack = ExitStack()
    sq = sb("sq", [P, 2, TOK], stack=nstack)
    hn = sb("hn", [P, 2, TOK], stack=nstack)
    hf = sb("hf", [P, 2, TOK], stack=nstack)
    std = sb("std", [P, TOK], stack=nstack)
    rstd = sb("rstd", [P, TOK], stack=nstack)
    nstack.close()
    xstack = ExitStack()
    xtok = sb("xtok", [P, NT, DM], stack=xstack)
    crow = sb("crow", [NSEQ, DM], stack=xstack)
    csil = sb("csil", [NSEQ, DM], stack=xstack)
    grow = sb("grow", [64, P], stack=xstack)
    rbrow = sb("rbrow", [DEPTH * HEADS, 2 * CLIP + 1], stack=xstack)
    band = sb("band", [DEPTH * HEADS, BAND], stack=xstack)
    neg = sb("neg", [P, P], stack=xstack)
    xstack.close()
    bstack = ExitStack()
    yhi = sb("yhi", [P, 3 * HEADS, TOK], F32R, stack=bstack)
    ylo = sb("ylo", [P, 3 * HEADS, TOK], F32R, stack=bstack)
    bstack.close()
    ystack.close()
    mstack = ExitStack()
    mhi = sb("mhi", [P, KT, TOK], F32R, stack=mstack)
    mlo = sb("mlo", [P, KT, TOK], F32R, stack=mstack)
    gate = sb("gate", [P, 2, TOK], stack=mstack)
    part = sb("part", [P, 2, TOK], stack=mstack)
    mix = sb("mix", [P, 2, TOK], stack=mstack)
    rtm = sb("rtm", [P, 2, TOK], stack=mstack)
    mstack.close()
    fstack = ExitStack()
    fhi = sb("fhi", [P, FF // P, TOK], F32R, stack=fstack)
    flo = sb("flo", [P, FF // P, TOK], F32R, stack=fstack)
    frelu = sb("frelu", [P, 2, TOK], stack=fstack)
    fsq = sb("fsq", [P, 2, TOK], stack=fstack)
    rtf = sb("rtf", [P, 2, TOK], stack=fstack)
    fstack.close()

    G = [ctx.enter_context(nc.psum_tensor(f"G{b}", [P, 512], F32)) for b in range(4)]
    X = [ctx.enter_context(nc.psum_tensor(f"X{b}", [P, 512], F32)) for b in range(4)]

    band_d = nc.dram_tensor("band_d", [DEPTH * HEADS, BAND], F32, kind="Internal").ap()
    bias_d = nc.dram_tensor("bias_d", [DEPTH * HEADS, P, W_BIAS], F32, kind="Internal").ap()

    raw_full = [sem(f"raw_full{s}") for s in range(RAW)]
    blk_hi = sem("blk_hi")
    blk_split = sem("blk_split")
    blk_used = sem("blk_used")
    acc_ready = sem("acc_ready")
    acc_free = [sem(f"acc_free{b}") for b in range(4)]
    act_own, dve_own, pool_own = sem("act_own"), sem("dve_own"), sem("pool_own")
    ada_full = [sem(f"ada_full{s}") for s in range(2)]
    ada_bfull, ada_used, ada_mm, ada_cp, ada_tr, mod_ready = (
        sem(n) for n in ("ada_bfull", "ada_used", "ada_mm", "ada_cp", "ada_tr", "mod_ready"))
    sq_ready, sq_used, std_ready, hn_ready, hp_ready, hf_ready, hhi_ready, h_ready = (
        sem(n) for n in ("sq_ready", "sq_used", "std_ready", "hn_ready", "hp_ready", "hf_ready", "hhi_ready", "h_ready"))
    ld_x, ld_c, ld_g, ld_rb, ld_k, consts = (sem(n) for n in ("ld_x", "ld_c", "ld_g", "ld_rb", "ld_k", "consts"))
    band_ready, band_out, mask_out, band_in = (sem(n) for n in ("band_ready", "band_out", "mask_out", "band_in"))
    csil_ready, pre_pe, pre_d, pre_a = (sem(n) for n in ("csil_ready", "pre_pe", "pre_d", "pre_a"))
    kc_full = [sem(f"kc_full{e}") for e in range(2)]
    vc_full, st_full, bias_full, dec_full = (sem(n) for n in ("vc_full", "st_full", "bias_full", "dec_full"))
    va_out, ka_out, st_out, stp_out, y_out = (sem(n) for n in ("va_out", "ka_out", "st_out", "stp_out", "y_out"))
    qk_msr, qk_pow, qk_norm, ta_done, qa_ev, ka_ev = (
        sem(n) for n in ("qk_msr", "qk_pow", "qk_norm", "ta_done", "qa_ev", "ka_ev"))
    kt_done = [sem(f"kt_done{e}") for e in range(2)]
    kt_a = [sem(f"kt_a{e}") for e in range(2)]
    kt_d = [sem(f"kt_d{e}") for e in range(2)]
    sp_done, sn_done, ss_done, sp_read, ss_read, max_ready, exp_done = (
        sem(n) for n in ("sp_done", "sn_done", "ss_done", "sp_read", "ss_read", "max_ready", "exp_done"))
    rope_ready, tr_done, qr_ev, kr_ev, rs_done, sd_ready = (
        sem(n) for n in ("rope_ready", "tr_done", "qr_ev", "kr_ev", "rs_done", "sd_ready"))
    pt_done, pt_a, pt_d, pv_done, oa_ready, oaT_done, oaT_ev = (
        sem(n) for n in ("pt_done", "pt_a", "pt_d", "pv_done", "oa_ready", "oaT_done", "oaT_ev"))
    o_done, oss_ready, o_msr, o_pow, on_ready, orT_done, orT_ev = (
        sem(n) for n in ("o_done", "oss_ready", "o_msr", "o_pow", "on_ready", "orT_done", "orT_ev"))
    kdec_ready, kdm_ready, stp_done, stp_ev, pair_done, pair_ev = (
        sem(n) for n in ("kdec_ready", "kdm_ready", "stp_done", "stp_ev", "pair_done", "pair_ev"))
    yhi_ready, y_ready, mix_ready, mhi_ready, m_ready = (
        sem(n) for n in ("yhi_ready", "y_ready", "mix_ready", "mhi_ready", "m_ready"))
    dma_go = sem("dma_go")
    f_hi, f_ready, res_ready, fin_pe, fin_a, fin_d = (
        sem(n) for n in ("f_hi", "f_ready", "res_ready", "fin_pe", "fin_a", "fin_d"))

    block = ctx.enter_context(nc.Block())

    def seqs(ap):
        return ap.rearrange("p (b t) -> p b t", b=SB)

    def par(ap, e):
        return ap.rearrange("p (g e t) -> p g e t", g=4, e=2)[:, :, e, :]

    @block.sync
    def _(sp):
        cnt = Counts(sp, None, ("blk",))
        sp.dma_start(xtok[:, 0:2, :], x_prompt[0].rearrange("(t p) d -> p t d", p=P)).then_inc(ld_x, 16)
        sp.dma_start(xtok[:, 2, :], x_sample.rearrange("b t d -> (b t) d")).then_inc(ld_x, 16)

        def load(c, j, parts):
            sp.wait_ge(blk_split, c.blk + (j + 1))
            off = 0
            for src in parts:
                w = src.shape[-1]
                sp.dma_start(raw[:, j % RAW, :, off:off + w], src.rearrange("(k p) n -> p k n", p=P))\
                    .then_inc(raw_full[j % RAW], 32 // len(parts))
                off += w

        def rows(w, l, k, c, n=BC):
            return w[l, k * BK * P:(k + 1) * BK * P, bass.ds(c, n)]

        with sp.Fori(0, DEPTH) as l:
            with sp.Fori(0, S_V.turns) as i, cnt.turn(S_V.adds) as c:
                for j in range(4):
                    load(c, j, [rows(w_in, l, j % 2, i * (2 * BC) + (C_VA + j // 2 * BC))])
            with sp.Fori(0, HEADS) as h, cnt.turn(S_HEAD.adds) as c:
                for j in range(2):
                    load(c, j, [rows(w_in, l, j, h * DH + C_QA, DH), rows(w_in, l, j, h * DH + C_KA, DH)])
                for j in range(2):
                    load(c, 2 + j, [rows(w_in, l, j, h * DH + C_QR, DH), rows(w_in, l, j, h * DH + C_KR, DH)])
                for j in range(2):
                    load(c, 4 + j, [rows(w_in, l, j, h * DV + C_VR)])
                for j in range(2):
                    load(c, 6 + j, [rows(w_in, l, j, h * DV + C_ZR)])
            with sp.Fori(0, S_MERGE.turns) as i, cnt.turn(S_MERGE.adds) as c:
                j = 0
                for g in range(2):
                    for w, base, ks in ((w_in, C_MR, 2), (w_br_ret, 0, 4), (w_in, C_MA, 2), (w_br_att, 0, 2)):
                        for k in range(ks):
                            load(c, j, [rows(w, l, k, i * (2 * BC) + (base + g * BC))])
                            j += 1
            with sp.Fori(0, S_OUT.turns) as i, cnt.turn(S_OUT.adds) as c:
                for j in range(4):
                    load(c, j, [rows(w_out, l, j % 2, i * (2 * BC) + j // 2 * BC)])
            with sp.Fori(0, S_UP.turns) as i, cnt.turn(S_UP.adds) as c:
                for j in range(4):
                    load(c, j, [rows(w_up, l, j % 2, i * (2 * BC) + j // 2 * BC)])
            with sp.Fori(0, S_DOWN.turns) as i, cnt.turn(S_DOWN.adds) as c:
                for j in range(8):
                    load(c, j, [rows(w_down, l, j, i * BC)])
        with cnt.turn({}, use=("blk",)) as c:
            load(c, 0, [w_in[0, 0:BK * P, 0:BC]])
        sp.wait_ge(fin_a, 3)
        sp.wait_ge(fin_d, 3)
        sp.dma_start(y_prompt[0].rearrange("(t p) d -> p t d", p=P), xtok[:, 0:2, :]).then_inc(y_out, 16)
        sp.dma_start(y_sample.rearrange("b t d -> (b t) d"), xtok[:, 2, :]).then_inc(y_out, 16)
        sp.wait_ge(y_out, 32)
        sp.wait_ge(raw_full[0], (DEPTH * 184 // RAW + 1) * 32)

    @block.gpsimd
    def _(pool):
        g = nc.gpsimd
        cnt = Counts(pool, pool_own, ("head", "norm", "ada", "own"))
        for m in (ident, ones, eps_t, mhalf, cT, qa_par, qr_par, p_par, neg):
            value = {"ones": 1.0, "eps_t": EPS, "mhalf": -0.5, "neg": NEG}.get(m.name, 0.0)
            ap = m[:, :] if len(m.shape) == 2 else m[:, :, :] if len(m.shape) == 3 else m[:, :, :, :]
            g.memset(ap, value).then_inc(pool_own, 1)
        pool.wait_ge(pool_own, 9)
        g.affine_select(out=ident[:, :], in_=ident[:, :], compare_op=ALU.not_equal, fill=1.0, base=0,
                        pattern=[[-1, P]], channel_multiplier=1).then_inc(consts, 1)
        pool.reg_add(cnt.regs["own"], cnt.regs["own"], 9)

        lh = DEPTH * HEADS
        for rows_, c0, n in ((CHUNK, B_Q0 + CHUNK, CHUNK), (CHUNK, B_Q1 + 3 * CHUNK, CHUNK), (P, B_N, P)):
            g.dma_start(bias_d[:, 0:rows_, c0:c0 + n].rearrange("l p n -> p l n"),
                        neg[0:rows_, 0:n].unsqueeze(1).to_broadcast([rows_, lh, n])).then_inc(mask_out, 16)
        pool.wait_ge(band_ready, 1)
        g.dma_start(band_d, band[:, :]).then_inc(band_out, 16)
        pool.wait_ge(band_out, 16)
        pool.wait_ge(mask_out, 48)

        def place(p0, n, c0, w, m0):
            src = bass.AP(tensor=band_d.tensor, offset=m0, ap=[[BAND, lh], [-1, n], [1, w]])
            g.dma_start(bias_d[:, p0:p0 + n, c0:c0 + w], src).then_inc(band_in, 16)

        at0 = BAND_TOP
        place(0, CHUNK, B_Q0, CHUNK, at0)
        place(CHUNK, CHUNK, B_Q0, P, at0 - CHUNK)
        place(0, CHUNK, B_Q1, 3 * CHUNK, at0 - P)
        place(CHUNK, CHUNK, B_Q1, SEQ, at0 - P - CHUNK)
        for b in range(SB):
            place(b * ST, ST, B_C, PAST, at0 - PAST)
            place(b * ST, ST, B_N + b * ST, ST, at0)

        def dma(out, in_):
            pool.sem_inc(dma_go, 1)
            return g.dma_start(out, in_)

        def ada_loads(c, l, s):
            pool.wait_ge(ada_mm, c.ada)
            dma(ada_b[:, :], b_ada[bass.ds(l, 1), bass.ds(s * ADA_C, ADA_C)]).then_inc(ada_bfull, 16)
            for q in range(4):
                pool.wait_ge(ada_used, c.ada * 4 + (q + 1))
                dma(ada_w[:, q % 2, :, :],
                            w_ada[l, q * 2 * P:(q + 1) * 2 * P, bass.ds(s * ADA_C, ADA_C)]
                            .rearrange("(k p) n -> p k n", p=P)).then_inc(ada_full[q % 2], 16)

        def norm_sample(c, shift):
            for k in range(KT):
                pool.wait_ge(hn_ready, c.norm * KT + (k + 1))
                pool.wait_ge(h_ready, c.norm * KT + (max(k - 1, 0) + H0))
                d = seqs(hf[:, k % 2, PR:TOK])
                c.op(g.tensor_tensor(d, seqs(hn[:, k % 2, PR:TOK]),
                                     modA[:, k, 1:NSEQ].unsqueeze(2).to_broadcast([P, SB, ST]), ALU.mult))
                c.settle()
                g.tensor_tensor(d, d, modT[:, shift * KT + k, 1:NSEQ].unsqueeze(2).to_broadcast([P, SB, ST]),
                                ALU.add).then_inc(hf_ready, 1)

        with pool.Fori(0, DEPTH) as l:
            with pool.Fori(0, 4) as s, cnt.turn({"ada": 1}) as c:
                ada_loads(c, l, s)
            with cnt.turn({"norm": 1}) as c:
                norm_sample(c, 0)
            with pool.Fori(0, HEADS) as h, cnt.turn({"head": 1, "ada": 1}) as c:
                H = c.head
                pool.wait_ge(kt_done[1], H)
                for e in range(2):
                    for t in range(2):
                        src = cache_attn_k[l, e:SB:2, t * P:(t + 1) * P, bass.ds(h, 1), :]
                        dma(kc[:, e, t, :, :], src.rearrange("b k h d -> k b (h d)")).then_inc(kc_full[e], 16)
                pool.wait_ge(ss_read, H)
                pool.wait_ge(sp_read, H)
                pool.wait_ge(band_in, 20 * 16)
                dma(bias[:, :], bias_d[bass.ds(l * HEADS + h, 1)].rearrange("a p n -> p (a n)")).then_inc(bias_full, 16)
                pool.wait_ge(pair_ev, H * 4)
                dma(dec[:, :], decay[bass.ds(h, 1)].rearrange("a p n -> p (a n)")).then_inc(dec_full, 16)
                pool.wait_ge(st_out, H * 16)
                for t in range(2):
                    dma(st[:, 4 * t:4 * t + 4, :], state_ret[l, 4 * t:4 * t + 4, bass.ds(h, 1), :, :]
                                .rearrange("b h d v -> d b (h v)")).then_inc(st_full, 16)
                pool.wait_ge(pv_done, H)
                for t in range(2):
                    src = cache_attn_v[l, :, t * P:(t + 1) * P, bass.ds(h, 1), :]
                    dma(vc[:, t, :, :], src.rearrange("b k h d -> k b (h d)")).then_inc(vc_full, 16)
                ada_loads(c, l, h + 4)
                pool.wait_ge(qk_msr, H + 1)
                g.tensor_tensor(qk_rs, qk_ms, mhalf[:, 0:6], ALU.pow).then_inc(qk_pow, 1)
                pool.wait_ge(qk_norm, H + 1)
                dma(k_prompt[l, 0, :, bass.ds(h, 1), :].rearrange("(t p) h d -> p t (h d)", p=P),
                            qkA[:, 0:2, DH:2 * DH]).then_inc(ka_out, 16)
                dma(k_sample[l, :, :, bass.ds(h, 1), :].rearrange("b t h d -> (b t) (h d)"),
                            qkA[:, 2, DH:2 * DH]).then_inc(ka_out, 16)
                pool.wait_ge(rope_ready, H + 1)
                pool.wait_ge(dec_full, H * 16 + 16)
                pool.wait_ge(stp_done, H)
                g.tensor_tensor(kdec[:, :, :], qkR[:, 0:2, DH:2 * DH],
                                dec[:, DC_K:DC_K + 2].unsqueeze(2).to_broadcast([P, 2, DH]), ALU.mult).then_inc(kdec_ready, 1)
                pool.wait_ge(ss_done, H + 1)
                g.tensor_tensor(kdm, qkR[:, 2:3, DH:2 * DH].to_broadcast([P, SB, DH]),
                                dec[:, DC_SEQ:DC_SEQ + SB].unsqueeze(2).to_broadcast([P, SB, DH]), ALU.mult).then_inc(kdm_ready, 1)
                pool.wait_ge(o_msr, H + 1)
                g.tensor_tensor(o_rs, o_ms, mhalf[:, 0:3], ALU.pow).then_inc(o_pow, 1)
                pool.wait_ge(stp_ev, H + 1)
                dma(st_prompt[l, 0, bass.ds(h, 1)].rearrange("a d v -> d (a v)"), stp[:, :]).then_inc(stp_out, 16)
                pool.wait_ge(pair_ev, H * 4 + 4)
                dma(st_sample[l, :, bass.ds(h, 1)].rearrange("b a d v -> d b (a v)"), st[:, :, :]).then_inc(st_out, 16)
            with cnt.turn({"norm": 1}) as c:
                norm_sample(c, 3)
        pool.wait_ge(va_out, DEPTH * 32)
        pool.wait_ge(ka_out, DEPTH * HEADS * 32)
        pool.wait_ge(stp_out, DEPTH * HEADS * 16)
        pool.wait_ge(st_out, DEPTH * HEADS * 16)

    @block.scalar
    def _(act):
        a = nc.scalar
        cnt = Counts(act, act_own, Counts.NAMES)
        act.dma_start(crow[0:1, :], c_prompt).then_inc(ld_c, 16)
        act.dma_start(crow[1:NSEQ, :], c_sample).then_inc(ld_c, 16)
        for l in range(DEPTH):
            for src, r, n in ((norm_mix_g, 0, KT), (norm_ffn_g, KT, KT), (ret_gn_g, 2 * KT, 2 * KT)):
                act.dma_start(grow[32 * l + r:32 * l + r + n, :], src[l].rearrange("(k p) -> k p", p=P)).then_inc(ld_g, 16)
            act.dma_start(gqk[:, l, 0:DH], q_norm_g[l].partition_broadcast(P)).then_inc(ld_k, 16)
            act.dma_start(gqk[:, l, DH:2 * DH], k_norm_g[l].partition_broadcast(P)).then_inc(ld_k, 16)
        act.dma_start(rbrow[:, :], rel_bias.rearrange("l h n -> (l h) n")).then_inc(ld_rb, 16)
        act.dma_start(rope_t[:, :, :, :], rope).then_inc(ld_k, 16)

        def copy(out, in_):
            return a.activation(out, in_, ACT.Copy)

        def high(c, j):
            act.wait_ge(raw_full[j % RAW], (c.round + j // RAW + 1) * 32)
            act.wait_ge(blk_used, c.blk + (j + 1))
            copy(whi[:, j % SPLIT, :, :], raw[:, j % RAW, :, :]).then_inc(blk_hi, 1)

        def acc(c, entry):
            _, _, kind, n = entry
            act.wait_ge(acc_ready, c.ready + n) if kind == "ready" else act.wait_ge(blk_used, c.blk + n)

        act.wait_ge(ld_c, 32)
        a.activation(csil[:, :], crow[:, :], ACT.Silu).then_inc(csil_ready, 1)
        for n in (1, 3, 5):
            act.wait_ge(pre_pe, n + 3)
            copy(xT[:, n % 2 * 4:n % 2 * 4 + 4, n // 2 * P:(n // 2 + 1) * P],
                 X[n % 4][:, :].rearrange("p (k t) -> p k t", k=4)).then_inc(pre_a, 1)

        def norm(c):
            act.wait_ge(res_ready, c.norm * KT)
            for k in range(KT):
                if k >= 2:
                    act.wait_ge(sq_used, c.norm * KT + (k - 1))
                a.activation(sq[:, k % 2, :], xT[:, k, :], ACT.Square).then_inc(sq_ready, 1)
            act.wait_ge(sq_used, c.norm * KT + KT)
            a.activation(std[:, :], X[0][:, 0:TOK], ACT.Sqrt, scale=1.0 / DM, bias=eps_t[:, 0:1]).then_inc(std_ready, 1)
            for k in range(KT):
                act.wait_ge(hf_ready, c.norm * KT + (k + 1))
                act.wait_ge(hp_ready, c.norm * KT + (k + 1))
                copy(hhi[:, k, :], hf[:, k % 2, :]).then_inc(hhi_ready, 1)

        act.wait_ge(pre_d, 5)
        act.wait_ge(consts, 1)
        with cnt.turn({}, use=("blk", "round")) as c:
            high(c, 0)
        with act.Fori(0, DEPTH) as l:
            with cnt.turn({"norm": 1}) as c:
                norm(c)
            with act.Fori(0, S_V.turns) as i, cnt.turn(S_V.adds) as c:
                for j in range(4):
                    high(c, j + 1)
                    if j % 2:
                        for t, e in enumerate(S_V.groups[j // 2]):
                            acc(c, e)
                            copy(vaT[:, t, bass.ds(i * (2 * BC) + j // 2 * BC, BC)],
                                 G[e[0]][:, 0:BC]).then_inc(acc_free[e[0]], 1)
            with cnt.turn({}, use=("bank0", "bank1", "bank3")) as c:
                for b in (0, 1, 3):
                    act.wait_ge(acc_free[b], c.now[f"bank{b}"])
                act.dma_start(v_prompt[bass.ds(l, 1), 0].rearrange("l (t p) h d -> p (l t) (h d)", p=P),
                              vaT[:, 0:2, :]).then_inc(va_out, 16)
                act.dma_start(v_sample[bass.ds(l, 1)].rearrange("l b t h d -> (l b t) (h d)"),
                              vaT[:, 2, :]).then_inc(va_out, 16)
            with act.Fori(0, HEADS) as h, cnt.turn(S_HEAD.adds) as c:
                H = c.head
                gr = S_HEAD.groups

                def out_of(group, dst):
                    for t, e in enumerate(group):
                        acc(c, e)
                        copy(dst[:, t, :], G[e[0]][:, 0:2 * DH]).then_inc(acc_free[e[0]], 1)

                high(c, 1)
                high(c, 2)
                act.wait_ge(ta_done, H)
                act.wait_ge(ka_out, H * 32)
                out_of(gr[0], qkA)
                high(c, 3)
                act.wait_ge(ta_done, H + 1)
                c.op(copy(qaT[:, :], X[0][:, 0:TOK]))
                c.op(copy(par(qa_par[:, 0, :], 0), par(X[0][:, PR:TOK], 0)))
                copy(par(qa_par[:, 1, :], 1), par(X[0][:, PR:TOK], 1)).then_inc(qa_ev, 1)
                act.wait_ge(kt_done[0], H + 1)
                act.wait_ge(pair_done, H * 4)
                copy(kcT[:, :, P:2 * P], X[3][:, :].rearrange("p (g k) -> p g k", g=4)).then_inc(kt_a[0], 1)
                high(c, 4)
                act.wait_ge(orT_ev, H * 2)
                out_of(gr[1], rraw)
                act.wait_ge(kt_done[1], H + 1)
                act.wait_ge(sn_done, H + 1)
                copy(kcT[:, :, P:2 * P], X[1][:, :].rearrange("p (g k) -> p g k", g=4)).then_inc(kt_a[1], 1)
                high(c, 5)
                act.wait_ge(tr_done, H + 1)
                copy(krT[:, :], X[1][:, 0:TOK]).then_inc(kr_ev, 1)
                high(c, 6)
                act.wait_ge(pair_done, H * 4)
                out_of(gr[2], vR)
                act.wait_ge(max_ready, H + 1)
                for n, (lo, w) in enumerate(((B_Q0, P), (B_Q1, SEQ), (B_C, PAST + P))):
                    a.activation(prob[:, lo:lo + w], prob[:, lo:lo + w], ACT.Exp, bias=negmax[:, n:n + 1],
                                 accum_out=rowsum[:, n:n + 1]).then_inc(exp_done, 1)
                act.wait_ge(pt_done, H + 1)
                for e in range(2):
                    c.op(copy(p_par[:, :, e, :].rearrange("p k (g e t) -> p k g e t", g=4, e=2)[:, :, :, e, :],
                              X[0][:, 0:2 * P].rearrange("p (k g e t) -> p k g e t", k=2, g=4, e=2)[:, :, :, e, :]))
                copy(pT[:, 0:2 * P], X[0][:, 2 * P:4 * P]).then_inc(pt_a, 1)
                high(c, 7)
                act.wait_ge(o_done, H + 1)
                for t, src in enumerate((X[2][:, 0:DV], X[2][:, DV:2 * DV], X[0][:, 0:DV])):
                    a.activation(onorm[:, t, :], src, ACT.Square, accum_out=o_ss[:, t:t + 1]).then_inc(oss_ready, 1)
                act.wait_ge(stp_done, H + 1)
                act.wait_ge(stp_out, H * 16)
                copy(stp[:, :], X[1][:, 0:DV]).then_inc(stp_ev, 1)
                high(c, 8)
                for n, e in enumerate(gr[3]):
                    acc(c, e)
                    a.activation(zs[:, n, :], G[e[0]][:, 0:TOK], ACT.Silu).then_inc(acc_free[e[0]], 1)
                act.wait_ge(oaT_done, H + 1)
                copy(y_att[:, bass.ds(h, 1), :].rearrange("p a t -> p (a t)"), X[3][:, 0:TOK]).then_inc(oaT_ev, 1)
            with cnt.turn({}, use=("head",)) as c:
                act.wait_ge(pair_ev, c.head * 4)
                act.wait_ge(orT_ev, c.head * 2)
                act.wait_ge(oaT_ev, c.head)
                act.wait_ge(st_out, c.head * 16)
                act.wait_ge(stp_out, c.head * 16)
                act.wait_ge(ka_out, c.head * 32)
                act.wait_ge(va_out, l * 32 + 32)
                for n in range(3 * HEADS):
                    src = y_ret[:, n, :] if n < 2 * HEADS else y_att[:, n - 2 * HEADS, :]
                    copy(yhi[:, n, :], src).then_inc(yhi_ready, 1)
                act.wait_ge(y_ready, l * (3 * HEADS) + 3 * HEADS)
            with act.Fori(0, S_MERGE.turns) as i, cnt.turn(S_MERGE.adds) as c:
                for j in range(20):
                    high(c, j + 1)
                    g, r = j // 10, j % 10
                    if r in (1, 7):
                        for e in (S_MERGE.groups[4 * g + 1] if r == 7 else S_MERGE.groups[3] if g else []):
                            act.wait_ge(acc_free[e[0]], c.now[f"bank{e[0]}"] + (e[1] + 1))
                        if r == 1 and not g:
                            for b in (2, 3):
                                act.wait_ge(acc_free[b], c.now[f"bank{b}"])
                        for n, e in enumerate(S_MERGE.groups[4 * g + (2 if r == 7 else 0)]):
                            acc(c, e)
                            a.activation(gate[:, n, :], G[e[0]][:, 0:TOK], ACT.Sigmoid).then_inc(acc_free[e[0]], 1)
                    if r == 9:
                        for n in range(2):
                            act.wait_ge(mix_ready, c.mix + (2 * g + n + 1))
                            copy(mhi[:, bass.ds(i * 4 + (2 * g + n), 1), :].rearrange("p a t -> p (a t)"),
                                 mix[:, n, :]).then_inc(mhi_ready, 1)
            with act.Fori(0, S_OUT.turns) as i, cnt.turn(S_OUT.adds) as c:
                for j in range(4):
                    high(c, j + 1)
            with cnt.turn({"norm": 1}) as c:
                norm(c)
            with act.Fori(0, S_UP.turns) as i, cnt.turn(S_UP.adds) as c:
                for j in range(4):
                    high(c, j + 1)
                    if j % 2:
                        for n, e in enumerate(S_UP.groups[j // 2]):
                            q = j // 2 * 2 + n
                            acc(c, e)
                            act.wait_ge(f_ready, c.ff + (q - 1 + F0))
                            a.activation(frelu[:, n, :], G[e[0]][:, 0:TOK], ACT.Relu).then_inc(acc_free[e[0]], 1)
                            act.wait_ge(acc_free[e[0]], c.now[f"bank{e[0]}"] + (e[1] + 1))
                            a.activation(fhi[:, bass.ds(i * 4 + q, 1), :].rearrange("p a t -> p (a t)"),
                                         frelu[:, n, :], ACT.Square).then_inc(f_hi, 1)
            with act.Fori(0, S_DOWN.turns) as i, cnt.turn(S_DOWN.adds) as c:
                for j in range(8):
                    high(c, j + 1)
        for n in (1, 3, 5):
            act.wait_ge(fin_pe, n + 1)
            copy(xtok[:, n // 2, 4 * P:8 * P], X[n % 4][:, :]).then_inc(fin_a, 1)
        act.wait_ge(va_out, DEPTH * 32)

    @block.vector
    def _(dve):
        v = nc.vector
        cnt = Counts(dve, dve_own, Counts.NAMES)
        dve.sem_inc(blk_split, RAW)
        dve.sem_inc(f_ready, F0)
        dve.sem_inc(h_ready, H0)
        dve.sem_inc(m_ready, M0)

        def low(c, j):
            dve.wait_ge(blk_hi, c.blk + (j + 1))
            v.tensor_tensor(wlo[:, j % SPLIT, :, :], raw[:, j % RAW, :, :],
                            whi[:, j % SPLIT, :, :].bitcast(F32), ALU.subtract).then_inc(blk_split, 1)

        def acc(c, entry):
            _, _, kind, n = entry
            dve.wait_ge(acc_ready, c.ready + n) if kind == "ready" else dve.wait_ge(blk_used, c.blk + n)

        def copied(c, group):
            for b, use, _, _ in group:
                dve.wait_ge(acc_free[b], c.now[f"bank{b}"] + (use + 1))

        dve.wait_ge(ld_rb, 16)
        far = BAND_TOP - CLIP + 1
        v.tensor_copy(band[:, 0:far], rbrow[:, 2 * CLIP:2 * CLIP + 1].to_broadcast([DEPTH * HEADS, far])).then_inc(dve_own, 1)
        v.tensor_copy(band[:, far:BAND], rbrow[:, 0:2 * CLIP][:, ::-1]).then_inc(band_ready, 1)
        dve.reg_add(cnt.regs["own"], cnt.regs["own"], 1)
        dve.wait_ge(pre_pe, 1)
        v.tensor_copy(gT[:, :], G[0][:, 0:64]).then_inc(pre_d, 1)
        dve.wait_ge(pre_pe, 2)
        v.tensor_copy(cT[:, :, 0:NSEQ], G[1][:, 0:KT * 16].rearrange("p (k b) -> p k b", k=KT)[:, :, 0:NSEQ]).then_inc(pre_d, 1)
        for n in (0, 2, 4):
            dve.wait_ge(pre_pe, n + 3)
            v.tensor_copy(xT[:, n % 2 * 4:n % 2 * 4 + 4, n // 2 * P:(n // 2 + 1) * P],
                          X[n % 4][:, :].rearrange("p (k t) -> p k t", k=4)).then_inc(pre_d, 1)
        dve.wait_ge(pre_a, 3)
        dve.wait_ge(ld_k, 80)

        def ada_rows(c):
            dve.wait_ge(ada_mm, c.ada + 1)
            v.tensor_copy(ada_s[:, :], X[2][:, 0:P]).then_inc(ada_cp, 1)

        def ada_cols(c, s):
            dve.wait_ge(ada_tr, c.ada + 1)
            v.tensor_copy(modT[:, bass.ds(s * 4, 4), :],
                          X[2][:, 0:P].rearrange("p (g b) -> p g b", g=4)[:, :, 0:NSEQ]).then_inc(mod_ready, 1)

        def norm(c, shift, gain):
            for_layer = gT[:, gain]
            c.op(v.scalar_tensor_tensor(out=modA[:, :, :], in0=modT[:, (shift + 1) * KT:(shift + 2) * KT, :], scalar=1.0,
                                        in1=for_layer.unsqueeze(2).to_broadcast([P, KT, NSEQ]), op0=ALU.add, op1=ALU.mult))
            dve.wait_ge(std_ready, c.norm + 1)
            c.op(v.reciprocal(rstd[:, :], std[:, :]))
            c.settle()

            def lo(k):
                dve.wait_ge(hhi_ready, c.norm * KT + (k + 1))
                v.tensor_tensor(hlo[:, k, :], hf[:, k % 2, :], hhi[:, k, :].bitcast(F32), ALU.subtract).then_inc(h_ready, 1)

            for k in range(KT):
                if k >= 2:
                    dve.wait_ge(hf_ready, c.norm * KT + (k - 1))
                    dve.wait_ge(hp_ready, c.norm * KT + (k - 1))
                v.tensor_tensor(hn[:, k % 2, :], xT[:, k, :], rstd[:, :], ALU.mult).then_inc(hn_ready, 1)
                if k >= 2:
                    dve.wait_ge(h_ready, c.norm * KT + (k - 1 + H0))
                dve.wait_ge(hn_ready, c.norm * KT + (k + 1))
                v.tensor_scalar(hf[:, k % 2, 0:PR], hn[:, k % 2, 0:PR], modA[:, k, 0:1],
                                modT[:, shift * KT + k, 0:1], ALU.mult, ALU.add).then_inc(hp_ready, 1)
                if k >= 1:
                    lo(k - 1)
            lo(KT - 1)

        def residual(c, x_tile, gate_of, e, t):
            acc(c, e)
            c.op(v.tensor_tensor(t[:, 0:PR], G[e[0]][:, 0:PR], gate_of[:, 0:1].to_broadcast([P, PR]), ALU.mult))
            v.tensor_tensor(seqs(t[:, PR:TOK]), seqs(G[e[0]][:, PR:TOK]),
                            gate_of[:, 1:NSEQ].unsqueeze(2).to_broadcast([P, SB, ST]), ALU.mult).then_inc(acc_free[e[0]], 1)
            dve.wait_ge(acc_free[e[0]], c.now[f"bank{e[0]}"] + (e[1] + 1))
            v.tensor_tensor(x_tile, x_tile, t, ALU.add).then_inc(res_ready, 1)

        with cnt.turn({}, use=("blk",)) as c:
            low(c, 0)
        with dve.Fori(0, DEPTH) as l:
            with dve.Fori(0, 4) as s, cnt.turn({"ada": 1}) as c:
                ada_rows(c)
                ada_cols(c, s)
            with cnt.turn({"norm": 1}, use=("norm", "res")) as c:
                dve.wait_ge(mod_ready, l * ADA_STEPS + 4)
                norm(c, 0, bass.ds(l * 32, KT))
            with dve.Fori(0, S_V.turns) as i, cnt.turn(S_V.adds) as c:
                for j in range(4):
                    low(c, j + 1)
            with dve.Fori(0, HEADS) as h, cnt.turn(S_HEAD.adds) as c:
                H = c.head
                gr = S_HEAD.groups
                low(c, 1)
                low(c, 2)
                ada_rows(c)
                low(c, 3)
                copied(c, gr[0])
                qk = qkA[:, :, :].rearrange("p t (a d) -> p (t a) d", a=2)
                tq = tmp[:, :].rearrange("p (a d) -> p a d", d=DH)
                c.op(v.tensor_tensor(tq, qk, qk, ALU.mult))
                c.settle()
                c.op(v.tensor_reduce(qk_ss, tq, axis=AXX, op=ALU.add))
                c.settle()
                v.tensor_scalar(qk_ms, qk_ss, 1.0 / DH, EPS, ALU.mult, ALU.add).then_inc(qk_msr, 1)
                ada_cols(c, h + 4)
                dve.wait_ge(qk_pow, H + 1)
                c.op(v.tensor_tensor(qk, qk, qk_rs.unsqueeze(2).to_broadcast([P, 6, DH]), ALU.mult))
                c.settle()
                v.tensor_tensor(qkA[:, :, :], qkA[:, :, :], gqk[:, bass.ds(l, 1), :].to_broadcast([P, NT, 2 * DH]),
                                ALU.mult).then_inc(qk_norm, 1)
                low(c, 4)
                dve.wait_ge(ta_done, H + 1)
                v.tensor_copy(kaT[:, :], X[1][:, 0:TOK]).then_inc(ka_ev, 1)
                dve.wait_ge(kt_done[0], H + 1)
                dve.wait_ge(pair_done, H * 4)
                v.tensor_copy(kcT[:, :, 0:P], X[2][:, :].rearrange("p (g k) -> p g k", g=4)).then_inc(kt_d[0], 1)
                low(c, 5)
                dve.wait_ge(kt_done[1], H + 1)
                dve.wait_ge(sn_done, H + 1)
                v.tensor_copy(kcT[:, :, 0:P], X[0][:, :].rearrange("p (g k) -> p g k", g=4)).then_inc(kt_d[1], 1)
                dve.wait_ge(sp_done, H + 1)
                dve.wait_ge(bias_full, H * 16 + 16)
                dve.wait_ge(orT_done, H)
                v.scalar_tensor_tensor(out=prob[:, 0:B_C], in0=X[3][:, 0:B_C], scalar=DH ** -0.5, in1=bias[:, 0:B_C],
                                       op0=ALU.mult, op1=ALU.add).then_inc(sp_read, 1)
                copied(c, gr[1])
                dve.wait_ge(kdm_ready, H)
                half = DH // 2
                rr = qkZ[:, :].rearrange("p (t a h d) -> p t a h d", t=NT, a=2, h=2)
                ro = qkR[:, :, :].rearrange("p t (a h d) -> p t a h d", a=2, h=2)
                rt = tmp[:, :].rearrange("p (t a h d) -> p t a h d", t=NT, a=2, h=2)
                for t in range(NT):
                    c.op(v.tensor_tensor(ro[:, t], rr[:, t], rope_t[:, t:t + 1, 0:1, :].to_broadcast([P, 2, 2, half]), ALU.mult))
                    c.op(v.tensor_tensor(rt[:, t], rr[:, t, :, ::-1, :],
                                         rope_t[:, t:t + 1, 1:3, :].to_broadcast([P, 2, 2, half]), ALU.mult))
                c.settle()
                v.tensor_tensor(qkR[:, :, :], qkR[:, :, :], tmp[:, :].rearrange("p (t c) -> p t c", t=NT), ALU.add)\
                    .then_inc(rope_ready, 1)
                low(c, 6)
                dve.wait_ge(ss_done, H + 1)
                v.scalar_tensor_tensor(out=prob[:, B_C:W_BIAS], in0=X[2][:, 0:PAST + P], scalar=DH ** -0.5,
                                       in1=bias[:, B_C:W_BIAS], op0=ALU.mult, op1=ALU.add).then_inc(ss_read, 1)
                dve.wait_ge(ss_read, H + 1)
                for n, (lo_, w) in enumerate(((B_Q0, P), (B_Q1, SEQ), (B_C, PAST + P))):
                    ins = v.tensor_reduce(negmax[:, n:n + 1], prob[:, lo_:lo_ + w], axis=AXX, op=ALU.max, negate=True)
                    ins.then_inc(max_ready, 1) if n == 2 else c.op(ins)
                dve.wait_ge(tr_done, H + 1)
                dve.wait_ge(dec_full, H * 16 + 16)
                c.op(v.tensor_copy(qrT[:, :], X[0][:, 0:TOK]))
                row = dec[:, DC_ROW:DC_ROW + 64].rearrange("p (g t) -> p g t", g=4)
                c.op(v.tensor_tensor(par(qr_par[:, 0, :], 0), par(X[0][:, PR:TOK], 0), row, ALU.mult))
                v.tensor_tensor(par(qr_par[:, 1, :], 1), par(X[0][:, PR:TOK], 1), row, ALU.mult).then_inc(qr_ev, 1)
                low(c, 7)
                dve.wait_ge(exp_done, H * 3 + 3)
                c.op(v.reciprocal(rinv, rowsum))
                dve.wait_ge(rs_done, H + 1)
                v.tensor_tensor(sdT[:, :], X[2][:, :], dec[:, 0:512], ALU.mult).then_inc(sd_ready, 1)
                dve.wait_ge(pt_done, H + 1)
                v.tensor_copy(pT[:, 2 * P:4 * P], X[1][:, 0:2 * P]).then_inc(pt_d, 1)
                low(c, 8)
                dve.wait_ge(pv_done, H + 1)
                c.op(v.tensor_copy(gcol[:, :], gT[:, bass.ds(l * 32 + h * 2 + 16, 2)]))
                c.settle()
                v.tensor_tensor(oa[:, :, :], X[3][:, 0:TOK].rearrange("p (t d) -> p t d", t=NT),
                                rinv.unsqueeze(2).to_broadcast([P, NT, DH]), ALU.mult).then_inc(oa_ready, 1)
                dve.wait_ge(oss_ready, H * 3 + 3)
                v.tensor_scalar(o_ms, o_ss, 1.0 / DV, EPS, ALU.mult, ALU.add).then_inc(o_msr, 1)
                dve.wait_ge(o_pow, H + 1)
                c.op(v.tensor_tensor(onorm[:, 0:2, :], X[2][:, :].rearrange("p (t v) -> p t v", t=2),
                                     o_rs[:, 0:2].unsqueeze(2).to_broadcast([P, 2, DV]), ALU.mult))
                v.tensor_scalar(onorm[:, 2, :], X[0][:, 0:DV], o_rs[:, 2:3], None, ALU.mult).then_inc(on_ready, 1)

                def pair(q):
                    dve.wait_ge(pair_done, H * 4 + (q + 1))
                    s2 = st[:, 2 * q:2 * q + 2, :].rearrange("p b v -> p (b v)")
                    v.scalar_tensor_tensor(out=s2, in0=s2, scalar=dec[:, DC_S:DC_S + 1], in1=X[3 if q == 2 else 1][:, :],
                                           op0=ALU.mult, op1=ALU.add).then_inc(pair_ev, 1)

                pair(0)
                copied(c, gr[3])
                dve.wait_ge(orT_done, H + 1)
                for n in range(2):
                    v.scalar_tensor_tensor(out=y_ret[:, bass.ds(h * 2 + n, 1), :].rearrange("p a t -> p (a t)"),
                                           in0=X[2 * n][:, 0:TOK], scalar=gcol[:, n:n + 1], in1=zs[:, n, :],
                                           op0=ALU.mult, op1=ALU.mult).then_inc(orT_ev, 1)
                for q in (1, 2, 3):
                    pair(q)
            for n in range(3 * HEADS):
                src = y_ret[:, n, :] if n < 2 * HEADS else y_att[:, n - 2 * HEADS, :]
                dve.wait_ge(yhi_ready, l * (3 * HEADS) + (n + 1))
                v.tensor_tensor(ylo[:, n, :], src, yhi[:, n, :].bitcast(F32), ALU.subtract).then_inc(y_ready, 1)
            with dve.Fori(0, S_MERGE.turns) as i, cnt.turn(S_MERGE.adds) as c:
                for j in range(20):
                    low(c, j + 1)
                    g, r = j // 10, j % 10
                    if r == 5:
                        copied(c, S_MERGE.groups[4 * g])
                        for n, e in enumerate(S_MERGE.groups[4 * g + 1]):
                            acc(c, e)
                            v.tensor_tensor(part[:, n, :], G[e[0]][:, 0:TOK], gate[:, n, :], ALU.mult).then_inc(acc_free[e[0]], 1)
                    if r == 9:
                        copied(c, S_MERGE.groups[4 * g + 2])
                        for n, e in enumerate(S_MERGE.groups[4 * g + 3]):
                            acc(c, e)
                            v.tensor_tensor(mix[:, n, :], G[e[0]][:, 0:TOK], gate[:, n, :], ALU.mult).then_inc(acc_free[e[0]], 1)
                            dve.wait_ge(acc_free[e[0]], c.now[f"bank{e[0]}"] + (e[1] + 1))
                            v.tensor_tensor(mix[:, n, :], mix[:, n, :], part[:, n, :], ALU.add).then_inc(mix_ready, 1)
                        for n in range(2):
                            dve.wait_ge(mhi_ready, c.mix + (2 * g + n + 1))
                            kt = bass.ds(i * 4 + (2 * g + n), 1)
                            v.tensor_tensor(mlo[:, kt, :].rearrange("p a t -> p (a t)"), mix[:, n, :],
                                            mhi[:, kt, :].rearrange("p a t -> p (a t)").bitcast(F32),
                                            ALU.subtract).then_inc(m_ready, 1)
            with dve.Fori(0, S_OUT.turns) as i, cnt.turn(S_OUT.adds) as c:
                for j in range(4):
                    low(c, j + 1)
                    if j % 2:
                        for n, e in enumerate(S_OUT.groups[j // 2]):
                            q = i * 4 + (j // 2 * 2 + n)
                            residual(c, xT[:, bass.ds(q, 1), :].rearrange("p a t -> p (a t)"),
                                     modT[:, bass.ds(q + 2 * KT, 1), :].rearrange("p a b -> p (a b)"), e, rtm[:, n, :])
            with cnt.turn({"norm": 1}) as c:
                dve.wait_ge(res_ready, c.norm * KT)
                norm(c, 3, bass.ds(l * 32 + KT, KT))
            with dve.Fori(0, S_UP.turns) as i, cnt.turn(S_UP.adds) as c:
                for j in range(4):
                    low(c, j + 1)
                    if j % 2:
                        for n, e in enumerate(S_UP.groups[j // 2]):
                            q = j // 2 * 2 + n
                            copied(c, [e])
                            c.op(v.tensor_tensor(fsq[:, n, :], frelu[:, n, :], frelu[:, n, :], ALU.mult))
                            c.settle()
                            dve.wait_ge(f_hi, c.ff + (q + 1))
                            kt = bass.ds(i * 4 + q, 1)
                            v.tensor_tensor(flo[:, kt, :].rearrange("p a t -> p (a t)"), fsq[:, n, :],
                                            fhi[:, kt, :].rearrange("p a t -> p (a t)").bitcast(F32),
                                            ALU.subtract).then_inc(f_ready, 1)
            with dve.Fori(0, S_DOWN.turns) as i, cnt.turn(S_DOWN.adds) as c:
                for j in range(8):
                    low(c, j + 1)
                for n, e in enumerate(S_DOWN.groups[0]):
                    q = i * 2 + n
                    residual(c, xT[:, bass.ds(q, 1), :].rearrange("p a t -> p (a t)"),
                             modT[:, bass.ds(q + 5 * KT, 1), :].rearrange("p a b -> p (a b)"), e, rtf[:, n, :])
        for n in (0, 2, 4):
            dve.wait_ge(fin_pe, n + 1)
            v.tensor_copy(xtok[:, n // 2, 0:4 * P], X[n % 4][:, :]).then_inc(fin_d, 1)

    @block.tensor
    def _(pe):
        t = nc.tensor
        cnt = Counts(pe, None, tuple(n for n in Counts.NAMES if n != "own"))
        pe.sem_inc(blk_used, SPLIT)
        pe.sem_inc(ada_used, 2)

        def turned(out, in_, k=P):
            return t.transpose(out, in_, ident[0:k, 0:k])

        pe.wait_ge(consts, 1)
        pe.wait_ge(ld_g, 6 * 16)
        turned(G[0][:, 0:64], grow[:, :], 64).then_inc(pre_pe, 1)
        pe.wait_ge(csil_ready, 1)
        for k in range(KT):
            ins = turned(G[1][:, k * 16:k * 16 + NSEQ], csil[:, k * P:(k + 1) * P], NSEQ)
        ins.then_inc(pre_pe, 1)
        pe.wait_ge(ld_x, 32)
        for n in range(6):
            if n >= 4:
                pe.wait_ge(pre_d, 3) if n == 4 else pe.wait_ge(pre_a, 1)
            for k in range(4):
                kt = n % 2 * 4 + k
                ins = turned(X[n % 4][:, k * P:(k + 1) * P], xtok[:, n // 2, kt * P:(kt + 1) * P])
            ins.then_inc(pre_pe, 1)
        pe.wait_ge(pre_d, 5)
        pe.wait_ge(pre_a, 3)

        def products(c, stage, j, banks, hi, lo, k0, first, last):
            tokens = len(banks) == 3
            pe.wait_ge(blk_split, c.blk + (j + 1 + RAW))
            s = j % SPLIT
            for n, (b, use, _, _) in enumerate(banks):
                if first:
                    pe.wait_ge(acc_free[b], c.now[f"bank{b}"] + use if use else c.now[f"bank{b}"])
                for k in range(BK):
                    for x, w in ((hi, whi), (lo, whi), (hi, wlo)):
                        start = first and k == 0 and x is hi and w is whi
                        stop = last and k == BK - 1 and w is wlo
                        if tokens:
                            ins = t.matmul(G[b][:, 0:BC], x[:, k0 + k, n * P:(n + 1) * P], w[:, s, k, :],
                                           start=start, stop=stop)
                        else:
                            ins = t.matmul(G[b][:, 0:TOK], w[:, s, k, n * P:(n + 1) * P], x[:, k0 + k, :],
                                           start=start, stop=stop)
                if n == len(banks) - 1:
                    ins.then_inc(blk_used, 1)
                elif last:
                    ins.then_inc(acc_ready, 1)

        def norm(c):
            pe.wait_ge(std_ready, c.norm)
            pe.wait_ge(orT_ev, c.head * 2)
            for k in range(KT):
                pe.wait_ge(sq_ready, c.norm * KT + (k + 1))
                t.matmul(X[0][:, 0:TOK], ones[:, :], sq[:, k % 2, :], start=(k == 0), stop=(k == KT - 1)).then_inc(sq_used, 1)

        def ada_products(c):
            pe.wait_ge(mod_ready, c.ada)
            for q in range(4):
                if q == 3:
                    pe.wait_ge(ada_bfull, c.ada * 16 + 16)
                pe.wait_ge(ada_full[q % 2], c.ada * 32 + (q // 2 * 16 + 16))
                for k in range(2):
                    for g in range(4):
                        ins = t.matmul(X[2][32 * g:32 * g + 32, 0:P], cT[:, 2 * q + k, :], ada_w[:, q % 2, k, g * P:(g + 1) * P],
                                       start=(q == 0 and k == 0), stop=False, skip_group_check=True)
                ins.then_inc(ada_used, 1)
            for g in range(4):
                ins = t.matmul(X[2][32 * g:32 * g + 32, 0:P], ones[0:1, 0:32], ada_b[0:1, g * P:(g + 1) * P],
                               start=False, stop=True, skip_group_check=True)
            ins.then_inc(ada_mm, 1)

        def ada_turned(c):
            pe.wait_ge(ada_cp, c.ada + 1)
            turned(X[2][:, 0:P], ada_s[:, :]).then_inc(ada_tr, 1)

        with pe.Fori(0, DEPTH) as l:
            with cnt.turn({"norm": 1}, use=("norm", "head")) as c:
                norm(c)
            with pe.Fori(0, 4) as s, cnt.turn({"ada": 1}) as c:
                ada_products(c)
                ada_turned(c)
            with pe.Fori(0, S_V.turns) as i, cnt.turn(S_V.adds, use=("blk", "bank0", "bank1", "bank2", "bank3", "norm")) as c:
                for j in range(4):
                    pe.wait_ge(h_ready, c.norm * KT + (j % 2 * BK))
                    products(c, S_V, j, S_V.groups[j // 2], hhi, hlo, j % 2 * BK, j % 2 == 0, j % 2 == 1)
            with pe.Fori(0, HEADS) as h, cnt.turn(S_HEAD.adds) as c:
                H = c.head
                gr = S_HEAD.groups
                hd = bass.ds(h * DH, DH)

                def gemm(j):
                    products(c, S_HEAD, j, gr[j // 2], hhi, hlo, j % 2 * BK, j % 2 == 0, j % 2 == 1)

                def mm(out, lhsT, rhs, start=True, stop=True):
                    return t.matmul(out, lhsT, rhs, start=start, stop=stop, skip_group_check=True)

                def cached_scores(e):
                    for g in range(4):
                        ins = mm(X[2][32 * g:32 * g + 32, 0:PAST], qa_par[:, e, 32 * g:32 * g + 32], kcT[:, g, :],
                                 start=(e == 0), stop=(e == 1))
                    return ins

                gemm(0)
                pe.wait_ge(orT_ev, H * 2)
                ada_products(c)
                gemm(1)
                ada_turned(c)
                gemm(2)
                pe.wait_ge(qk_norm, H + 1)
                pe.wait_ge(pair_ev, H * 4)
                for n in range(NT):
                    turned(X[0][:, n * P:(n + 1) * P], qkA[:, n, 0:DH])
                for n in range(NT):
                    ins = turned(X[1][:, n * P:(n + 1) * P], qkA[:, n, DH:2 * DH])
                ins.then_inc(ta_done, 1)

                def keys_turned(e, banks):
                    pe.wait_ge(kc_full[e], H * 32 + 32)
                    for kt in range(2):
                        for g in range(4):
                            ins = turned(X[banks[kt]][:, g * P:(g + 1) * P], kc[:, e, kt, g, :])
                    ins.then_inc(kt_done[e], 1)

                pe.wait_ge(mod_ready, c.ada + 1)
                keys_turned(0, (2, 3))
                gemm(3)
                pe.wait_ge(qa_ev, H + 1)
                pe.wait_ge(ka_ev, H + 1)
                keys_turned(1, (0, 1))
                pe.wait_ge(kt_d[0], H + 1)
                pe.wait_ge(kt_a[0], H + 1)
                mm(X[3][:, 0:P], qaT[:, 0:P], kaT[:, 0:P])
                mm(X[3][:, P:3 * P], qaT[:, P:2 * P], kaT[:, 0:2 * P]).then_inc(sp_done, 1)
                mm(X[2][:, PAST:PAST + P], qaT[:, PR:TOK], kaT[:, PR:TOK])
                cached_scores(0).then_inc(sn_done, 1)
                gemm(4)
                pe.wait_ge(kt_d[1], H + 1)
                pe.wait_ge(kt_a[1], H + 1)
                cached_scores(1).then_inc(ss_done, 1)
                pe.wait_ge(rope_ready, H + 1)
                for n in range(NT):
                    turned(X[0][:, n * P:(n + 1) * P], qkR[:, n, 0:DH])
                for n in range(NT):
                    ins = turned(X[1][:, n * P:(n + 1) * P], qkR[:, n, DH:2 * DH])
                ins.then_inc(tr_done, 1)
                gemm(5)
                pe.wait_ge(ss_read, H + 1)
                pe.wait_ge(qr_ev, H + 1)
                pe.wait_ge(kr_ev, H + 1)
                mm(X[2][:, 0:256], krT[:, 0:P], qrT[:, 0:2 * P])
                mm(X[2][:, 256:384], krT[:, P:2 * P], qrT[:, P:2 * P])
                mm(X[2][:, 384:512], krT[:, PR:TOK], qrT[:, PR:TOK]).then_inc(rs_done, 1)
                pe.wait_ge(exp_done, H * 3 + 3)
                for n, at in enumerate((B_C, B_C + P, B_N, B_Q0)):
                    turned(X[0][:, n * P:(n + 1) * P], prob[:, at:at + P])
                for n in range(2):
                    ins = turned(X[1][:, n * P:(n + 1) * P], prob[:, B_Q1 + n * P:B_Q1 + (n + 1) * P])
                ins.then_inc(pt_done, 1)
                gemm(6)
                pe.wait_ge(pt_a, H + 1)
                pe.wait_ge(pt_d, H + 1)
                pe.wait_ge(sp_read, H + 1)
                pe.wait_ge(vc_full, H * 32 + 32)
                mm(X[3][:, 0:P], pT[:, P:2 * P], vaT[:, 0, hd])
                mm(X[3][:, P:2 * P], pT[:, 2 * P:3 * P], vaT[:, 0, hd], stop=False)
                mm(X[3][:, P:2 * P], pT[:, 3 * P:4 * P], vaT[:, 1, hd], start=False)
                mm(X[3][:, 2 * P:3 * P], pT[:, 0:P], vaT[:, 2, hd], stop=False)
                for kt in range(2):
                    for e in range(2):
                        for g in range(4):
                            ins = mm(X[3][32 * g:32 * g + 32, 2 * P:3 * P], p_par[:, kt, e, 32 * g:32 * g + 32],
                                     vc[:, kt, 2 * g + e, :], start=False, stop=(kt == 1 and e == 1))
                ins.then_inc(pv_done, 1)
                pe.wait_ge(sd_ready, H + 1)
                for b in (0, 2, 3):
                    pe.wait_ge(acc_free[b], c.now[f"bank{b}"] + ([e[1] for e in gr[2] if e[0] == b][0] + 1))
                mm(X[2][:, 0:DV], sdT[:, 0:P], vR[:, 0, :])
                mm(X[2][:, DV:2 * DV], sdT[:, P:2 * P], vR[:, 0, :], stop=False)
                mm(X[2][:, DV:2 * DV], sdT[:, 2 * P:3 * P], vR[:, 1, :], start=False)
                mm(X[0][:, 0:DV], sdT[:, 3 * P:4 * P], vR[:, 2, :], stop=False)
                pe.wait_ge(st_full, H * 32 + 32)
                for e in range(2):
                    for g in range(4):
                        ins = mm(X[0][32 * g:32 * g + 32, 0:DV], qr_par[:, e, 32 * g:32 * g + 32], st[:, 2 * g + e, :],
                                 start=False, stop=(e == 1))
                ins.then_inc(o_done, 1)
                pe.wait_ge(kdec_ready, H + 1)
                mm(X[1][:, 0:DV], kdec[:, 0, :], vR[:, 0, :], stop=False)
                mm(X[1][:, 0:DV], kdec[:, 1, :], vR[:, 1, :], start=False).then_inc(stp_done, 1)
                gemm(7)

                def pair(q):
                    x = X[3 if q == 2 else 1]
                    mm(x[:, 0:DV], kdm[:, 2 * q, :], vR[:, 2, :])
                    mm(x[:, DV:2 * DV], kdm[:, 2 * q + 1, :], vR[:, 2, :]).then_inc(pair_done, 1)

                pe.wait_ge(stp_ev, H + 1)
                pe.wait_ge(kdm_ready, H + 1)
                pair(0)
                pe.wait_ge(oa_ready, H + 1)
                for n in range(NT):
                    ins = turned(X[3][:, n * P:(n + 1) * P], oa[:, n, :])
                ins.then_inc(oaT_done, 1)
                pe.wait_ge(on_ready, H + 1)
                for r in range(2):
                    for n in range(NT):
                        ins = turned(X[2 * r][:, n * P:(n + 1) * P], onorm[:, n, r * P:(r + 1) * P])
                ins.then_inc(orT_done, 1)
                pe.wait_ge(pair_ev, H * 4 + 1)
                pair(1)
                pe.wait_ge(oaT_ev, H + 1)
                pair(2)
                pe.wait_ge(pair_ev, H * 4 + 2)
                pair(3)
            with pe.Fori(0, S_MERGE.turns) as i, cnt.turn(S_MERGE.adds) as c:
                j = 0
                for g in range(2):
                    for n, (hi, lo, k0, ks, y0) in enumerate(((hhi, hlo, 0, 2, None), (yhi, ylo, 0, 4, 0),
                                                              (hhi, hlo, 0, 2, None), (yhi, ylo, 2 * HEADS, 2, 2 * HEADS))):
                        for k in range(ks):
                            if y0 is not None:
                                pe.wait_ge(y_ready, l * (3 * HEADS) + (y0 + (k + 1) * BK))
                            products(c, S_MERGE, j, S_MERGE.groups[4 * g + n], hi, lo, k0 + k * BK, k == 0, k == ks - 1)
                            j += 1
            with pe.Fori(0, S_OUT.turns) as i, cnt.turn(S_OUT.adds, use=("blk", "bank0", "bank1", "bank2", "bank3", "mix")) as c:
                for j in range(4):
                    pe.wait_ge(m_ready, c.mix + j % 2 * BK)
                    products(c, S_OUT, j, S_OUT.groups[j // 2], mhi, mlo, j % 2 * BK, j % 2 == 0, j % 2 == 1)
            with cnt.turn({"norm": 1}, use=("norm", "head")) as c:
                norm(c)
            with pe.Fori(0, S_UP.turns) as i, cnt.turn(S_UP.adds, use=("blk", "bank0", "bank1", "bank2", "bank3", "norm")) as c:
                for j in range(4):
                    pe.wait_ge(h_ready, c.norm * KT + (j % 2 * BK))
                    products(c, S_UP, j, S_UP.groups[j // 2], hhi, hlo, j % 2 * BK, j % 2 == 0, j % 2 == 1)
            with pe.Fori(0, S_DOWN.turns) as i, cnt.turn(S_DOWN.adds, use=("blk", "bank0", "bank1", "ff")) as c:
                for j in range(8):
                    pe.wait_ge(f_ready, c.ff + (BK * j + 2))
                    products(c, S_DOWN, j, S_DOWN.groups[0], fhi, flo, j * BK, j == 0, j == 7)
        pe.wait_ge(res_ready, 2 * DEPTH * KT)
        for n in range(6):
            if n >= 4:
                pe.wait_ge(fin_d, 1) if n == 4 else pe.wait_ge(fin_a, 1)
            for k in range(4):
                ins = turned(X[n % 4][:, k * P:(k + 1) * P], xT[:, n % 2 * 4 + k, n // 2 * P:(n // 2 + 1) * P])
            ins.then_inc(fin_pe, 1)

    ctx.close()


_INS = ["x_prompt", "x_sample", "state_ret", "cache_attn_k", "cache_attn_v", "c_prompt", "c_sample", "w_ada", "b_ada",
        "norm_mix_g", "norm_ffn_g", "w_in", "ret_gn_g", "q_norm_g", "k_norm_g", "rel_bias", "w_br_ret", "w_br_att",
        "w_out", "w_up", "w_down"]
_OUTS = [(1, SEQ, DM), (SB, ST, DM), (DEPTH, 1, HEADS, DH, DV), (DEPTH, 1, SEQ, HEADS, DH), (DEPTH, 1, SEQ, HEADS, DH),
         (DEPTH, SB, HEADS, DH, DV), (DEPTH, SB, ST, HEADS, DH), (DEPTH, SB, ST, HEADS, DH)]


def kernel(**inputs):
    import numpy as _np
    import concourse.bacc as _bacc
    from concourse import mybir as _mybir
    from concourse.bass_utils import run_bass_kernel_spmd as _run

    nc = _bacc.Bacc("TRN2", target_bir_lowering=False, num_devices=1)
    rope, decay = tables()
    given = {**{n: inputs[n] for n in _INS}, "rope": rope, "decay": decay}
    arrays, args = {}, []
    for name, value in given.items():
        a = _np.ascontiguousarray(value)
        arrays[f"in_{name}_dram"] = a
        args.append(nc.dram_tensor(f"in_{name}_dram", a.shape, _mybir.dt.from_np(a.dtype), kind="ExternalInput").ap())
    for i, shape in enumerate(_OUTS):
        args.append(nc.dram_tensor(f"out_{i}_dram", shape, F32, kind="ExternalOutput").ap())
    trunk(nc, *args)
    r = _run(nc, [arrays], core_ids=[0])
    return tuple(r.results[0][f"out_{i}_dram"] for i in range(len(_OUTS)))
```

```python
from contextlib import ExitStack, contextmanager

import numpy as np
import concourse.bass as bass
from concourse import mybir
from concourse.alu_op_type import AluOpType as ALU

F32 = mybir.dt.float32
F32R = mybir.dt.float32r
ACT = mybir.ActivationFunctionType
AXX = mybir.AxisListType.X

P = 128
DM, DEPTH, HEADS, DH, DV, FF = 1024, 2, 8, 128, 256, 4096
SEQ, SB, ST, PAST, CHUNK, CLIP = 256, 8, 16, 256, 64, 128
TOK = SEQ + SB * ST
NT, KT = TOK // P, DM // P
PR = SEQ
NSEQ = 1 + SB
RQK, RV, AW = HEADS * DH, HEADS * DV, HEADS * DH
D_IN = 2 * RQK + 2 * RV + 3 * AW + 2 * DM
C_QR, C_KR, C_VR, C_ZR = 0, RQK, 2 * RQK, 2 * RQK + RV
C_QA = C_ZR + RV
C_KA, C_VA, C_MR, C_MA = C_QA + AW, C_QA + 2 * AW, C_QA + 3 * AW, C_QA + 3 * AW + DM
EPS, NEG = 1e-6, -1e30
BK, BC = 4, 256
RAW, SPLIT = 4, 2
W_DEC = 592
DC_K, DC_SEQ, DC_S, DC_ROW = 512, 514, 522, 528
B_Q0, B_Q1, B_C, B_N, W_BIAS = 0, 128, 384, 640, 768
BAND = 400
BAND_TOP = PAST + ST - 1
ADA_C, ADA0 = 512, 4
H0, M0, F0, P0 = 4, 4, 30, 4
PAIR_BANK = (1, 1, 2, 0)


def tables():
    half = DH // 2
    inv = np.float32(10000.0) ** (-np.arange(half, dtype=np.float32) / np.float32(half))
    pos = np.concatenate([np.arange(SEQ), np.tile(PAST + np.arange(ST), SB)]).astype(np.float32)
    ang = (pos[:, None] * inv[None, :]).astype(np.float32)
    cos = np.cos(ang).reshape(NT, P, half)
    sin = np.sin(ang).reshape(NT, P, half)
    rope = np.stack([cos, -sin, sin], axis=2).transpose(1, 0, 2, 3)
    dec = np.zeros((HEADS, P, W_DEC), np.float64)
    p = np.arange(P)[:, None]
    i = np.arange(SEQ)[None, :]
    for h in range(HEADS):
        lg = np.float64(np.log(np.float32(1.0 - 2.0 ** (-5.0 - h))))
        s = DH ** -0.5
        dec[h, :, 0:256] = np.where(i >= p, np.exp(lg * np.maximum(i - p, 0)), 0) * s
        dec[h, :, 256:384] = dec[h, :, 0:128]
        q = np.arange(P)[None, :]
        same = (q // ST == p // ST) & (q >= p)
        dec[h, :, 384:512] = np.where(same, np.exp(lg * np.maximum(q - p, 0)), 0) * s
        dec[h, :, DC_K] = np.exp(lg * (SEQ - 1 - p[:, 0]))
        dec[h, :, DC_K + 1] = np.exp(lg * (SEQ - 1 - P - p[:, 0]))
        for b in range(SB):
            dec[h, :, DC_SEQ + b] = np.where(p[:, 0] // ST == b, np.exp(lg * (ST - 1 - p[:, 0] % ST)), 0)
        dec[h, :, DC_S] = np.exp(lg * ST)
        dec[h, :, DC_ROW:DC_ROW + 64] = np.tile(np.exp(lg * (np.arange(ST) + 1)), 4)[None, :] * s
    return np.ascontiguousarray(rope, np.float32), dec.astype(np.float32)


def plan(groups):
    uses, ready, out = [0] * 4, 0, []
    for banks, last in groups:
        entries = []
        for n, b in enumerate(banks):
            if n < len(banks) - 1:
                ready += 1
                entries.append((b, uses[b], "ready", ready))
            else:
                entries.append((b, uses[b], "block", last + 1 + SPLIT))
            uses[b] += 1
        out.append(entries)
    return out, uses, ready


class Stage:
    def __init__(self, turns, blocks, groups, **more):
        self.turns, self.blocks = turns, blocks
        self.groups, self.uses, self.ready = plan(groups)
        self.adds = {"blk": blocks, "round": blocks // RAW, "ready": self.ready, **more,
                     **{f"bank{b}": self.uses[b] for b in range(4)}}


S_V = Stage(2, 4, [((0, 1, 2), 1), ((3, 0, 1), 3)])
S_HEAD = Stage(HEADS, 8, [((0, 1, 2), 1), ((3, 0, 1), 3), ((2, 3, 0), 5), ((1, 2), 7)], head=1, ada=1)
S_MERGE = Stage(2, 20, [g for c in (0, 10) for g in (((0, 1), c + 1), ((2, 3), c + 5), ((0, 1), c + 7), ((2, 3), c + 9))], mix=4)
S_OUT = Stage(2, 4, [((0, 1), 1), ((2, 3), 3)], res=4)
S_UP = Stage(8, 4, [((0, 1), 1), ((2, 3), 3)], ff=4)
S_DOWN = Stage(4, 8, [((0, 1), 7)], res=2, ada=1)


class Counts:

    NAMES = ("blk", "round", "ready", "bank0", "bank1", "bank2", "bank3", "head", "norm", "ada", "mix", "ff",
             "res", "own")

    def __init__(self, eng, own, names):
        self.eng, self.own_sem = eng, own
        self.regs = {}
        for n in self.NAMES:
            if n in names:
                self.regs[n] = eng.alloc_register(f"count_{n}")
                eng.reg_mov(self.regs[n], 0)

    @contextmanager
    def turn(self, adds, use=None, also=()):
        names = [n for n in self.regs if (use is None and adds.get(n)) or n == "own" or (use and n in use) or n in also]
        self.now = {n: self.eng.snap(self.regs[n]) for n in names}
        self.mine = 0
        yield self
        for n, r in self.regs.items():
            k = self.mine if n == "own" else adds.get(n, 0)
            if k:
                self.eng.reg_add(r, r, k)

    def __getattr__(self, n):
        return self.now[n]

    def op(self, ins):
        self.mine += 1
        return ins.then_inc(self.own_sem, 1)

    def settle(self):
        self.eng.wait_ge(self.own_sem, self.now["own"] + self.mine)


def trunk(nc, x_prompt, x_sample, state_ret, cache_attn_k, cache_attn_v, c_prompt, c_sample, w_ada,
          b_ada, norm_mix_g, norm_ffn_g, w_in, ret_gn_g, q_norm_g, k_norm_g, rel_bias, w_br_ret,
          w_br_att, w_out, w_up, w_down, rope, decay, y_prompt, y_sample, st_prompt, k_prompt,
          v_prompt, st_sample, k_sample, v_sample):
    ctx = ExitStack()

    def sem(name):
        return ctx.enter_context(nc.semaphore(name))

    def sb(name, shape, dt=F32, stack=ctx):
        return stack.enter_context(nc.sbuf_tensor(name, shape, dt))

    raw = sb("raw", [P, RAW, BK, BC])
    whi = sb("whi", [P, SPLIT, BK, BC], F32R)
    wlo = sb("wlo", [P, SPLIT, BK, BC], F32R)
    xT = sb("xT", [P, KT, TOK])
    hhi = sb("hhi", [P, KT, TOK], F32R)
    hlo = sb("hlo", [P, KT, TOK], F32R)
    ada_w = sb("ada_w", [P, 2, 2, ADA_C])
    ada_b = sb("ada_b", [1, ADA_C])
    ada_s = sb("ada_s", [P, P])
    modT = sb("modT", [P, 6 * KT, NSEQ])
    modA = sb("modA", [P, KT, NSEQ])
    cT = sb("cT", [P, KT, 32])
    gT = sb("gT", [P, 64])
    gqk = sb("gqk", [P, DEPTH, 2 * DH])
    rope_t = sb("rope_t", [P, NT, 3, DH // 2])
    ident = sb("ident", [P, P])
    ones = sb("ones", [P, P])
    eps_t = sb("eps_t", [P, 1])
    mhalf = sb("mhalf", [P, 8])
    qa_par = sb("qa_par", [P, 2, P])
    qr_par = sb("qr_par", [P, 2, P])
    p_par = sb("p_par", [P, 2, 2, P])
    gcol = sb("gcol", [P, 2])
    small = sb("small", [P, 64])
    qk_ms, qk_rs = small[:, 0:6], small[:, 8:14]
    negmax, rowsum, rinv = small[:, 16:19], small[:, 20:23], small[:, 24:27]
    o_ms, o_rs, qk_ss, o_ss = small[:, 28:31], small[:, 32:35], small[:, 36:42], small[:, 44:47]

    xstack = ExitStack()
    xtok = sb("xtok", [P, NT, DM], stack=xstack)
    crow = sb("crow", [NSEQ, DM], stack=xstack)
    csil = sb("csil", [NSEQ, DM], stack=xstack)
    grow = sb("grow", [64, P], stack=xstack)
    rbrow = sb("rbrow", [DEPTH * HEADS, 2 * CLIP + 1], stack=xstack)
    band = sb("band", [DEPTH * HEADS, BAND], stack=xstack)
    neg = sb("neg", [P, P], stack=xstack)
    ada0_w = sb("ada0_w", [P, ADA0, KT, ADA_C], stack=xstack)
    ada0_b = sb("ada0_b", [1, ADA0 * ADA_C], stack=xstack)
    xstack.close()
    ystack = ExitStack()
    y_ret = sb("y_ret", [P, 2 * HEADS, TOK], stack=ystack)
    y_att = sb("y_att", [P, HEADS, TOK], stack=ystack)
    hstack = ExitStack()
    vaT = sb("va_tok", [P, NT, AW], stack=hstack)
    kc = sb("kc", [P, 2, 2, 4, DH], stack=hstack)
    vc = sb("vc", [P, 2, SB, DH], stack=hstack)
    qkA = sb("qkA", [P, NT, 2 * DH], stack=hstack)
    qkR = sb("qkR", [P, NT, 2 * DH], stack=hstack)
    tmp = sb("tmp", [P, NT * 2 * DH], stack=hstack)
    bias = sb("bias", [P, W_BIAS], stack=hstack)
    qaT = sb("qaT", [P, TOK], stack=hstack)
    kaT = sb("kaT", [P, TOK], stack=hstack)
    qrT = sb("qrT", [P, SEQ + P], stack=hstack)
    krT = sb("krT", [P, TOK], stack=hstack)
    pT = sb("pT", [P, 512], stack=hstack)
    sdT = sb("sdT", [P, 512], stack=hstack)
    kdec = sb("kdec", [P, 2, DH], stack=hstack)
    dec = sb("dec", [P, W_DEC], stack=hstack)
    oa = sb("oa", [P, NT, DH], stack=hstack)
    stp = sb("stp", [P, DV], stack=hstack)
    prob = sb("prob", [P, W_BIAS], stack=hstack)
    vR = sb("vR", [P, NT, DV], stack=hstack)
    qkZ = sb("qkZ", [P, 2 * TOK], stack=hstack)
    kcT = sb("kcT", [P, 4, PAST], stack=hstack)
    st = sb("st", [P, SB, DV], stack=hstack)
    kdm = kcT[:, :, :].rearrange("p a b -> p (a b)").rearrange("p (b d) -> p b d", b=SB)
    rraw = qkZ[:, :].rearrange("p (t c) -> p t c", t=NT)
    zs = qkZ[:, :].rearrange("p (n t) -> p n t", n=2)
    onorm = prob[:, :].rearrange("p (t v) -> p t v", t=NT)
    hstack.close()
    nstack = ExitStack()
    sq = sb("sq", [P, 2, TOK], stack=nstack)
    hn = sb("hn", [P, 2, TOK], stack=nstack)
    hf = sb("hf", [P, 2, TOK], stack=nstack)
    std = sb("std", [P, TOK], stack=nstack)
    rstd = sb("rstd", [P, TOK], stack=nstack)
    nstack.close()
    bstack = ExitStack()
    gate = sb("gate", [P, 2, TOK], stack=bstack)
    yhi = sb("yhi", [P, 3 * HEADS, TOK], F32R, stack=bstack)
    ylo = sb("ylo", [P, 3 * HEADS, TOK], F32R, stack=bstack)
    bstack.close()
    ystack.close()
    mstack = ExitStack()
    mhi = sb("mhi", [P, KT, TOK], F32R, stack=mstack)
    mlo = sb("mlo", [P, KT, TOK], F32R, stack=mstack)
    part = sb("part", [P, 2, TOK], stack=mstack)
    mix = sb("mix", [P, 2, TOK], stack=mstack)
    rtm = sb("rtm", [P, 2, TOK], stack=mstack)
    mstack.close()
    fstack = ExitStack()
    fhi = sb("fhi", [P, FF // P, TOK], F32R, stack=fstack)
    flo = sb("flo", [P, FF // P, TOK], F32R, stack=fstack)
    frelu = sb("frelu", [P, 2, TOK], stack=fstack)
    fsq = sb("fsq", [P, 2, TOK], stack=fstack)
    rtf = sb("rtf", [P, 2, TOK], stack=fstack)
    fstack.close()

    G = [ctx.enter_context(nc.psum_tensor(f"G{b}", [P, 512], F32)) for b in range(4)]
    X = [ctx.enter_context(nc.psum_tensor(f"X{b}", [P, 512], F32)) for b in range(4)]

    band_d = nc.dram_tensor("band_d", [DEPTH * HEADS, BAND], F32, kind="Internal").ap()
    bias_d = nc.dram_tensor("bias_d", [DEPTH * HEADS, P, W_BIAS], F32, kind="Internal").ap()

    raw_full = [sem(f"raw_full{s}") for s in range(RAW)]
    blk_hi = sem("blk_hi")
    blk_split = sem("blk_split")
    blk_used = sem("blk_used")
    acc_ready = sem("acc_ready")
    acc_free = [sem(f"acc_free{b}") for b in range(4)]
    act_own, dve_own, pool_own = sem("act_own"), sem("dve_own"), sem("pool_own")
    ada_full = [sem(f"ada_full{s}") for s in range(2)]
    ada0_full = [sem(f"ada0_full{s}") for s in range(ADA0)]
    ada_bfull, ada_used, ada_mm, ada_cp, ada_tr, mod_ready = (
        sem(n) for n in ("ada_bfull", "ada_used", "ada_mm", "ada_cp", "ada_tr", "mod_ready"))
    sq_ready, sq_used, std_ready, hn_ready, hp_ready, hf_ready, hhi_ready, h_ready = (
        sem(n) for n in ("sq_ready", "sq_used", "std_ready", "hn_ready", "hp_ready", "hf_ready", "hhi_ready", "h_ready"))
    ld_x, ld_c, ld_g, ld_rb, ld_k, consts = (sem(n) for n in ("ld_x", "ld_c", "ld_g", "ld_rb", "ld_k", "consts"))
    band_ready, band_out, mask_out, band_in = (sem(n) for n in ("band_ready", "band_out", "mask_out", "band_in"))
    csil_ready, pre_pe, pre_d, pre_a = (sem(n) for n in ("csil_ready", "pre_pe", "pre_d", "pre_a"))
    kc_full = [sem(f"kc_full{e}") for e in range(2)]
    vc_full, st_full, bias_full, dec_full = (sem(n) for n in ("vc_full", "st_full", "bias_full", "dec_full"))
    va_out, ka_out, st_out, stp_out, y_out = (sem(n) for n in ("va_out", "ka_out", "st_out", "stp_out", "y_out"))
    qk_msr, qk_pow, qk_norm, ta_done, qa_ev, ka_ev = (
        sem(n) for n in ("qk_msr", "qk_pow", "qk_norm", "ta_done", "qa_ev", "ka_ev"))
    kt_done = [sem(f"kt_done{e}") for e in range(2)]
    kt_a = [sem(f"kt_a{e}") for e in range(2)]
    kt_d = [sem(f"kt_d{e}") for e in range(2)]
    sp_done, sn_done, ss_done, sp_read, ss_read, maxp_ready, maxs_ready, exp_done = (
        sem(n) for n in ("sp_done", "sn_done", "ss_done", "sp_read", "ss_read", "maxp_ready", "maxs_ready", "exp_done"))
    rope_ready, tr_done, qr_ev, kr_ev, rs_done, sd_ready = (
        sem(n) for n in ("rope_ready", "tr_done", "qr_ev", "kr_ev", "rs_done", "sd_ready"))
    pt_done, pt_a, pt_d, pv_done, oa_ready, oaT_done, oaT_ev = (
        sem(n) for n in ("pt_done", "pt_a", "pt_d", "pv_done", "oa_ready", "oaT_done", "oaT_ev"))
    o_done, oss_ready, o_msr, o_pow, on_ready, orT_done, orT_ev = (
        sem(n) for n in ("o_done", "oss_ready", "o_msr", "o_pow", "on_ready", "orT_done", "orT_ev"))
    kdec_ready, kdm_ready, stp_done, stp_ev, pair_done, pair_ev = (
        sem(n) for n in ("kdec_ready", "kdm_ready", "stp_done", "stp_ev", "pair_done", "pair_ev"))
    yhi_ready, y_ready, mix_ready, mhi_ready, m_ready = (
        sem(n) for n in ("yhi_ready", "y_ready", "mix_ready", "mhi_ready", "m_ready"))
    dma_go = sem("dma_go")
    f_hi, f_ready, res_ready, fin_pe, fin_a, fin_d = (
        sem(n) for n in ("f_hi", "f_ready", "res_ready", "fin_pe", "fin_a", "fin_d"))

    block = ctx.enter_context(nc.Block())

    def seqs(ap):
        return ap.rearrange("p (b t) -> p b t", b=SB)

    def par(ap, e):
        return ap.rearrange("p (g e t) -> p g e t", g=4, e=2)[:, :, e, :]

    def ada0_load(eng, s):
        for k in range(2):
            eng.dma_start(ada0_w[:, s, k * 4:k * 4 + 4, :], w_ada[0, k * 4 * P:(k + 1) * 4 * P, s * ADA_C:(s + 1) * ADA_C]
                          .rearrange("(k p) n -> p k n", p=P)).then_inc(ada0_full[s], 16)
        eng.dma_start(ada0_b[:, s * ADA_C:(s + 1) * ADA_C], b_ada[0:1, s * ADA_C:(s + 1) * ADA_C]).then_inc(ada0_full[s], 16)

    def ada_load(eng, n, l, s, half):
        if half == 0:
            eng.wait_ge(ada_mm, n + ADA0)
            eng.dma_start(ada_b[:, :], (b_ada[l:l + 1] if isinstance(l, int) else b_ada[bass.ds(l, 1)])
                          [:, bass.ds(s * ADA_C, ADA_C)]).then_inc(ada_bfull, 16)
        for q in (2 * half, 2 * half + 1):
            eng.wait_ge(ada_used, n * 4 + (q + 1))
            eng.dma_start(ada_w[:, q % 2, :, :], w_ada[l, q * 2 * P:(q + 1) * 2 * P, bass.ds(s * ADA_C, ADA_C)]
                          .rearrange("(k p) n -> p k n", p=P)).then_inc(ada_full[q % 2], 16)

    @block.sync
    def _(sp):
        cnt = Counts(sp, None, ("blk", "ada", "head"))
        sp.dma_start(xtok[:, 0:2, :], x_prompt[0].rearrange("(t p) d -> p t d", p=P)).then_inc(ld_x, 16)
        sp.dma_start(xtok[:, 2, :], x_sample.rearrange("b t d -> (b t) d")).then_inc(ld_x, 16)
        ada0_load(sp, 0)
        ada0_load(sp, 2)

        lh = DEPTH * HEADS
        sp.wait_ge(consts, 1)
        for rows_, c0, n in ((CHUNK, B_Q0 + CHUNK, CHUNK), (CHUNK, B_Q1 + 3 * CHUNK, CHUNK), (P, B_N, P)):
            sp.dma_start(bias_d[:, 0:rows_, c0:c0 + n].rearrange("l p n -> p l n"),
                        neg[0:rows_, 0:n].unsqueeze(1).to_broadcast([rows_, lh, n])).then_inc(mask_out, 16)
        sp.wait_ge(band_ready, 1)
        sp.dma_start(band_d, band[:, :]).then_inc(band_out, 16)
        sp.wait_ge(band_out, 16)
        sp.wait_ge(mask_out, 48)

        def place(p0, n, c0, w, m0):
            src = bass.AP(tensor=band_d.tensor, offset=m0, ap=[[BAND, lh], [-1, n], [1, w]])
            sp.dma_start(bias_d[:, p0:p0 + n, c0:c0 + w], src).then_inc(band_in, 16)

        at0 = BAND_TOP
        place(0, CHUNK, B_Q0, CHUNK, at0)
        place(CHUNK, CHUNK, B_Q0, P, at0 - CHUNK)
        place(0, CHUNK, B_Q1, 3 * CHUNK, at0 - P)
        place(CHUNK, CHUNK, B_Q1, SEQ, at0 - P - CHUNK)
        for b in range(SB):
            place(b * ST, ST, B_C, PAST, at0 - PAST)
            place(b * ST, ST, B_N + b * ST, ST, at0)

        def load(c, j, parts):
            sp.wait_ge(blk_split, c.blk + (j + 1))
            off = 0
            for src in parts:
                w = src.shape[-1]
                sp.dma_start(raw[:, j % RAW, :, off:off + w], src.rearrange("(k p) n -> p k n", p=P))\
                    .then_inc(raw_full[j % RAW], 32 // len(parts))
                off += w

        def rows(w, l, k, c, n=BC):
            return w[l, k * BK * P:(k + 1) * BK * P, bass.ds(c, n)]

        with sp.Fori(0, DEPTH) as l:
            with sp.Fori(0, S_V.turns) as i, cnt.turn(S_V.adds) as c:
                for j in range(4):
                    load(c, j, [rows(w_in, l, j % 2, i * (2 * BC) + (C_VA + j // 2 * BC))])
            with sp.Fori(0, HEADS) as h, cnt.turn(S_HEAD.adds) as c:
                for j in range(2):
                    load(c, j, [rows(w_in, l, j, h * DH + C_QA, DH), rows(w_in, l, j, h * DH + C_KA, DH)])
                    if j == 0:
                        ada_load(sp, c.ada, l, h + 4, 0)
                for j in range(2):
                    load(c, 2 + j, [rows(w_in, l, j, h * DH + C_QR, DH), rows(w_in, l, j, h * DH + C_KR, DH)])
                sp.wait_ge(kt_done[1], c.head)
                for e in range(2):
                    for t in range(2):
                        src = cache_attn_k[l, e:SB:2, t * P:(t + 1) * P, bass.ds(h, 1), :]
                        sp.dma_start(kc[:, e, t, :, :], src.rearrange("b k h d -> k b (h d)")).then_inc(kc_full[e], 16)
                for j in range(2):
                    load(c, 4 + j, [rows(w_in, l, j, h * DV + C_VR)])
                sp.wait_ge(ss_read, c.head)
                sp.wait_ge(sp_read, c.head)
                sp.wait_ge(band_in, 20 * 16)
                sp.dma_start(bias[:, :], bias_d[bass.ds(l * HEADS + h, 1)].rearrange("a p n -> p (a n)")).then_inc(bias_full, 16)
                for j in range(2):
                    load(c, 6 + j, [rows(w_in, l, j, h * DV + C_ZR)])
                    if j == 0:
                        ada_load(sp, c.ada, l, h + 4, 1)
                sp.wait_ge(pv_done, c.head)
                for t in range(2):
                    src = cache_attn_v[l, :, t * P:(t + 1) * P, bass.ds(h, 1), :]
                    sp.dma_start(vc[:, t, :, :], src.rearrange("b k h d -> k b (h d)")).then_inc(vc_full, 16)
            with sp.Fori(0, S_MERGE.turns) as i, cnt.turn(S_MERGE.adds) as c:
                j = 0
                for g in range(2):
                    for w, base, ks in ((w_in, C_MR, 2), (w_br_ret, 0, 4), (w_in, C_MA, 2), (w_br_att, 0, 2)):
                        for k in range(ks):
                            load(c, j, [rows(w, l, k, i * (2 * BC) + (base + g * BC))])
                            j += 1
            with sp.Fori(0, S_OUT.turns) as i, cnt.turn(S_OUT.adds) as c:
                for j in range(4):
                    load(c, j, [rows(w_out, l, j % 2, i * (2 * BC) + j // 2 * BC)])
            with sp.Fori(0, S_UP.turns) as i, cnt.turn(S_UP.adds) as c:
                for j in range(4):
                    load(c, j, [rows(w_up, l, j % 2, i * (2 * BC) + j // 2 * BC)])
            with sp.Fori(0, S_DOWN.turns) as i, cnt.turn(S_DOWN.adds) as c:
                for j in range(8):
                    load(c, j, [rows(w_down, l, j, i * BC)])
                    if j in (1, 5):
                        ada_load(sp, c.ada, DEPTH - 1, i, j // 4)
        with cnt.turn({}, use=("blk",)) as c:
            load(c, 0, [w_in[0, 0:BK * P, 0:BC]])
        sp.wait_ge(fin_a, 3)
        sp.wait_ge(fin_d, 3)
        sp.dma_start(y_prompt[0].rearrange("(t p) d -> p t d", p=P), xtok[:, 0:2, :]).then_inc(y_out, 16)
        sp.dma_start(y_sample.rearrange("b t d -> (b t) d"), xtok[:, 2, :]).then_inc(y_out, 16)
        sp.wait_ge(y_out, 32)
        sp.wait_ge(raw_full[0], (DEPTH * 184 // RAW + 1) * 32)

    @block.gpsimd
    def _(pool):
        g = nc.gpsimd
        cnt = Counts(pool, pool_own, ("head", "norm", "own"))
        for m in (ident, ones, eps_t, mhalf, cT, qa_par, qr_par, p_par, neg):
            value = {"ones": 1.0, "eps_t": EPS, "mhalf": -0.5, "neg": NEG}.get(m.name, 0.0)
            ap = m[:, :] if len(m.shape) == 2 else m[:, :, :] if len(m.shape) == 3 else m[:, :, :, :]
            g.memset(ap, value).then_inc(pool_own, 1)
        pool.wait_ge(pool_own, 9)
        g.affine_select(out=ident[:, :], in_=ident[:, :], compare_op=ALU.not_equal, fill=1.0, base=0,
                        pattern=[[-1, P]], channel_multiplier=1).then_inc(consts, 1)
        pool.reg_add(cnt.regs["own"], cnt.regs["own"], 9)

        def dma(out, in_):
            pool.sem_inc(dma_go, 1)
            return g.dma_start(out, in_)

        def norm_sample(c, shift):
            for k in range(KT):
                pool.wait_ge(hn_ready, c.norm * KT + (k + 1))
                pool.wait_ge(h_ready, c.norm * KT + (max(k - 1, 0) + H0))
                d = seqs(hf[:, k % 2, PR:TOK])
                c.op(g.tensor_tensor(d, seqs(hn[:, k % 2, PR:TOK]),
                                     modA[:, k, 1:NSEQ].unsqueeze(2).to_broadcast([P, SB, ST]), ALU.mult))
                c.settle()
                g.tensor_tensor(d, d, modT[:, shift * KT + k, 1:NSEQ].unsqueeze(2).to_broadcast([P, SB, ST]),
                                ALU.add).then_inc(hf_ready, 1)

        def store_prompt_state(c, l, h):
            pool.wait_ge(stp_ev, c.head)
            dma(st_prompt[l, 0, bass.ds(h, 1)].rearrange("a d v -> d (a v)"), stp[:, :]).then_inc(stp_out, 16)

        def store_sample_state(c, l, h):
            pool.wait_ge(pair_ev, c.head * 4 + P0)
            dma(st_sample[l, :, bass.ds(h, 1)].rearrange("b a d v -> d b (a v)"), st[:, :, :]).then_inc(st_out, 16)

        def power_o(c):
            pool.wait_ge(o_msr, c.head)
            g.tensor_tensor(o_rs, o_ms, mhalf[:, 0:3], ALU.pow).then_inc(o_pow, 1)

        def head(c, l, h, prev):
            H = c.head
            if prev is not None:
                power_o(c)
            if prev is not None:
                store_prompt_state(c, l, prev)
            pool.wait_ge(qk_msr, H + 1)
            g.tensor_tensor(qk_rs, qk_ms, mhalf[:, 0:6], ALU.pow).then_inc(qk_pow, 1)
            if prev is not None:
                store_sample_state(c, l, prev)
            pool.wait_ge(pair_ev, H * 4 + P0)
            dma(dec[:, :], decay[bass.ds(h, 1)].rearrange("a p n -> p (a n)")).then_inc(dec_full, 16)
            pool.wait_ge(qk_norm, H + 1)
            dma(k_prompt[l, 0, :, bass.ds(h, 1), :].rearrange("(t p) h d -> p t (h d)", p=P),
                qkA[:, 0:2, DH:2 * DH]).then_inc(ka_out, 16)
            dma(k_sample[l, :, :, bass.ds(h, 1), :].rearrange("b t h d -> (b t) (h d)"),
                qkA[:, 2, DH:2 * DH]).then_inc(ka_out, 16)
            pool.wait_ge(st_out, H * 16)
            for t in range(2):
                dma(st[:, 4 * t:4 * t + 4, :], state_ret[l, 4 * t:4 * t + 4, bass.ds(h, 1), :, :]
                    .rearrange("b h d v -> d b (h v)")).then_inc(st_full, 16)
            pool.wait_ge(rope_ready, H + 1)
            pool.wait_ge(dec_full, H * 16 + 16)
            pool.wait_ge(stp_done, H)
            g.tensor_tensor(kdec[:, :, :], qkR[:, 0:2, DH:2 * DH],
                            dec[:, DC_K:DC_K + 2].unsqueeze(2).to_broadcast([P, 2, DH]), ALU.mult).then_inc(kdec_ready, 1)
            pool.wait_ge(ss_done, H + 1)
            g.tensor_tensor(kdm, qkR[:, 2:3, DH:2 * DH].to_broadcast([P, SB, DH]),
                            dec[:, DC_SEQ:DC_SEQ + SB].unsqueeze(2).to_broadcast([P, SB, DH]), ALU.mult).then_inc(kdm_ready, 1)

        with pool.Fori(0, DEPTH) as l:
            with cnt.turn({"norm": 1}) as c:
                norm_sample(c, 0)
            with cnt.turn({"head": 1}) as c:
                head(c, l, 0, None)
            with pool.Fori(0, HEADS - 1) as h, cnt.turn({"head": 1}) as c:
                head(c, l, h + 1, h)
            with cnt.turn({}, use=("head",)) as c:
                power_o(c)
                store_prompt_state(c, l, HEADS - 1)
                store_sample_state(c, l, HEADS - 1)
            with cnt.turn({"norm": 1}) as c:
                norm_sample(c, 3)
        pool.wait_ge(va_out, DEPTH * 32)
        pool.wait_ge(ka_out, DEPTH * HEADS * 32)
        pool.wait_ge(stp_out, DEPTH * HEADS * 16)
        pool.wait_ge(st_out, DEPTH * HEADS * 16)

    @block.scalar
    def _(act):
        a = nc.scalar
        cnt = Counts(act, act_own, Counts.NAMES)
        act.dma_start(rbrow[:, :], rel_bias.rearrange("l h n -> (l h) n")).then_inc(ld_rb, 16)
        act.dma_start(crow[0:1, :], c_prompt).then_inc(ld_c, 16)
        act.dma_start(crow[1:NSEQ, :], c_sample).then_inc(ld_c, 16)
        for l in range(DEPTH):
            for src, r, n in ((norm_mix_g, 0, KT), (norm_ffn_g, KT, KT), (ret_gn_g, 2 * KT, 2 * KT)):
                act.dma_start(grow[32 * l + r:32 * l + r + n, :], src[l].rearrange("(k p) -> k p", p=P)).then_inc(ld_g, 16)
        act.dma_start(rope_t[:, :, :, :], rope).then_inc(ld_k, 16)

        def copy(out, in_):
            return a.activation(out, in_, ACT.Copy)

        def high(c, j):
            act.wait_ge(raw_full[j % RAW], (c.round + j // RAW + 1) * 32)
            act.wait_ge(blk_used, c.blk + (j + 1))
            copy(whi[:, j % SPLIT, :, :], raw[:, j % RAW, :, :]).then_inc(blk_hi, 1)

        def acc(c, entry):
            _, _, kind, n = entry
            act.wait_ge(acc_ready, c.ready + n) if kind == "ready" else act.wait_ge(blk_used, c.blk + n)

        ada0_load(act, 1)
        ada0_load(act, 3)
        act.wait_ge(ld_c, 32)
        for l in range(DEPTH):
            act.dma_start(gqk[:, l, 0:DH], q_norm_g[l].partition_broadcast(P)).then_inc(ld_k, 16)
            act.dma_start(gqk[:, l, DH:2 * DH], k_norm_g[l].partition_broadcast(P)).then_inc(ld_k, 16)
        a.activation(csil[:, :], crow[:, :], ACT.Silu).then_inc(csil_ready, 1)
        for n in (1, 3, 5):
            act.wait_ge(pre_pe, n + 3)
            copy(xT[:, n % 2 * 4:n % 2 * 4 + 4, n // 2 * P:(n // 2 + 1) * P],
                 X[n % 4][:, :].rearrange("p (k t) -> p k t", k=4)).then_inc(pre_a, 1)

        def norm(c):
            act.wait_ge(res_ready, c.norm * KT)
            for k in range(KT):
                if k >= 2:
                    act.wait_ge(sq_used, c.norm * KT + (k - 1))
                a.activation(sq[:, k % 2, :], xT[:, k, :], ACT.Square).then_inc(sq_ready, 1)
            act.wait_ge(sq_used, c.norm * KT + KT)
            a.activation(std[:, :], X[0][:, 0:TOK], ACT.Sqrt, scale=1.0 / DM, bias=eps_t[:, 0:1]).then_inc(std_ready, 1)
            for k in range(KT):
                act.wait_ge(hf_ready, c.norm * KT + (k + 1))
                act.wait_ge(hp_ready, c.norm * KT + (k + 1))
                copy(hhi[:, k, :], hf[:, k % 2, :]).then_inc(hhi_ready, 1)

        def squares(c):
            act.wait_ge(o_done, c.head)
            for t, src in enumerate((X[2][:, 0:DV], X[2][:, DV:2 * DV], X[0][:, 0:DV])):
                a.activation(onorm[:, t, :], src, ACT.Square, accum_out=o_ss[:, t:t + 1]).then_inc(oss_ready, 1)
            act.wait_ge(stp_done, c.head)
            copy(stp[:, :], X[1][:, 0:DV]).then_inc(stp_ev, 1)

        def attended(c, h):
            act.wait_ge(oaT_done, c.head)
            copy(y_att[:, bass.ds(h, 1), :].rearrange("p a t -> p (a t)"), X[3][:, 0:TOK]).then_inc(oaT_ev, 1)

        def head(c, h, prev):
            H = c.head
            gr = S_HEAD.groups

            def out_of(group, dst):
                for t, e in enumerate(group):
                    acc(c, e)
                    copy(dst[:, t, :], G[e[0]][:, 0:2 * DH]).then_inc(acc_free[e[0]], 1)

            def exponentials(lo, n, w):
                a.activation(prob[:, lo:lo + w], prob[:, lo:lo + w], ACT.Exp, bias=negmax[:, n:n + 1],
                             accum_out=rowsum[:, n:n + 1]).then_inc(exp_done, 1)

            high(c, 1)
            if prev is not None:
                squares(c)
            high(c, 2)
            if prev is not None:
                attended(c, prev)
            act.wait_ge(ta_done, H)
            act.wait_ge(ka_out, H * 32)
            out_of(gr[0], qkA)
            high(c, 3)
            high(c, 4)
            act.wait_ge(orT_ev, H * 2)
            out_of(gr[1], rraw)
            high(c, 5)
            act.wait_ge(ta_done, H + 1)
            c.op(copy(qaT[:, :], X[0][:, 0:TOK]))
            c.op(copy(par(qa_par[:, 0, :], 0), par(X[0][:, PR:TOK], 0)))
            copy(par(qa_par[:, 1, :], 1), par(X[0][:, PR:TOK], 1)).then_inc(qa_ev, 1)
            act.wait_ge(kt_done[0], H + 1)
            act.wait_ge(pair_done, H * 4 + P0)
            copy(kcT[:, :, P:2 * P], X[3][:, :].rearrange("p (g k) -> p g k", g=4)).then_inc(kt_a[0], 1)
            high(c, 6)
            act.wait_ge(kt_done[1], H + 1)
            act.wait_ge(sn_done, H + 1)
            copy(kcT[:, :, P:2 * P], X[1][:, :].rearrange("p (g k) -> p g k", g=4)).then_inc(kt_a[1], 1)
            act.wait_ge(maxp_ready, H + 1)
            exponentials(B_Q0, 0, P)
            exponentials(B_Q1, 1, SEQ)
            act.wait_ge(pair_done, H * 4 + P0)
            out_of(gr[2], vR)
            high(c, 7)
            act.wait_ge(tr_done, H + 1)
            copy(krT[:, :], X[1][:, 0:TOK]).then_inc(kr_ev, 1)
            act.wait_ge(maxs_ready, H + 1)
            exponentials(B_C, 2, PAST + P)
            high(c, 8)
            act.wait_ge(stp_out, H * 16)
            act.wait_ge(pt_done, H + 1)
            for e in range(2):
                c.op(copy(p_par[:, :, e, :].rearrange("p k (g e t) -> p k g e t", g=4, e=2)[:, :, :, e, :],
                          X[0][:, 0:2 * P].rearrange("p (k g e t) -> p k g e t", k=2, g=4, e=2)[:, :, :, e, :]))
            copy(pT[:, 0:2 * P], X[0][:, 2 * P:4 * P]).then_inc(pt_a, 1)
            for n, e in enumerate(gr[3]):
                acc(c, e)
                a.activation(zs[:, n, :], G[e[0]][:, 0:TOK], ACT.Silu).then_inc(acc_free[e[0]], 1)

        def branch_high(c, l, part):
            if part == 0:
                act.wait_ge(pv_done, c.head)
                act.wait_ge(kdm_ready, c.head)
                act.wait_ge(ka_out, c.head * 32)
                act.wait_ge(va_out, l * 32 + 32)
            if part == 3:
                act.wait_ge(orT_ev, c.head * 2)
            if part == 5:
                act.wait_ge(oaT_ev, c.head)
            for n in range(4 * part, 4 * part + 4):
                src = y_ret[:, n, :] if n < 2 * HEADS else y_att[:, n - 2 * HEADS, :]
                copy(yhi[:, n, :], src).then_inc(yhi_ready, 1)

        def merge(c, l, i, first):
            for j in range(20):
                high(c, j + 1)
                if first and j == 0:
                    squares(c)
                if first and j == 1:
                    attended(c, HEADS - 1)
                if first and j < 6:
                    branch_high(c, l, j)
                g, r = j // 10, j % 10
                if r in (1, 7):
                    for e in (S_MERGE.groups[4 * g + 1] if r == 7 else S_MERGE.groups[3] if g else []):
                        act.wait_ge(acc_free[e[0]], c.now[f"bank{e[0]}"] + (e[1] + 1))
                    if r == 1 and not g:
                        for b in (2, 3):
                            act.wait_ge(acc_free[b], c.now[f"bank{b}"])
                    for n, e in enumerate(S_MERGE.groups[4 * g + (2 if r == 7 else 0)]):
                        acc(c, e)
                        a.activation(gate[:, n, :], G[e[0]][:, 0:TOK], ACT.Sigmoid).then_inc(acc_free[e[0]], 1)
                if r == 9:
                    for n in range(2):
                        act.wait_ge(mix_ready, c.mix + (2 * g + n + 1))
                        copy(mhi[:, bass.ds(i * 4 + (2 * g + n), 1), :].rearrange("p a t -> p (a t)"),
                             mix[:, n, :]).then_inc(mhi_ready, 1)

        act.wait_ge(ada_mm, ADA0)
        act.wait_ge(pre_d, 5)
        act.wait_ge(consts, 1)
        with cnt.turn({}, use=("blk", "round")) as c:
            high(c, 0)
        with act.Fori(0, DEPTH) as l:
            with cnt.turn({"norm": 1}) as c:
                norm(c)
            with act.Fori(0, S_V.turns) as i, cnt.turn(S_V.adds) as c:
                for j in range(4):
                    high(c, j + 1)
                    if j % 2:
                        for t, e in enumerate(S_V.groups[j // 2]):
                            acc(c, e)
                            copy(vaT[:, t, bass.ds(i * (2 * BC) + j // 2 * BC, BC)],
                                 G[e[0]][:, 0:BC]).then_inc(acc_free[e[0]], 1)
            with cnt.turn({}, use=("bank0", "bank1", "bank3")) as c:
                for b in (0, 1, 3):
                    act.wait_ge(acc_free[b], c.now[f"bank{b}"])
                act.dma_start(v_prompt[bass.ds(l, 1), 0].rearrange("l (t p) h d -> p (l t) (h d)", p=P),
                              vaT[:, 0:2, :]).then_inc(va_out, 16)
                act.dma_start(v_sample[bass.ds(l, 1)].rearrange("l b t h d -> (l b t) (h d)"),
                              vaT[:, 2, :]).then_inc(va_out, 16)
            with cnt.turn(S_HEAD.adds) as c:
                head(c, 0, None)
            with act.Fori(0, HEADS - 1) as h, cnt.turn(S_HEAD.adds) as c:
                head(c, h + 1, h)
            with cnt.turn(S_MERGE.adds, also=("head",)) as c:
                merge(c, l, 0, True)
            with act.Fori(0, S_MERGE.turns - 1) as i, cnt.turn(S_MERGE.adds) as c:
                merge(c, l, i + 1, False)
            with act.Fori(0, S_OUT.turns) as i, cnt.turn(S_OUT.adds) as c:
                for j in range(4):
                    high(c, j + 1)
            with cnt.turn({"norm": 1}) as c:
                norm(c)
            with act.Fori(0, S_UP.turns) as i, cnt.turn(S_UP.adds) as c:
                for j in range(4):
                    high(c, j + 1)
                    if j % 2:
                        for n, e in enumerate(S_UP.groups[j // 2]):
                            q = j // 2 * 2 + n
                            acc(c, e)
                            act.wait_ge(f_ready, c.ff + (q - 1 + F0))
                            a.activation(frelu[:, n, :], G[e[0]][:, 0:TOK], ACT.Relu).then_inc(acc_free[e[0]], 1)
                            act.wait_ge(acc_free[e[0]], c.now[f"bank{e[0]}"] + (e[1] + 1))
                            a.activation(fhi[:, bass.ds(i * 4 + q, 1), :].rearrange("p a t -> p (a t)"),
                                         frelu[:, n, :], ACT.Square).then_inc(f_hi, 1)
            with act.Fori(0, S_DOWN.turns) as i, cnt.turn(S_DOWN.adds) as c:
                for j in range(8):
                    high(c, j + 1)
        for n in (1, 3, 5):
            act.wait_ge(fin_pe, n + 1)
            copy(xtok[:, n // 2, 4 * P:8 * P], X[n % 4][:, :]).then_inc(fin_a, 1)
        act.wait_ge(va_out, DEPTH * 32)

    @block.vector
    def _(dve):
        v = nc.vector
        cnt = Counts(dve, dve_own, Counts.NAMES)
        dve.sem_inc(blk_split, RAW)
        dve.sem_inc(f_ready, F0)
        dve.sem_inc(pair_ev, P0)
        dve.sem_inc(h_ready, H0)
        dve.sem_inc(m_ready, M0)

        def low(c, j):
            dve.wait_ge(blk_hi, c.blk + (j + 1))
            v.tensor_tensor(wlo[:, j % SPLIT, :, :], raw[:, j % RAW, :, :],
                            whi[:, j % SPLIT, :, :].bitcast(F32), ALU.subtract).then_inc(blk_split, 1)

        def acc(c, entry):
            _, _, kind, n = entry
            dve.wait_ge(acc_ready, c.ready + n) if kind == "ready" else dve.wait_ge(blk_used, c.blk + n)

        def copied(c, group):
            for b, use, _, _ in group:
                dve.wait_ge(acc_free[b], c.now[f"bank{b}"] + (use + 1))

        dve.wait_ge(ld_rb, 16)
        far = BAND_TOP - CLIP + 1
        v.tensor_copy(band[:, 0:far], rbrow[:, 2 * CLIP:2 * CLIP + 1].to_broadcast([DEPTH * HEADS, far])).then_inc(dve_own, 1)
        v.tensor_copy(band[:, far:BAND], rbrow[:, 0:2 * CLIP][:, ::-1]).then_inc(band_ready, 1)
        dve.reg_add(cnt.regs["own"], cnt.regs["own"], 1)
        dve.wait_ge(pre_pe, 1)
        v.tensor_copy(gT[:, :], G[0][:, 0:64]).then_inc(pre_d, 1)
        dve.wait_ge(pre_pe, 2)
        v.tensor_copy(cT[:, :, 0:NSEQ], G[1][:, 0:KT * 16].rearrange("p (k b) -> p k b", k=KT)[:, :, 0:NSEQ]).then_inc(pre_d, 1)
        for n in (0, 2, 4):
            dve.wait_ge(pre_pe, n + 3)
            v.tensor_copy(xT[:, n % 2 * 4:n % 2 * 4 + 4, n // 2 * P:(n // 2 + 1) * P],
                          X[n % 4][:, :].rearrange("p (k t) -> p k t", k=4)).then_inc(pre_d, 1)
        dve.wait_ge(pre_a, 3)
        dve.wait_ge(ld_k, 80)

        def ada_rows(c, x):
            dve.wait_ge(ada_mm, c.ada + (ADA0 + 1))
            v.tensor_copy(ada_s[:, :], x[:, 0:P]).then_inc(ada_cp, 1)

        def ada_cols(c, s, x):
            dve.wait_ge(ada_tr, c.ada + (ADA0 + 1))
            v.tensor_copy(modT[:, bass.ds(s * 4, 4), :],
                          x[:, 0:P].rearrange("p (g b) -> p g b", g=4)[:, :, 0:NSEQ]).then_inc(mod_ready, 1)

        def norm(c, shift, gain):
            for_layer = gT[:, gain]
            c.op(v.scalar_tensor_tensor(out=modA[:, :, :], in0=modT[:, (shift + 1) * KT:(shift + 2) * KT, :], scalar=1.0,
                                        in1=for_layer.unsqueeze(2).to_broadcast([P, KT, NSEQ]), op0=ALU.add, op1=ALU.mult))
            dve.wait_ge(std_ready, c.norm + 1)
            c.op(v.reciprocal(rstd[:, :], std[:, :]))
            c.settle()

            def lo(k):
                dve.wait_ge(hhi_ready, c.norm * KT + (k + 1))
                v.tensor_tensor(hlo[:, k, :], hf[:, k % 2, :], hhi[:, k, :].bitcast(F32), ALU.subtract).then_inc(h_ready, 1)

            for k in range(KT):
                if k >= 2:
                    dve.wait_ge(hf_ready, c.norm * KT + (k - 1))
                    dve.wait_ge(hp_ready, c.norm * KT + (k - 1))
                v.tensor_tensor(hn[:, k % 2, :], xT[:, k, :], rstd[:, :], ALU.mult).then_inc(hn_ready, 1)
                if k >= 2:
                    dve.wait_ge(h_ready, c.norm * KT + (k - 1 + H0))
                dve.wait_ge(hn_ready, c.norm * KT + (k + 1))
                v.tensor_scalar(hf[:, k % 2, 0:PR], hn[:, k % 2, 0:PR], modA[:, k, 0:1],
                                modT[:, shift * KT + k, 0:1], ALU.mult, ALU.add).then_inc(hp_ready, 1)
                if k >= 1:
                    lo(k - 1)
            lo(KT - 1)

        def residual(c, x_tile, gate_of, e, t):
            acc(c, e)
            c.op(v.tensor_tensor(t[:, 0:PR], G[e[0]][:, 0:PR], gate_of[:, 0:1].to_broadcast([P, PR]), ALU.mult))
            v.tensor_tensor(seqs(t[:, PR:TOK]), seqs(G[e[0]][:, PR:TOK]),
                            gate_of[:, 1:NSEQ].unsqueeze(2).to_broadcast([P, SB, ST]), ALU.mult).then_inc(acc_free[e[0]], 1)
            dve.wait_ge(acc_free[e[0]], c.now[f"bank{e[0]}"] + (e[1] + 1))
            v.tensor_tensor(x_tile, x_tile, t, ALU.add).then_inc(res_ready, 1)

        def normed(c, l, h):
            dve.wait_ge(pv_done, c.head)
            c.op(v.tensor_copy(gcol[:, :], gT[:, bass.ds(l * 32 + h * 2 + 16, 2)]))
            c.settle()
            v.tensor_tensor(oa[:, :, :], X[3][:, 0:TOK].rearrange("p (t d) -> p t d", t=NT),
                            rinv.unsqueeze(2).to_broadcast([P, NT, DH]), ALU.mult).then_inc(oa_ready, 1)
            dve.wait_ge(oss_ready, c.head * 3)
            v.tensor_scalar(o_ms, o_ss, 1.0 / DV, EPS, ALU.mult, ALU.add).then_inc(o_msr, 1)
            dve.wait_ge(o_pow, c.head)
            c.op(v.tensor_tensor(onorm[:, 0:2, :], X[2][:, :].rearrange("p (t v) -> p t v", t=2),
                                 o_rs[:, 0:2].unsqueeze(2).to_broadcast([P, 2, DV]), ALU.mult))
            v.tensor_scalar(onorm[:, 2, :], X[0][:, 0:DV], o_rs[:, 2:3], None, ALU.mult).then_inc(on_ready, 1)

        def pair(c, q):
            dve.wait_ge(pair_done, c.head * 4 + (q + 1))
            s2 = st[:, 2 * q:2 * q + 2, :].rearrange("p b v -> p (b v)")
            v.scalar_tensor_tensor(out=s2, in0=s2, scalar=dec[:, DC_S:DC_S + 1], in1=X[PAIR_BANK[q]][:, :],
                                   op0=ALU.mult, op1=ALU.add).then_inc(pair_ev, 1)

        def gated(c, h):
            for b in (1, 2):
                dve.wait_ge(acc_free[b], c.now[f"bank{b}"])
            dve.wait_ge(orT_done, c.head)
            for n in range(2):
                v.scalar_tensor_tensor(out=y_ret[:, bass.ds(h * 2 + n, 1), :].rearrange("p a t -> p (a t)"),
                                       in0=X[2 * n][:, 0:TOK], scalar=gcol[:, n:n + 1], in1=zs[:, n, :],
                                       op0=ALU.mult, op1=ALU.mult).then_inc(orT_ev, 1)

        def head(c, l, h, prev):
            H = c.head
            gr = S_HEAD.groups
            low(c, 1)
            if prev is not None:
                normed(c, l, prev)
            low(c, 2)
            if prev is not None:
                pair(c, 0)
            low(c, 3)
            copied(c, gr[0])
            qk = qkA[:, :, :].rearrange("p t (a d) -> p (t a) d", a=2)
            tq = tmp[:, :].rearrange("p (a d) -> p a d", d=DH)
            c.op(v.tensor_tensor(tq, qk, qk, ALU.mult))
            c.settle()
            c.op(v.tensor_reduce(qk_ss, tq, axis=AXX, op=ALU.add))
            c.settle()
            v.tensor_scalar(qk_ms, qk_ss, 1.0 / DH, EPS, ALU.mult, ALU.add).then_inc(qk_msr, 1)
            if prev is not None:
                gated(c, prev)
                pair(c, 1)
            dve.wait_ge(qk_pow, H + 1)
            c.op(v.tensor_tensor(qk, qk, qk_rs.unsqueeze(2).to_broadcast([P, 6, DH]), ALU.mult))
            c.settle()
            v.tensor_tensor(qkA[:, :, :], qkA[:, :, :], gqk[:, bass.ds(l, 1), :].to_broadcast([P, NT, 2 * DH]),
                            ALU.mult).then_inc(qk_norm, 1)
            low(c, 4)
            if prev is not None:
                pair(c, 2)
                pair(c, 3)
            ada_rows(c, X[3])
            ada_cols(c, h + ADA0, X[3])
            dve.wait_ge(ta_done, H + 1)
            v.tensor_copy(kaT[:, :], X[1][:, 0:TOK]).then_inc(ka_ev, 1)
            low(c, 5)
            dve.wait_ge(kt_done[0], H + 1)
            v.tensor_copy(kcT[:, :, 0:P], X[2][:, :].rearrange("p (g k) -> p g k", g=4)).then_inc(kt_d[0], 1)
            copied(c, gr[1])
            dve.wait_ge(kdm_ready, H)
            half = DH // 2
            rr = qkZ[:, :].rearrange("p (t a h d) -> p t a h d", t=NT, a=2, h=2)
            ro = qkR[:, :, :].rearrange("p t (a h d) -> p t a h d", a=2, h=2)
            rt = tmp[:, :].rearrange("p (t a h d) -> p t a h d", t=NT, a=2, h=2)
            for t in range(NT):
                c.op(v.tensor_tensor(ro[:, t], rr[:, t], rope_t[:, t:t + 1, 0:1, :].to_broadcast([P, 2, 2, half]), ALU.mult))
                c.op(v.tensor_tensor(rt[:, t], rr[:, t, :, ::-1, :],
                                     rope_t[:, t:t + 1, 1:3, :].to_broadcast([P, 2, 2, half]), ALU.mult))
            c.settle()
            v.tensor_tensor(qkR[:, :, :], qkR[:, :, :], tmp[:, :].rearrange("p (t c) -> p t c", t=NT), ALU.add)\
                .then_inc(rope_ready, 1)
            low(c, 6)
            dve.wait_ge(kt_done[1], H + 1)
            dve.wait_ge(sn_done, H + 1)
            v.tensor_copy(kcT[:, :, 0:P], X[0][:, :].rearrange("p (g k) -> p g k", g=4)).then_inc(kt_d[1], 1)
            dve.wait_ge(sp_done, H + 1)
            dve.wait_ge(bias_full, H * 16 + 16)
            dve.wait_ge(orT_done, H)
            v.scalar_tensor_tensor(out=prob[:, 0:B_C], in0=X[3][:, 0:B_C], scalar=DH ** -0.5, in1=bias[:, 0:B_C],
                                   op0=ALU.mult, op1=ALU.add).then_inc(sp_read, 1)
            dve.wait_ge(sp_read, H + 1)
            c.op(v.tensor_reduce(negmax[:, 0:1], prob[:, B_Q0:B_Q0 + P], axis=AXX, op=ALU.max, negate=True))
            v.tensor_reduce(negmax[:, 1:2], prob[:, B_Q1:B_Q1 + SEQ], axis=AXX, op=ALU.max, negate=True).then_inc(maxp_ready, 1)
            low(c, 7)
            dve.wait_ge(ss_done, H + 1)
            v.scalar_tensor_tensor(out=prob[:, B_C:W_BIAS], in0=X[2][:, 0:PAST + P], scalar=DH ** -0.5,
                                   in1=bias[:, B_C:W_BIAS], op0=ALU.mult, op1=ALU.add).then_inc(ss_read, 1)
            dve.wait_ge(ss_read, H + 1)
            v.tensor_reduce(negmax[:, 2:3], prob[:, B_C:W_BIAS], axis=AXX, op=ALU.max, negate=True).then_inc(maxs_ready, 1)
            dve.wait_ge(tr_done, H + 1)
            dve.wait_ge(dec_full, H * 16 + 16)
            c.op(v.tensor_copy(qrT[:, :], X[0][:, 0:TOK]))
            row = dec[:, DC_ROW:DC_ROW + 64].rearrange("p (g t) -> p g t", g=4)
            c.op(v.tensor_tensor(par(qr_par[:, 0, :], 0), par(X[0][:, PR:TOK], 0), row, ALU.mult))
            v.tensor_tensor(par(qr_par[:, 1, :], 1), par(X[0][:, PR:TOK], 1), row, ALU.mult).then_inc(qr_ev, 1)
            low(c, 8)
            dve.wait_ge(rs_done, H + 1)
            v.tensor_tensor(sdT[:, :], X[2][:, :], dec[:, 0:512], ALU.mult).then_inc(sd_ready, 1)
            dve.wait_ge(pt_done, H + 1)
            v.tensor_copy(pT[:, 2 * P:4 * P], X[1][:, 0:2 * P]).then_inc(pt_d, 1)
            dve.wait_ge(exp_done, H * 3 + 3)
            c.op(v.reciprocal(rinv, rowsum))

        def branch_low(c, l, part):
            if part == 0:
                dve.wait_ge(stp_done, c.head)
            if part == 2:
                dve.wait_ge(pair_ev, c.head * 4 + P0)
                dve.wait_ge(stp_out, c.head * 16)
            if part == 4:
                dve.wait_ge(st_out, c.head * 16)
            for n in range(4 * part, 4 * part + 4):
                src = y_ret[:, n, :] if n < 2 * HEADS else y_att[:, n - 2 * HEADS, :]
                dve.wait_ge(yhi_ready, l * (3 * HEADS) + (n + 1))
                v.tensor_tensor(ylo[:, n, :], src, yhi[:, n, :].bitcast(F32), ALU.subtract).then_inc(y_ready, 1)

        def merge(c, l, i, first):
            for j in range(20):
                low(c, j + 1)
                if first and j == 0:
                    normed(c, l, HEADS - 1)
                    branch_low(c, l, 0)
                if first and j == 1:
                    pair(c, 0)
                    branch_low(c, l, 1)
                if first and j == 2:
                    gated(c, HEADS - 1)
                    pair(c, 1)
                if first and j == 3:
                    pair(c, 2)
                    pair(c, 3)
                    branch_low(c, l, 2)
                if first and j == 4:
                    branch_low(c, l, 3)
                if first and j == 5:
                    branch_low(c, l, 4)
                    branch_low(c, l, 5)
                    dve.wait_ge(y_ready, l * (3 * HEADS) + 3 * HEADS)
                g, r = j // 10, j % 10
                if r == 5:
                    copied(c, S_MERGE.groups[4 * g])
                    for n, e in enumerate(S_MERGE.groups[4 * g + 1]):
                        acc(c, e)
                        v.tensor_tensor(part[:, n, :], G[e[0]][:, 0:TOK], gate[:, n, :], ALU.mult).then_inc(acc_free[e[0]], 1)
                if r == 9:
                    copied(c, S_MERGE.groups[4 * g + 2])
                    for n, e in enumerate(S_MERGE.groups[4 * g + 3]):
                        acc(c, e)
                        v.tensor_tensor(mix[:, n, :], G[e[0]][:, 0:TOK], gate[:, n, :], ALU.mult).then_inc(acc_free[e[0]], 1)
                        dve.wait_ge(acc_free[e[0]], c.now[f"bank{e[0]}"] + (e[1] + 1))
                        v.tensor_tensor(mix[:, n, :], mix[:, n, :], part[:, n, :], ALU.add).then_inc(mix_ready, 1)
                    for n in range(2):
                        dve.wait_ge(mhi_ready, c.mix + (2 * g + n + 1))
                        kt = bass.ds(i * 4 + (2 * g + n), 1)
                        v.tensor_tensor(mlo[:, kt, :].rearrange("p a t -> p (a t)"), mix[:, n, :],
                                        mhi[:, kt, :].rearrange("p a t -> p (a t)").bitcast(F32),
                                        ALU.subtract).then_inc(m_ready, 1)

        for s in range(ADA0):
            dve.wait_ge(ada_mm, s + 1)
            if s:
                dve.wait_ge(ada_tr, s)
            v.tensor_copy(ada_s[:, :], G[s][:, 0:P]).then_inc(ada_cp, 1)
            dve.wait_ge(ada_tr, s + 1)
            v.tensor_copy(modT[:, s * 4:s * 4 + 4, :],
                          G[s][:, 0:P].rearrange("p (g b) -> p g b", g=4)[:, :, 0:NSEQ]).then_inc(mod_ready, 1)
        with cnt.turn({}, use=("blk",)) as c:
            low(c, 0)
        with dve.Fori(0, DEPTH) as l:
            with cnt.turn({"norm": 1}, use=("norm", "res", "ada")) as c:
                dve.wait_ge(mod_ready, c.ada + ADA0)
                norm(c, 0, bass.ds(l * 32, KT))
            with dve.Fori(0, S_V.turns) as i, cnt.turn(S_V.adds) as c:
                for j in range(4):
                    low(c, j + 1)
            with cnt.turn(S_HEAD.adds) as c:
                head(c, l, 0, None)
            with dve.Fori(0, HEADS - 1) as h, cnt.turn(S_HEAD.adds) as c:
                head(c, l, h + 1, h)
            with cnt.turn(S_MERGE.adds, also=("head",)) as c:
                merge(c, l, 0, True)
            with dve.Fori(0, S_MERGE.turns - 1) as i, cnt.turn(S_MERGE.adds) as c:
                merge(c, l, i + 1, False)
            with dve.Fori(0, S_OUT.turns) as i, cnt.turn(S_OUT.adds) as c:
                for j in range(4):
                    low(c, j + 1)
                    if j % 2:
                        for n, e in enumerate(S_OUT.groups[j // 2]):
                            q = i * 4 + (j // 2 * 2 + n)
                            residual(c, xT[:, bass.ds(q, 1), :].rearrange("p a t -> p (a t)"),
                                     modT[:, bass.ds(q + 2 * KT, 1), :].rearrange("p a b -> p (a b)"), e, rtm[:, n, :])
            with cnt.turn({"norm": 1}) as c:
                dve.wait_ge(res_ready, c.norm * KT)
                norm(c, 3, bass.ds(l * 32 + KT, KT))
            with dve.Fori(0, S_UP.turns) as i, cnt.turn(S_UP.adds) as c:
                for j in range(4):
                    low(c, j + 1)
                    if j % 2:
                        for n, e in enumerate(S_UP.groups[j // 2]):
                            q = j // 2 * 2 + n
                            copied(c, [e])
                            c.op(v.tensor_tensor(fsq[:, n, :], frelu[:, n, :], frelu[:, n, :], ALU.mult))
                            c.settle()
                            dve.wait_ge(f_hi, c.ff + (q + 1))
                            kt = bass.ds(i * 4 + q, 1)
                            v.tensor_tensor(flo[:, kt, :].rearrange("p a t -> p (a t)"), fsq[:, n, :],
                                            fhi[:, kt, :].rearrange("p a t -> p (a t)").bitcast(F32),
                                            ALU.subtract).then_inc(f_ready, 1)
            with dve.Fori(0, S_DOWN.turns) as i, cnt.turn(S_DOWN.adds) as c:
                for j in range(8):
                    low(c, j + 1)
                    if j == 5:
                        ada_rows(c, X[3])
                    if j == 6:
                        ada_cols(c, i, X[3])
                for n, e in enumerate(S_DOWN.groups[0]):
                    q = i * 2 + n
                    residual(c, xT[:, bass.ds(q, 1), :].rearrange("p a t -> p (a t)"),
                             modT[:, bass.ds(q + 5 * KT, 1), :].rearrange("p a b -> p (a b)"), e, rtf[:, n, :])
        for n in (0, 2, 4):
            dve.wait_ge(fin_pe, n + 1)
            v.tensor_copy(xtok[:, n // 2, 0:4 * P], X[n % 4][:, :]).then_inc(fin_d, 1)

    @block.tensor
    def _(pe):
        t = nc.tensor
        cnt = Counts(pe, None, tuple(n for n in Counts.NAMES if n != "own"))
        pe.sem_inc(blk_used, SPLIT)
        pe.sem_inc(ada_used, 2)
        pe.sem_inc(pair_done, P0)

        def turned(out, in_, k=P):
            return t.transpose(out, in_, ident[0:k, 0:k])

        pe.wait_ge(consts, 1)
        pe.wait_ge(ld_g, 6 * 16)
        turned(G[0][:, 0:64], grow[:, :], 64).then_inc(pre_pe, 1)
        pe.wait_ge(csil_ready, 1)
        for k in range(KT):
            ins = turned(G[1][:, k * 16:k * 16 + NSEQ], csil[:, k * P:(k + 1) * P], NSEQ)
        ins.then_inc(pre_pe, 1)
        pe.wait_ge(ld_x, 32)
        for n in range(6):
            if n >= 4:
                pe.wait_ge(pre_d, 3) if n == 4 else pe.wait_ge(pre_a, 1)
            for k in range(4):
                kt = n % 2 * 4 + k
                ins = turned(X[n % 4][:, k * P:(k + 1) * P], xtok[:, n // 2, kt * P:(kt + 1) * P])
            ins.then_inc(pre_pe, 1)
        pe.wait_ge(pre_d, 5)
        pe.wait_ge(pre_a, 3)

        def products(c, stage, j, banks, hi, lo, k0, first, last):
            tokens = len(banks) == 3
            pe.wait_ge(blk_split, c.blk + (j + 1 + RAW))
            s = j % SPLIT
            for n, (b, use, _, _) in enumerate(banks):
                if first:
                    pe.wait_ge(acc_free[b], c.now[f"bank{b}"] + use if use else c.now[f"bank{b}"])
                for k in range(BK):
                    for x, w in ((hi, whi), (lo, whi), (hi, wlo)):
                        start = first and k == 0 and x is hi and w is whi
                        stop = last and k == BK - 1 and w is wlo
                        if tokens:
                            ins = t.matmul(G[b][:, 0:BC], x[:, k0 + k, n * P:(n + 1) * P], w[:, s, k, :],
                                           start=start, stop=stop)
                        else:
                            ins = t.matmul(G[b][:, 0:TOK], w[:, s, k, n * P:(n + 1) * P], x[:, k0 + k, :],
                                           start=start, stop=stop)
                if n == len(banks) - 1:
                    ins.then_inc(blk_used, 1)
                elif last:
                    ins.then_inc(acc_ready, 1)

        def norm(c):
            pe.wait_ge(std_ready, c.norm)
            pe.wait_ge(orT_ev, c.head * 2)
            for k in range(KT):
                pe.wait_ge(sq_ready, c.norm * KT + (k + 1))
                t.matmul(X[0][:, 0:TOK], ones[:, :], sq[:, k % 2, :], start=(k == 0), stop=(k == KT - 1)).then_inc(sq_used, 1)

        def ada_products(c, half):
            if half == 0:
                pe.wait_ge(mod_ready, c.ada + ADA0)
            else:
                pe.wait_ge(ada_bfull, c.ada * 16 + 16)
            for q in (2 * half, 2 * half + 1):
                pe.wait_ge(ada_full[q % 2], c.ada * 32 + (q // 2 * 16 + 16))
                for k in range(2):
                    for g in range(4):
                        ins = t.matmul(X[3][32 * g:32 * g + 32, 0:P], cT[:, 2 * q + k, :], ada_w[:, q % 2, k, g * P:(g + 1) * P],
                                       start=(q == 0 and k == 0), stop=False, skip_group_check=True)
                ins.then_inc(ada_used, 1)
            if half == 1:
                for g in range(4):
                    ins = t.matmul(X[3][32 * g:32 * g + 32, 0:P], ones[0:1, 0:32], ada_b[0:1, g * P:(g + 1) * P],
                                   start=False, stop=True, skip_group_check=True)
                ins.then_inc(ada_mm, 1)

        def ada_turned(c):
            pe.wait_ge(ada_cp, c.ada + (ADA0 + 1))
            turned(X[3][:, 0:P], ada_s[:, :]).then_inc(ada_tr, 1)

        def pair(c, q):
            x = X[PAIR_BANK[q]]
            mm(x[:, 0:DV], kdm[:, 2 * q, :], vR[:, 2, :])
            mm(x[:, DV:2 * DV], kdm[:, 2 * q + 1, :], vR[:, 2, :]).then_inc(pair_done, 1)

        def attended(c):
            pe.wait_ge(stp_ev, c.head)
            pe.wait_ge(kdm_ready, c.head)
            pair(c, 0)
            pe.wait_ge(oa_ready, c.head)
            for n in range(NT):
                ins = turned(X[3][:, n * P:(n + 1) * P], oa[:, n, :])
            ins.then_inc(oaT_done, 1)

        def retained(c):
            pe.wait_ge(pair_ev, c.head * 4 + 1)
            pair(c, 1)
            pe.wait_ge(on_ready, c.head)
            for r in range(2):
                for n in range(NT):
                    ins = turned(X[2 * r][:, n * P:(n + 1) * P], onorm[:, n, r * P:(r + 1) * P])
            ins.then_inc(orT_done, 1)

        def last_states(c):
            pe.wait_ge(orT_ev, c.head * 2)
            pair(c, 2)
            pair(c, 3)

        def mm(out, lhsT, rhs, start=True, stop=True):
            return t.matmul(out, lhsT, rhs, start=start, stop=stop, skip_group_check=True)

        def head(c, h, prev):
            H = c.head
            gr = S_HEAD.groups
            hd = bass.ds(h * DH, DH)

            def gemm(j):
                products(c, S_HEAD, j, gr[j // 2], hhi, hlo, j % 2 * BK, j % 2 == 0, j % 2 == 1)

            def cached_scores(e):
                for g in range(4):
                    ins = mm(X[2][32 * g:32 * g + 32, 0:PAST], qa_par[:, e, 32 * g:32 * g + 32], kcT[:, g, :],
                             start=(e == 0), stop=(e == 1))
                return ins

            def keys_turned(e, banks):
                pe.wait_ge(kc_full[e], H * 32 + 32)
                for kt in range(2):
                    for g in range(4):
                        ins = turned(X[banks[kt]][:, g * P:(g + 1) * P], kc[:, e, kt, g, :])
                ins.then_inc(kt_done[e], 1)

            gemm(0)
            if prev is not None:
                attended(c)
            gemm(1)
            if prev is not None:
                retained(c)
            pe.wait_ge(oaT_ev, H)
            ada_products(c, 0)
            gemm(2)
            if prev is not None:
                last_states(c)
            ada_products(c, 1)
            gemm(3)
            ada_turned(c)
            pe.wait_ge(qk_norm, H + 1)
            pe.wait_ge(pair_ev, H * 4 + P0)
            for n in range(NT):
                turned(X[0][:, n * P:(n + 1) * P], qkA[:, n, 0:DH])
            for n in range(NT):
                ins = turned(X[1][:, n * P:(n + 1) * P], qkA[:, n, DH:2 * DH])
            ins.then_inc(ta_done, 1)
            pe.wait_ge(mod_ready, c.ada + (ADA0 + 1))
            keys_turned(0, (2, 3))
            gemm(4)
            pe.wait_ge(qa_ev, H + 1)
            pe.wait_ge(ka_ev, H + 1)
            keys_turned(1, (0, 1))
            pe.wait_ge(kt_d[0], H + 1)
            pe.wait_ge(kt_a[0], H + 1)
            mm(X[2][:, PAST:PAST + P], qaT[:, PR:TOK], kaT[:, PR:TOK])
            cached_scores(0).then_inc(sn_done, 1)
            mm(X[3][:, 0:P], qaT[:, 0:P], kaT[:, 0:P])
            mm(X[3][:, P:3 * P], qaT[:, P:2 * P], kaT[:, 0:2 * P]).then_inc(sp_done, 1)
            gemm(5)
            pe.wait_ge(kt_d[1], H + 1)
            pe.wait_ge(kt_a[1], H + 1)
            cached_scores(1).then_inc(ss_done, 1)
            pe.wait_ge(rope_ready, H + 1)
            for n in range(NT):
                turned(X[0][:, n * P:(n + 1) * P], qkR[:, n, 0:DH])
            for n in range(NT):
                ins = turned(X[1][:, n * P:(n + 1) * P], qkR[:, n, DH:2 * DH])
            ins.then_inc(tr_done, 1)
            gemm(6)
            pe.wait_ge(ss_read, H + 1)
            pe.wait_ge(qr_ev, H + 1)
            pe.wait_ge(kr_ev, H + 1)
            mm(X[2][:, 0:256], krT[:, 0:P], qrT[:, 0:2 * P])
            mm(X[2][:, 256:384], krT[:, P:2 * P], qrT[:, P:2 * P])
            mm(X[2][:, 384:512], krT[:, PR:TOK], qrT[:, PR:TOK]).then_inc(rs_done, 1)
            pe.wait_ge(exp_done, H * 3 + 3)
            for n, at in enumerate((B_C, B_C + P, B_N, B_Q0)):
                turned(X[0][:, n * P:(n + 1) * P], prob[:, at:at + P])
            for n in range(2):
                ins = turned(X[1][:, n * P:(n + 1) * P], prob[:, B_Q1 + n * P:B_Q1 + (n + 1) * P])
            ins.then_inc(pt_done, 1)
            gemm(7)
            pe.wait_ge(pt_a, H + 1)
            pe.wait_ge(pt_d, H + 1)
            pe.wait_ge(sp_read, H + 1)
            pe.wait_ge(vc_full, H * 32 + 32)
            mm(X[3][:, 0:P], pT[:, P:2 * P], vaT[:, 0, hd])
            mm(X[3][:, P:2 * P], pT[:, 2 * P:3 * P], vaT[:, 0, hd], stop=False)
            mm(X[3][:, P:2 * P], pT[:, 3 * P:4 * P], vaT[:, 1, hd], start=False)
            mm(X[3][:, 2 * P:3 * P], pT[:, 0:P], vaT[:, 2, hd], stop=False)
            for kt in range(2):
                for e in range(2):
                    for g in range(4):
                        ins = mm(X[3][32 * g:32 * g + 32, 2 * P:3 * P], p_par[:, kt, e, 32 * g:32 * g + 32],
                                 vc[:, kt, 2 * g + e, :], start=False, stop=(kt == 1 and e == 1))
            ins.then_inc(pv_done, 1)
            pe.wait_ge(sd_ready, H + 1)
            for b in (0, 2, 3):
                pe.wait_ge(acc_free[b], c.now[f"bank{b}"] + ([e[1] for e in gr[2] if e[0] == b][0] + 1))
            mm(X[2][:, 0:DV], sdT[:, 0:P], vR[:, 0, :])
            mm(X[2][:, DV:2 * DV], sdT[:, P:2 * P], vR[:, 0, :], stop=False)
            mm(X[2][:, DV:2 * DV], sdT[:, 2 * P:3 * P], vR[:, 1, :], start=False)
            mm(X[0][:, 0:DV], sdT[:, 3 * P:4 * P], vR[:, 2, :], stop=False)
            pe.wait_ge(st_full, H * 32 + 32)
            for e in range(2):
                for g in range(4):
                    ins = mm(X[0][32 * g:32 * g + 32, 0:DV], qr_par[:, e, 32 * g:32 * g + 32], st[:, 2 * g + e, :],
                             start=False, stop=(e == 1))
            ins.then_inc(o_done, 1)
            pe.wait_ge(kdec_ready, H + 1)
            mm(X[1][:, 0:DV], kdec[:, 0, :], vR[:, 0, :], stop=False)
            mm(X[1][:, 0:DV], kdec[:, 1, :], vR[:, 1, :], start=False).then_inc(stp_done, 1)

        def merge(c, l, first):
            j = 0
            for g in range(2):
                for n, (hi, lo, k0, ks, y0) in enumerate(((hhi, hlo, 0, 2, None), (yhi, ylo, 0, 4, 0),
                                                          (hhi, hlo, 0, 2, None), (yhi, ylo, 2 * HEADS, 2, 2 * HEADS))):
                    for k in range(ks):
                        if y0 is not None:
                            pe.wait_ge(y_ready, l * (3 * HEADS) + (y0 + (k + 1) * BK))
                        products(c, S_MERGE, j, S_MERGE.groups[4 * g + n], hi, lo, k0 + k * BK, k == 0, k == ks - 1)
                        if first and j < 3:
                            (attended, retained, last_states)[j](c)
                        j += 1

        for s in range(ADA0 + 1):
            if s < ADA0:
                pe.wait_ge(ada0_full[s], 48)
                for k in range(KT + 1):
                    for g in range(4):
                        at = s * ADA_C + g * P
                        ins = mm(G[s][32 * g:32 * g + 32, 0:P], cT[:, k, :] if k < KT else ones[0:1, 0:32],
                                 ada0_w[:, s, k, g * P:(g + 1) * P] if k < KT else ada0_b[0:1, at:at + P],
                                 start=(k == 0), stop=(k == KT))
                ins.then_inc(ada_mm, 1)
            if s:
                pe.wait_ge(ada_cp, s)
                turned(G[s - 1][:, 0:P], ada_s[:, :]).then_inc(ada_tr, 1)
        with pe.Fori(0, DEPTH) as l:
            with cnt.turn({"norm": 1}, use=("norm", "head")) as c:
                norm(c)
            with pe.Fori(0, S_V.turns) as i, cnt.turn(S_V.adds, use=("blk", "bank0", "bank1", "bank2", "bank3", "norm")) as c:
                for j in range(4):
                    pe.wait_ge(h_ready, c.norm * KT + (j % 2 * BK))
                    products(c, S_V, j, S_V.groups[j // 2], hhi, hlo, j % 2 * BK, j % 2 == 0, j % 2 == 1)
            with cnt.turn(S_HEAD.adds) as c:
                head(c, 0, None)
            with pe.Fori(0, HEADS - 1) as h, cnt.turn(S_HEAD.adds) as c:
                head(c, h + 1, h)
            with cnt.turn(S_MERGE.adds, also=("head",)) as c:
                merge(c, l, True)
            with pe.Fori(0, S_MERGE.turns - 1) as i, cnt.turn(S_MERGE.adds) as c:
                merge(c, l, False)
            with pe.Fori(0, S_OUT.turns) as i, cnt.turn(S_OUT.adds, use=("blk", "bank0", "bank1", "bank2", "bank3", "mix")) as c:
                for j in range(4):
                    pe.wait_ge(m_ready, c.mix + j % 2 * BK)
                    products(c, S_OUT, j, S_OUT.groups[j // 2], mhi, mlo, j % 2 * BK, j % 2 == 0, j % 2 == 1)
            with cnt.turn({"norm": 1}, use=("norm", "head")) as c:
                norm(c)
            with pe.Fori(0, S_UP.turns) as i, cnt.turn(S_UP.adds, use=("blk", "bank0", "bank1", "bank2", "bank3", "norm")) as c:
                for j in range(4):
                    pe.wait_ge(h_ready, c.norm * KT + (j % 2 * BK))
                    products(c, S_UP, j, S_UP.groups[j // 2], hhi, hlo, j % 2 * BK, j % 2 == 0, j % 2 == 1)
            with pe.Fori(0, S_DOWN.turns) as i, cnt.turn(S_DOWN.adds, use=("blk", "bank0", "bank1", "ff", "ada")) as c:
                for j in range(8):
                    pe.wait_ge(f_ready, c.ff + (BK * j + 2))
                    products(c, S_DOWN, j, S_DOWN.groups[0], fhi, flo, j * BK, j == 0, j == 7)
                    if j in (2, 4):
                        ada_products(c, j // 4)
                    if j == 5:
                        ada_turned(c)
        pe.wait_ge(res_ready, 2 * DEPTH * KT)
        for n in range(6):
            if n >= 4:
                pe.wait_ge(fin_d, 1) if n == 4 else pe.wait_ge(fin_a, 1)
            for k in range(4):
                ins = turned(X[n % 4][:, k * P:(k + 1) * P], xT[:, n % 2 * 4 + k, n // 2 * P:(n // 2 + 1) * P])
            ins.then_inc(fin_pe, 1)

    ctx.close()


_INS = ["x_prompt", "x_sample", "state_ret", "cache_attn_k", "cache_attn_v", "c_prompt", "c_sample", "w_ada", "b_ada",
        "norm_mix_g", "norm_ffn_g", "w_in", "ret_gn_g", "q_norm_g", "k_norm_g", "rel_bias", "w_br_ret", "w_br_att",
        "w_out", "w_up", "w_down"]
_OUTS = [(1, SEQ, DM), (SB, ST, DM), (DEPTH, 1, HEADS, DH, DV), (DEPTH, 1, SEQ, HEADS, DH), (DEPTH, 1, SEQ, HEADS, DH),
         (DEPTH, SB, HEADS, DH, DV), (DEPTH, SB, ST, HEADS, DH), (DEPTH, SB, ST, HEADS, DH)]


def kernel(**inputs):
    import numpy as _np
    import concourse.bacc as _bacc
    from concourse import mybir as _mybir
    from concourse.bass_utils import run_bass_kernel_spmd as _run

    nc = _bacc.Bacc("TRN2", target_bir_lowering=False, num_devices=1)
    rope, decay = tables()
    given = {**{n: inputs[n] for n in _INS}, "rope": rope, "decay": decay}
    arrays, args = {}, []
    for name, value in given.items():
        a = _np.ascontiguousarray(value)
        arrays[f"in_{name}_dram"] = a
        args.append(nc.dram_tensor(f"in_{name}_dram", a.shape, _mybir.dt.from_np(a.dtype), kind="ExternalInput").ap())
    for i, shape in enumerate(_OUTS):
        args.append(nc.dram_tensor(f"out_{i}_dram", shape, F32, kind="ExternalOutput").ap())
    trunk(nc, *args)
    r = _run(nc, [arrays], core_ids=[0])
    return tuple(r.results[0][f"out_{i}_dram"] for i in range(len(_OUTS)))
```

```python
from contextlib import ExitStack, contextmanager

import numpy as np
import concourse.bass as bass
from concourse import mybir
from concourse.alu_op_type import AluOpType as ALU

F32 = mybir.dt.float32
F32R = mybir.dt.float32r
ACT = mybir.ActivationFunctionType
AXX = mybir.AxisListType.X

P = 128
DM, DEPTH, HEADS, DH, DV, FF = 1024, 2, 8, 128, 256, 4096
SEQ, SB, ST, PAST, CHUNK, CLIP = 256, 8, 16, 256, 64, 128
TOK = SEQ + SB * ST
NT, KT = TOK // P, DM // P
PR = SEQ
NSEQ = 1 + SB
RQK, RV, AW = HEADS * DH, HEADS * DV, HEADS * DH
C_QR, C_KR, C_VR, C_ZR = 0, RQK, 2 * RQK, 2 * RQK + RV
C_QA = C_ZR + RV
C_KA, C_VA, C_MR, C_MA = C_QA + AW, C_QA + 2 * AW, C_QA + 3 * AW, C_QA + 3 * AW + DM
EPS, NEG = 1e-6, -1e30
BK, BC = 4, 256
RAW, SPLIT = 4, 2
W_DEC = 592
DC_K, DC_SEQ, DC_S, DC_ROW = 512, 514, 522, 528
B_Q0, B_Q1, B_C, B_N, W_BIAS = 0, 128, 384, 640, 768
BAND = 400
BAND_TOP = PAST + ST - 1
ADA_C, ADA0 = 512, 4
H0, M0, F0, R0, P0 = KT, 4, 30, KT, 4
NS = 4
PAIR_BANK = (1, 1, 2, 0)
FIN_BANK = (0, 3, 1, 0, 2, 1)


def tables():
    half = DH // 2
    inv = np.float32(10000.0) ** (-np.arange(half, dtype=np.float32) / np.float32(half))
    pos = np.concatenate([np.arange(SEQ), np.tile(PAST + np.arange(ST), SB)]).astype(np.float32)
    ang = (pos[:, None] * inv[None, :]).astype(np.float32)
    cos = np.cos(ang).reshape(NT, P, half)
    sin = np.sin(ang).reshape(NT, P, half)
    rope = np.stack([cos, -sin, sin], axis=2).transpose(1, 0, 2, 3)
    dec = np.zeros((HEADS, P, W_DEC), np.float64)
    p = np.arange(P)[:, None]
    i = np.arange(SEQ)[None, :]
    for h in range(HEADS):
        lg = np.float64(np.log(np.float32(1.0 - 2.0 ** (-5.0 - h))))
        s = DH ** -0.5
        dec[h, :, 0:256] = np.where(i >= p, np.exp(lg * np.maximum(i - p, 0)), 0) * s
        dec[h, :, 256:384] = dec[h, :, 0:128]
        q = np.arange(P)[None, :]
        same = (q // ST == p // ST) & (q >= p)
        dec[h, :, 384:512] = np.where(same, np.exp(lg * np.maximum(q - p, 0)), 0) * s
        dec[h, :, DC_K] = np.exp(lg * (SEQ - 1 - p[:, 0]))
        dec[h, :, DC_K + 1] = np.exp(lg * (SEQ - 1 - P - p[:, 0]))
        for b in range(SB):
            dec[h, :, DC_SEQ + b] = np.where(p[:, 0] // ST == b, np.exp(lg * (ST - 1 - p[:, 0] % ST)), 0)
        dec[h, :, DC_S] = np.exp(lg * ST)
        dec[h, :, DC_ROW:DC_ROW + 64] = np.tile(np.exp(lg * (np.arange(ST) + 1)), 4)[None, :] * s
    return np.ascontiguousarray(rope, np.float32), dec.astype(np.float32)


def plan(groups):
    uses, ready, out = [0] * 4, 0, []
    for banks, last in groups:
        entries = []
        for n, b in enumerate(banks):
            if n < len(banks) - 1:
                ready += 1
                entries.append((b, uses[b], "ready", ready))
            else:
                entries.append((b, uses[b], "block", last + 1 + SPLIT))
            uses[b] += 1
        out.append(entries)
    return out, uses, ready


class Stage:
    def __init__(self, turns, blocks, groups, **more):
        self.turns, self.blocks = turns, blocks
        self.groups, self.uses, self.ready = plan(groups)
        self.adds = {"blk": blocks, "round": blocks // RAW, "ready": self.ready, **more,
                     **{f"bank{b}": self.uses[b] for b in range(4)}}


S_V = Stage(2, 4, [((0, 1, 2), 1), ((3, 0, 1), 3)])
S_HEAD = Stage(HEADS, 8, [((0, 1, 2), 1), ((3, 0, 1), 3), ((2, 3, 0), 5), ((1, 2), 7)], head=1, ada=1)
S_MERGE = Stage(2, 20, [g for c in (0, 10) for g in (((0, 1), c + 1), ((2, 3), c + 5), ((0, 1), c + 7), ((2, 3), c + 9))], mix=4)
S_OUT = Stage(2, 4, [((0, 1), 1), ((2, 3), 3)], res=4)
S_UP = Stage(8, 4, [((0, 1), 1), ((2, 3), 3)], ff=4)
S_DOWN = Stage(4, 8, [((0, 1), 7)], res=2, ada=1)


class Counts:

    NAMES = ("blk", "round", "ready", "bank0", "bank1", "bank2", "bank3", "head", "norm", "ada", "mix", "ff",
             "res", "own")

    def __init__(self, eng, own, names):
        self.eng, self.own_sem = eng, own
        self.regs = {}
        for n in self.NAMES:
            if n in names:
                self.regs[n] = eng.alloc_register(f"count_{n}")
                eng.reg_mov(self.regs[n], 0)

    @contextmanager
    def turn(self, adds, use=None, also=()):
        names = [n for n in self.regs if (use is None and adds.get(n)) or n == "own" or (use and n in use) or n in also]
        self.now = {n: self.eng.snap(self.regs[n]) for n in names}
        self.mine = 0
        yield self
        for n, r in self.regs.items():
            k = self.mine if n == "own" else adds.get(n, 0)
            if k:
                self.eng.reg_add(r, r, k)

    def __getattr__(self, n):
        return self.now[n]

    def op(self, ins):
        self.mine += 1
        return ins.then_inc(self.own_sem, 1)

    def settle(self):
        self.eng.wait_ge(self.own_sem, self.now["own"] + self.mine)


def trunk(nc, x_prompt, x_sample, state_ret, cache_attn_k, cache_attn_v, c_prompt, c_sample, w_ada,
          b_ada, norm_mix_g, norm_ffn_g, w_in, ret_gn_g, q_norm_g, k_norm_g, rel_bias, w_br_ret,
          w_br_att, w_out, w_up, w_down, rope, decay, y_prompt, y_sample, st_prompt, k_prompt,
          v_prompt, st_sample, k_sample, v_sample):
    ctx = ExitStack()

    def sem(name):
        return ctx.enter_context(nc.semaphore(name))

    def sb(name, shape, dt=F32, stack=ctx):
        return stack.enter_context(nc.sbuf_tensor(name, shape, dt))

    raw = sb("raw", [P, RAW, BK, BC])
    whi = sb("whi", [P, SPLIT, BK, BC], F32R)
    wlo = sb("wlo", [P, SPLIT, BK, BC], F32R)
    xT = sb("xT", [P, KT, TOK])
    hhi = sb("hhi", [P, KT, TOK], F32R)
    hlo = sb("hlo", [P, KT, TOK], F32R)
    ada_w = sb("ada_w", [P, 2, 2, ADA_C])
    ada_b = sb("ada_b", [1, ADA_C])
    ada_s = sb("ada_s", [P, P])
    modT = sb("modT", [P, 6 * KT, NSEQ])
    modA = sb("modA", [P, KT, NSEQ])
    cT = sb("cT", [P, KT, 32])
    gT = sb("gT", [P, 64])
    gqk = sb("gqk", [P, DEPTH, 2 * DH])
    rope_t = sb("rope_t", [P, NT, 3, DH // 2])
    ident = sb("ident", [P, P])
    ones = sb("ones", [P, P])
    eps_t = sb("eps_t", [P, 1])
    warm = sb("warm", [P, 1])
    mhalf = sb("mhalf", [P, 8])
    qa_par = sb("qa_par", [P, 2, P])
    qr_par = sb("qr_par", [P, 2, P])
    p_par = sb("p_par", [P, 2, 2, P])
    gcol = sb("gcol", [P, 2])
    small = sb("small", [P, 64])
    qk_ms, qk_rs = small[:, 0:6], small[:, 8:14]
    negmax, rowsum, rinv = small[:, 16:19], small[:, 20:23], small[:, 24:27]
    o_ms, o_rs, qk_ss, o_ss = small[:, 28:31], small[:, 32:35], small[:, 36:42], small[:, 44:47]

    xstack = ExitStack()
    xtok = sb("xtok", [P, NT, DM], stack=xstack)
    crow = sb("crow", [NSEQ, DM], stack=xstack)
    csil = sb("csil", [NSEQ, DM], stack=xstack)
    grow = sb("grow", [64, P], stack=xstack)
    rbrow = sb("rbrow", [DEPTH * HEADS, 2 * CLIP + 1], stack=xstack)
    band = sb("band", [DEPTH * HEADS, BAND], stack=xstack)
    neg = sb("neg", [P, P], stack=xstack)
    ada0_w = sb("ada0_w", [P, ADA0, KT, ADA_C], stack=xstack)
    ada0_b = sb("ada0_b", [1, ADA0 * ADA_C], stack=xstack)
    xstack.close()
    ystack = ExitStack()
    y_ret = sb("y_ret", [P, 2 * HEADS, TOK], stack=ystack)
    y_att = sb("y_att", [P, HEADS, TOK], stack=ystack)
    hstack = ExitStack()
    vaT = sb("va_tok", [P, NT, AW], stack=hstack)
    kc = sb("kc", [P, 2, 2, 4, DH], stack=hstack)
    vc = sb("vc", [P, 2, SB, DH], stack=hstack)
    qkA = sb("qkA", [P, NT, 2 * DH], stack=hstack)
    qkR = sb("qkR", [P, NT, 2 * DH], stack=hstack)
    tmp = sb("tmp", [P, NT * 2 * DH], stack=hstack)
    bias = sb("bias", [P, W_BIAS], stack=hstack)
    qaT = sb("qaT", [P, TOK], stack=hstack)
    kaT = sb("kaT", [P, TOK], stack=hstack)
    qrT = sb("qrT", [P, SEQ + P], stack=hstack)
    krT = sb("krT", [P, TOK], stack=hstack)
    pT = sb("pT", [P, 512], stack=hstack)
    sdT = sb("sdT", [P, 512], stack=hstack)
    kdec = sb("kdec", [P, 2, DH], stack=hstack)
    dec = sb("dec", [P, W_DEC], stack=hstack)
    oa = sb("oa", [P, NT, DH], stack=hstack)
    stp = sb("stp", [P, DV], stack=hstack)
    prob = sb("prob", [P, W_BIAS], stack=hstack)
    vR = sb("vR", [P, NT, DV], stack=hstack)
    qkZ = sb("qkZ", [P, 2 * TOK], stack=hstack)
    kcT = sb("kcT", [P, 4, PAST], stack=hstack)
    st = sb("st", [P, SB, DV], stack=hstack)
    kdm = kcT[:, :, :].rearrange("p a b -> p (a b)").rearrange("p (b d) -> p b d", b=SB)
    rraw = qkZ[:, :].rearrange("p (t c) -> p t c", t=NT)
    zs = qkZ[:, :].rearrange("p (n t) -> p n t", n=2)
    onorm = prob[:, :].rearrange("p (t v) -> p t v", t=NT)
    hstack.close()
    nstack = ExitStack()
    hp = sb("hp", [P, NS, PR], stack=nstack)
    hs = sb("hs", [P, KT, P], stack=nstack)
    std = sb("std", [P, TOK], stack=nstack)
    rstd = sb("rstd", [P, TOK], stack=nstack)
    nstack.close()
    bstack = ExitStack()
    gate = sb("gate", [P, 2, TOK], stack=bstack)
    yhi = sb("yhi", [P, 3 * HEADS, TOK], F32R, stack=bstack)
    ylo = sb("ylo", [P, 3 * HEADS, TOK], F32R, stack=bstack)
    bstack.close()
    ystack.close()
    mstack = ExitStack()
    mhi = sb("mhi", [P, KT, TOK], F32R, stack=mstack)
    mlo = sb("mlo", [P, KT, TOK], F32R, stack=mstack)
    part = sb("part", [P, 2, TOK], stack=mstack)
    mix = sb("mix", [P, 2, TOK], stack=mstack)
    rtm = sb("rtm", [P, 2, TOK], stack=mstack)
    mstack.close()
    fstack = ExitStack()
    fhi = sb("fhi", [P, FF // P, TOK], F32R, stack=fstack)
    flo = sb("flo", [P, FF // P, TOK], F32R, stack=fstack)
    frelu = sb("frelu", [P, 2, TOK], stack=fstack)
    fsq = sb("fsq", [P, 2, TOK], stack=fstack)
    rtf = sb("rtf", [P, 2, TOK], stack=fstack)
    sq = sb("sq", [P, 2, TOK], stack=fstack)
    sq_sum = sb("sq_sum", [P, TOK], stack=fstack)
    fstack.close()

    G = [ctx.enter_context(nc.psum_tensor(f"G{b}", [P, 512], F32)) for b in range(4)]
    X = [ctx.enter_context(nc.psum_tensor(f"X{b}", [P, 512], F32)) for b in range(4)]

    band_d = nc.dram_tensor("band_d", [DEPTH * HEADS, BAND], F32, kind="Internal").ap()
    bias_d = nc.dram_tensor("bias_d", [DEPTH * HEADS, P, W_BIAS], F32, kind="Internal").ap()

    raw_full = [sem(f"raw_full{s}") for s in range(RAW)]
    blk_hi = sem("blk_hi")
    blk_split = sem("blk_split")
    blk_used = sem("blk_used")
    acc_ready = sem("acc_ready")
    acc_free = [sem(f"acc_free{b}") for b in range(4)]
    act_own, dve_own, pool_own = sem("act_own"), sem("dve_own"), sem("pool_own")
    ada_full = [sem(f"ada_full{s}") for s in range(2)]
    ada0_full = [sem(f"ada0_full{s}") for s in range(ADA0)]
    ada_bfull, ada_used, ada_mm, ada_cp, ada_tr, mod_ready = (
        sem(n) for n in ("ada_bfull", "ada_used", "ada_mm", "ada_cp", "ada_tr", "mod_ready"))
    sq_ready, sq_used, moda_ready, std_ready, rstd_ready, hp_ready, hs_ready, hhi_ready, h_ready = (
        sem(n) for n in ("sq_ready", "sq_used", "moda_ready", "std_ready", "rstd_ready", "hp_ready", "hs_ready", "hhi_ready",
                            "h_ready"))
    ld_x, ld_c, ld_g, ld_rb, ld_k, consts = (sem(n) for n in ("ld_x", "ld_c", "ld_g", "ld_rb", "ld_k", "consts"))
    band_ready, band_out, mask_out, band_in = (sem(n) for n in ("band_ready", "band_out", "mask_out", "band_in"))
    csil_ready, pre_pe, pre_d, pre_a = (sem(n) for n in ("csil_ready", "pre_pe", "pre_d", "pre_a"))
    kc_full = [sem(f"kc_full{e}") for e in range(2)]
    vc_full, st_full, bias_full, dec_full = (sem(n) for n in ("vc_full", "st_full", "bias_full", "dec_full"))
    va_out, ka_out, st_out, stp_out, y_out = (sem(n) for n in ("va_out", "ka_out", "st_out", "stp_out", "y_out"))
    qk_msr, qk_pow, qk_norm, ta_done, qa_ev, ka_ev = (
        sem(n) for n in ("qk_msr", "qk_pow", "qk_norm", "ta_done", "qa_ev", "ka_ev"))
    kt_done = [sem(f"kt_done{e}") for e in range(2)]
    kt_a = [sem(f"kt_a{e}") for e in range(2)]
    kt_d = [sem(f"kt_d{e}") for e in range(2)]
    sp_done, sn_done, ss_done, sp_read, ss_read, maxp_ready, maxs_ready, exp_done = (
        sem(n) for n in ("sp_done", "sn_done", "ss_done", "sp_read", "ss_read", "maxp_ready", "maxs_ready", "exp_done"))
    rope_ready, tr_done, qr_ev, kr_ev, rs_done, sd_ready = (
        sem(n) for n in ("rope_ready", "tr_done", "qr_ev", "kr_ev", "rs_done", "sd_ready"))
    pt_done, pt_a, pt_d, pv_done, oa_ready, oaT_done, oaT_ev = (
        sem(n) for n in ("pt_done", "pt_a", "pt_d", "pv_done", "oa_ready", "oaT_done", "oaT_ev"))
    o_done, oss_ready, o_msr, o_pow, on_ready, orT_done, orT_ev = (
        sem(n) for n in ("o_done", "oss_ready", "o_msr", "o_pow", "on_ready", "orT_done", "orT_ev"))
    kdec_ready, kdm_ready, stp_done, stp_ev, pair_done, pair_ev = (
        sem(n) for n in ("kdec_ready", "kdm_ready", "stp_done", "stp_ev", "pair_done", "pair_ev"))
    yhi_ready, y_ready, mix_ready, mhi_ready, m_ready = (
        sem(n) for n in ("yhi_ready", "y_ready", "mix_ready", "mhi_ready", "m_ready"))
    dma_go = sem("dma_go")
    f_hi, f_ready, res_ready, fin_pe, fin_a, fin_d = (
        sem(n) for n in ("f_hi", "f_ready", "res_ready", "fin_pe", "fin_a", "fin_d"))

    block = ctx.enter_context(nc.Block())

    def seqs(ap):
        return ap.rearrange("p (b t) -> p b t", b=SB)

    def par(ap, e):
        return ap.rearrange("p (g e t) -> p g e t", g=4, e=2)[:, :, e, :]

    def ada0_load(eng, s):
        for k in range(2):
            eng.dma_start(ada0_w[:, s, k * 4:k * 4 + 4, :], w_ada[0, k * 4 * P:(k + 1) * 4 * P, s * ADA_C:(s + 1) * ADA_C]
                          .rearrange("(k p) n -> p k n", p=P)).then_inc(ada0_full[s], 16)
        eng.dma_start(ada0_b[:, s * ADA_C:(s + 1) * ADA_C], b_ada[0:1, s * ADA_C:(s + 1) * ADA_C]).then_inc(ada0_full[s], 16)

    def ada_load(eng, n, l, s, half):
        if half == 0:
            eng.wait_ge(ada_mm, n + ADA0)
            eng.dma_start(ada_b[:, :], (b_ada[l:l + 1] if isinstance(l, int) else b_ada[bass.ds(l, 1)])
                          [:, bass.ds(s * ADA_C, ADA_C)]).then_inc(ada_bfull, 16)
        for q in (2 * half, 2 * half + 1):
            eng.wait_ge(ada_used, n * 4 + (q + 1))
            eng.dma_start(ada_w[:, q % 2, :, :], w_ada[l, q * 2 * P:(q + 1) * 2 * P, bass.ds(s * ADA_C, ADA_C)]
                          .rearrange("(k p) n -> p k n", p=P)).then_inc(ada_full[q % 2], 16)

    def add_squares(eng, ops, n, k):
        eng.wait_ge(sq_ready, n * KT + (k + 2))
        if k == 0:
            ops.tensor_tensor(sq_sum[:, :], sq[:, 0, :], sq[:, 1, :], ALU.add).then_inc(sq_used, 2)
        else:
            for m in range(2):
                eng.wait_ge(sq_used, n * KT + (k + m))
                ops.tensor_tensor(sq_sum[:, :], sq_sum[:, :], sq[:, m, :], ALU.add).then_inc(sq_used, 1)

    @block.sync
    def _(sp):
        cnt = Counts(sp, None, ("blk", "ada", "head"))
        sp.dma_start(xtok[:, 0:2, :], x_prompt[0].rearrange("(t p) d -> p t d", p=P)).then_inc(ld_x, 16)
        sp.dma_start(xtok[:, 2, :], x_sample.rearrange("b t d -> (b t) d")).then_inc(ld_x, 16)
        sp.wait_ge(ld_c, 32)
        sp.wait_ge(ld_g, 6 * 16)
        for s in range(ADA0):
            ada0_load(sp, s)

        def load(c, j, parts):
            sp.wait_ge(blk_split, c.blk + (j + 1))
            off = 0
            for src in parts:
                w = src.shape[-1]
                sp.dma_start(raw[:, j % RAW, :, off:off + w], src.rearrange("(k p) n -> p k n", p=P))\
                    .then_inc(raw_full[j % RAW], 32 // len(parts))
                off += w

        def rows(w, l, k, c, n=BC):
            return w[l, k * BK * P:(k + 1) * BK * P, bass.ds(c, n)]

        with sp.Fori(0, DEPTH) as l:
            with sp.Fori(0, S_V.turns) as i, cnt.turn(S_V.adds) as c:
                for j in range(4):
                    load(c, j, [rows(w_in, l, j % 2, i * (2 * BC) + (C_VA + j // 2 * BC))])
            with sp.Fori(0, HEADS) as h, cnt.turn(S_HEAD.adds) as c:
                for j in range(2):
                    load(c, j, [rows(w_in, l, j, h * DH + C_QA, DH), rows(w_in, l, j, h * DH + C_KA, DH)])
                    if j == 0:
                        ada_load(sp, c.ada, l, h + 4, 0)
                for j in range(2):
                    load(c, 2 + j, [rows(w_in, l, j, h * DH + C_QR, DH), rows(w_in, l, j, h * DH + C_KR, DH)])
                sp.wait_ge(kt_done[1], c.head)
                for e in range(2):
                    for t in range(2):
                        src = cache_attn_k[l, e:SB:2, t * P:(t + 1) * P, bass.ds(h, 1), :]
                        sp.dma_start(kc[:, e, t, :, :], src.rearrange("b k h d -> k b (h d)")).then_inc(kc_full[e], 16)
                for j in range(2):
                    load(c, 4 + j, [rows(w_in, l, j, h * DV + C_VR)])
                sp.wait_ge(ss_read, c.head)
                sp.wait_ge(sp_read, c.head)
                sp.wait_ge(band_in, 20 * 16)
                sp.dma_start(bias[:, :], bias_d[bass.ds(l * HEADS + h, 1)].rearrange("a p n -> p (a n)")).then_inc(bias_full, 16)
                for j in range(2):
                    load(c, 6 + j, [rows(w_in, l, j, h * DV + C_ZR)])
                    if j == 0:
                        ada_load(sp, c.ada, l, h + 4, 1)
                sp.wait_ge(pv_done, c.head)
                for t in range(2):
                    src = cache_attn_v[l, :, t * P:(t + 1) * P, bass.ds(h, 1), :]
                    sp.dma_start(vc[:, t, :, :], src.rearrange("b k h d -> k b (h d)")).then_inc(vc_full, 16)
            with sp.Fori(0, S_MERGE.turns) as i, cnt.turn(S_MERGE.adds) as c:
                j = 0
                for g in range(2):
                    for w, base, ks in ((w_in, C_MR, 2), (w_br_ret, 0, 4), (w_in, C_MA, 2), (w_br_att, 0, 2)):
                        for k in range(ks):
                            load(c, j, [rows(w, l, k, i * (2 * BC) + (base + g * BC))])
                            j += 1
            with sp.Fori(0, S_OUT.turns) as i, cnt.turn(S_OUT.adds) as c:
                for j in range(4):
                    load(c, j, [rows(w_out, l, j % 2, i * (2 * BC) + j // 2 * BC)])
            with sp.Fori(0, S_UP.turns) as i, cnt.turn(S_UP.adds) as c:
                for j in range(4):
                    load(c, j, [rows(w_up, l, j % 2, i * (2 * BC) + j // 2 * BC)])
            with sp.Fori(0, S_DOWN.turns) as i, cnt.turn(S_DOWN.adds) as c:
                for j in range(8):
                    load(c, j, [rows(w_down, l, j, i * BC)])
                    if j in (1, 5):
                        ada_load(sp, c.ada, DEPTH - 1, i, j // 4)
        with cnt.turn({}, use=("blk",)) as c:
            load(c, 0, [w_in[0, 0:BK * P, 0:BC]])
        for t, dst in enumerate((y_prompt[0, 0:P, :], y_prompt[0, P:2 * P, :], y_sample.rearrange("b t d -> (b t) d"))):
            sp.wait_ge(fin_a, t + 1)
            sp.wait_ge(fin_d, t + 1)
            sp.dma_start(dst, xtok[:, t, :]).then_inc(y_out, 16)
        sp.wait_ge(y_out, 48)
        sp.wait_ge(raw_full[0], (DEPTH * 184 // RAW + 1) * 32)

    @block.gpsimd
    def _(pool):
        g = nc.gpsimd
        cnt = Counts(pool, pool_own, ("head", "norm", "own"))
        for m in (ident, ones, eps_t, mhalf, cT, qa_par, qr_par, p_par, neg):
            value = {"ones": 1.0, "eps_t": EPS, "mhalf": -0.5, "neg": NEG}.get(m.name, 0.0)
            ap = m[:, :] if len(m.shape) == 2 else m[:, :, :] if len(m.shape) == 3 else m[:, :, :, :]
            g.memset(ap, value).then_inc(pool_own, 1)
        pool.wait_ge(pool_own, 9)
        g.affine_select(out=ident[:, :], in_=ident[:, :], compare_op=ALU.not_equal, fill=1.0, base=0,
                        pattern=[[-1, P]], channel_multiplier=1).then_inc(consts, 1)
        pool.reg_add(cnt.regs["own"], cnt.regs["own"], 9)

        lh = DEPTH * HEADS
        for rows_, c0, n in ((CHUNK, B_Q0 + CHUNK, CHUNK), (CHUNK, B_Q1 + 3 * CHUNK, CHUNK), (P, B_N, P)):
            g.dma_start(bias_d[:, 0:rows_, c0:c0 + n].rearrange("l p n -> p l n"),
                        neg[0:rows_, 0:n].unsqueeze(1).to_broadcast([rows_, lh, n])).then_inc(mask_out, 16)
        pool.wait_ge(band_ready, 1)
        g.dma_start(band_d, band[:, :]).then_inc(band_out, 16)
        pool.wait_ge(band_out, 16)
        pool.wait_ge(mask_out, 48)

        def place(p0, n, c0, w, m0):
            src = bass.AP(tensor=band_d.tensor, offset=m0, ap=[[BAND, lh], [-1, n], [1, w]])
            g.dma_start(bias_d[:, p0:p0 + n, c0:c0 + w], src).then_inc(band_in, 16)

        at0 = BAND_TOP
        place(0, CHUNK, B_Q0, CHUNK, at0)
        place(CHUNK, CHUNK, B_Q0, P, at0 - CHUNK)
        place(0, CHUNK, B_Q1, 3 * CHUNK, at0 - P)
        place(CHUNK, CHUNK, B_Q1, SEQ, at0 - P - CHUNK)
        for b in range(SB):
            place(b * ST, ST, B_C, PAST, at0 - PAST)
            place(b * ST, ST, B_N + b * ST, ST, at0)

        def dma(out, in_):
            pool.sem_inc(dma_go, 1)
            return g.dma_start(out, in_)

        def norm_sample(c, shift):
            pool.wait_ge(moda_ready, c.norm + 1)
            pool.wait_ge(res_ready, c.norm * KT + R0)
            for k in range(KT):
                c.op(g.tensor_tensor(seqs(hs[:, k, :]), seqs(xT[:, k, PR:TOK]),
                                     modA[:, k, 1:NSEQ].unsqueeze(2).to_broadcast([P, SB, ST]), ALU.mult))
            c.settle()
            pool.wait_ge(rstd_ready, c.norm * 2 + 1)
            for k in range(KT + 1):
                if k < KT:
                    c.op(g.tensor_tensor(hs[:, k, :], hs[:, k, :], rstd[:, PR:TOK], ALU.mult))
                if k:
                    pool.wait_ge(pool_own, c.now["own"] + (c.mine - 1 if k < KT else c.mine))
                    d = seqs(hs[:, k - 1, :])
                    g.tensor_tensor(d, d, modT[:, shift * KT + k - 1, 1:NSEQ].unsqueeze(2).to_broadcast([P, SB, ST]),
                                    ALU.add).then_inc(hs_ready, 1)

        def store_prompt_state(c, l, h):
            pool.wait_ge(stp_ev, c.head)
            dma(st_prompt[l, 0, bass.ds(h, 1)].rearrange("a d v -> d (a v)"), stp[:, :]).then_inc(stp_out, 16)

        def store_sample_state(c, l, h):
            pool.wait_ge(pair_ev, c.head * 4 + P0)
            dma(st_sample[l, :, bass.ds(h, 1)].rearrange("b a d v -> d b (a v)"), st[:, :, :]).then_inc(st_out, 16)

        def power_o(c):
            pool.wait_ge(o_msr, c.head)
            g.tensor_tensor(o_rs, o_ms, mhalf[:, 0:3], ALU.pow).then_inc(o_pow, 1)

        def head(c, l, h, prev):
            H = c.head
            if prev is not None:
                power_o(c)
            if prev is not None:
                store_prompt_state(c, l, prev)
            pool.wait_ge(qk_msr, H + 1)
            g.tensor_tensor(qk_rs, qk_ms, mhalf[:, 0:6], ALU.pow).then_inc(qk_pow, 1)
            if prev is not None:
                store_sample_state(c, l, prev)
            pool.wait_ge(pair_ev, H * 4 + P0)
            dma(dec[:, :], decay[bass.ds(h, 1)].rearrange("a p n -> p (a n)")).then_inc(dec_full, 16)
            pool.wait_ge(qk_norm, H + 1)
            dma(k_prompt[l, 0, :, bass.ds(h, 1), :].rearrange("(t p) h d -> p t (h d)", p=P),
                qkA[:, 0:2, DH:2 * DH]).then_inc(ka_out, 16)
            dma(k_sample[l, :, :, bass.ds(h, 1), :].rearrange("b t h d -> (b t) (h d)"),
                qkA[:, 2, DH:2 * DH]).then_inc(ka_out, 16)
            pool.wait_ge(st_out, H * 16)
            for t in range(2):
                dma(st[:, 4 * t:4 * t + 4, :], state_ret[l, 4 * t:4 * t + 4, bass.ds(h, 1), :, :]
                    .rearrange("b h d v -> d b (h v)")).then_inc(st_full, 16)
            pool.wait_ge(rope_ready, H + 1)
            pool.wait_ge(dec_full, H * 16 + 16)
            pool.wait_ge(stp_done, H)
            g.tensor_tensor(kdec[:, :, :], qkR[:, 0:2, DH:2 * DH],
                            dec[:, DC_K:DC_K + 2].unsqueeze(2).to_broadcast([P, 2, DH]), ALU.mult).then_inc(kdec_ready, 1)
            pool.wait_ge(ss_done, H + 1)
            g.tensor_tensor(kdm, qkR[:, 2:3, DH:2 * DH].to_broadcast([P, SB, DH]),
                            dec[:, DC_SEQ:DC_SEQ + SB].unsqueeze(2).to_broadcast([P, SB, DH]), ALU.mult).then_inc(kdm_ready, 1)

        with pool.Fori(0, DEPTH) as l:
            with cnt.turn({"norm": 1}) as c:
                norm_sample(c, 0)
            with cnt.turn({"head": 1}) as c:
                head(c, l, 0, None)
            with pool.Fori(0, HEADS - 1) as h, cnt.turn({"head": 1}) as c:
                head(c, l, h + 1, h)
            with cnt.turn({}, use=("head",)) as c:
                power_o(c)
                store_prompt_state(c, l, HEADS - 1)
                store_sample_state(c, l, HEADS - 1)
            with cnt.turn({"norm": 1}) as c:
                pool.wait_ge(std_ready, c.norm)
                for k in (0, 2, 4):
                    add_squares(pool, g, c.norm, k)
                norm_sample(c, 3)
            with cnt.turn({}, use=("norm",)) as c:
                pool.wait_ge(std_ready, c.norm)
                for k in (0, 2, 4):
                    add_squares(pool, g, c.norm, k)
        pool.wait_ge(va_out, DEPTH * 32)
        pool.wait_ge(ka_out, DEPTH * HEADS * 32)
        pool.wait_ge(stp_out, DEPTH * HEADS * 16)
        pool.wait_ge(st_out, DEPTH * HEADS * 16)

    @block.scalar
    def _(act):
        a = nc.scalar
        cnt = Counts(act, act_own, Counts.NAMES)
        act.dma_start(crow[0:1, :], c_prompt).then_inc(ld_c, 16)
        act.dma_start(crow[1:NSEQ, :], c_sample).then_inc(ld_c, 16)
        for l in range(DEPTH):
            for src, r, n in ((norm_mix_g, 0, KT), (norm_ffn_g, KT, KT), (ret_gn_g, 2 * KT, 2 * KT)):
                act.dma_start(grow[32 * l + r:32 * l + r + n, :], src[l].rearrange("(k p) -> k p", p=P)).then_inc(ld_g, 16)
        act.dma_start(rbrow[:, :], rel_bias.rearrange("l h n -> (l h) n")).then_inc(ld_rb, 16)

        def copy(out, in_):
            return a.activation(out, in_, ACT.Copy)

        def high(c, j):
            act.wait_ge(raw_full[j % RAW], (c.round + j // RAW + 1) * 32)
            act.wait_ge(blk_used, c.blk + (j + 1))
            copy(whi[:, j % SPLIT, :, :], raw[:, j % RAW, :, :]).then_inc(blk_hi, 1)

        def acc(c, entry):
            _, _, kind, n = entry
            act.wait_ge(acc_ready, c.ready + n) if kind == "ready" else act.wait_ge(blk_used, c.blk + n)

        act.wait_ge(ld_c, 32)
        a.activation(csil[:, :], crow[:, :], ACT.Silu).then_inc(csil_ready, 1)
        for l in range(DEPTH):
            act.dma_start(gqk[:, l, 0:DH], q_norm_g[l].partition_broadcast(P)).then_inc(ld_k, 16)
            act.dma_start(gqk[:, l, DH:2 * DH], k_norm_g[l].partition_broadcast(P)).then_inc(ld_k, 16)
        act.dma_start(rope_t[:, :, :, :], rope).then_inc(ld_k, 16)
        for n in (1, 3, 5):
            act.wait_ge(pre_pe, n + 2)
            copy(xT[:, n % 2 * 4:n % 2 * 4 + 4, n // 2 * P:(n // 2 + 1) * P],
                 X[n % 4][:, :].rearrange("p (k t) -> p k t", k=4)).then_inc(pre_a, 1)

        def square(c, k0):
            act.wait_ge(sq_used, c.norm * KT + k0)
            for n in range(2):
                act.wait_ge(res_ready, c.norm * KT + (k0 + (n + 1)))
                a.activation(sq[:, n, :], xT[:, bass.ds(k0 + n, 1), :].rearrange("p a t -> p (a t)"), ACT.Square)\
                    .then_inc(sq_ready, 1)

        def norm(c, shift):
            c.op(a.activation(warm[:, :], eps_t[:, :], ACT.Sqrt))
            high(c, 1)
            square(c, KT - 2)
            act.wait_ge(sq_used, c.norm * KT + KT)
            act.wait_ge(ada_mm, ADA0)
            a.activation(std[:, :], X[0][:, 0:TOK], ACT.Sqrt, scale=1.0 / DM, bias=eps_t[:, 0:1]).then_inc(std_ready, 1)
            for k in range(KT):
                act.wait_ge(hp_ready, c.norm * KT + (k + 1))
                c.op(a.activation(hhi[:, k, 0:PR], hp[:, k % NS, :], ACT.Identity, bias=modT[:, shift * KT + k, 0:1]))
                act.wait_ge(hs_ready, c.norm * KT + (k + 1))
                copy(hhi[:, k, PR:TOK], hs[:, k, :]).then_inc(hhi_ready, 1)

        def squares(c):
            act.wait_ge(o_done, c.head)
            for t, src in enumerate((X[2][:, 0:DV], X[2][:, DV:2 * DV], X[0][:, 0:DV])):
                a.activation(onorm[:, t, :], src, ACT.Square, accum_out=o_ss[:, t:t + 1]).then_inc(oss_ready, 1)
            act.wait_ge(stp_done, c.head)
            copy(stp[:, :], X[1][:, 0:DV]).then_inc(stp_ev, 1)

        def attended(c, h):
            act.wait_ge(oaT_done, c.head)
            copy(y_att[:, bass.ds(h, 1), :].rearrange("p a t -> p (a t)"), X[3][:, 0:TOK]).then_inc(oaT_ev, 1)

        def head(c, h, prev):
            H = c.head
            gr = S_HEAD.groups

            def out_of(group, dst):
                for t, e in enumerate(group):
                    acc(c, e)
                    copy(dst[:, t, :], G[e[0]][:, 0:2 * DH]).then_inc(acc_free[e[0]], 1)

            def exponentials(lo, n, w):
                a.activation(prob[:, lo:lo + w], prob[:, lo:lo + w], ACT.Exp, bias=negmax[:, n:n + 1],
                             accum_out=rowsum[:, n:n + 1]).then_inc(exp_done, 1)

            high(c, 1)
            if prev is not None:
                squares(c)
            high(c, 2)
            if prev is not None:
                attended(c, prev)
            act.wait_ge(ta_done, H)
            act.wait_ge(ka_out, H * 32)
            out_of(gr[0], qkA)
            high(c, 3)
            high(c, 4)
            act.wait_ge(orT_ev, H * 2)
            out_of(gr[1], rraw)
            high(c, 5)
            act.wait_ge(ta_done, H + 1)
            c.op(copy(qaT[:, :], X[0][:, 0:TOK]))
            c.op(copy(par(qa_par[:, 0, :], 0), par(X[0][:, PR:TOK], 0)))
            copy(par(qa_par[:, 1, :], 1), par(X[0][:, PR:TOK], 1)).then_inc(qa_ev, 1)
            act.wait_ge(kt_done[0], H + 1)
            act.wait_ge(pair_done, H * 4 + P0)
            copy(kcT[:, :, P:2 * P], X[3][:, :].rearrange("p (g k) -> p g k", g=4)).then_inc(kt_a[0], 1)
            high(c, 6)
            act.wait_ge(kt_done[1], H + 1)
            act.wait_ge(sn_done, H + 1)
            copy(kcT[:, :, P:2 * P], X[1][:, :].rearrange("p (g k) -> p g k", g=4)).then_inc(kt_a[1], 1)
            act.wait_ge(maxp_ready, H + 1)
            exponentials(B_Q0, 0, P)
            exponentials(B_Q1, 1, SEQ)
            act.wait_ge(pair_done, H * 4 + P0)
            out_of(gr[2], vR)
            high(c, 7)
            act.wait_ge(tr_done, H + 1)
            copy(krT[:, :], X[1][:, 0:TOK]).then_inc(kr_ev, 1)
            act.wait_ge(maxs_ready, H + 1)
            exponentials(B_C, 2, PAST + P)
            high(c, 8)
            act.wait_ge(stp_out, H * 16)
            act.wait_ge(pt_done, H + 1)
            for e in range(2):
                c.op(copy(p_par[:, :, e, :].rearrange("p k (g e t) -> p k g e t", g=4, e=2)[:, :, :, e, :],
                          X[0][:, 0:2 * P].rearrange("p (k g e t) -> p k g e t", k=2, g=4, e=2)[:, :, :, e, :]))
            copy(pT[:, 0:2 * P], X[0][:, 2 * P:4 * P]).then_inc(pt_a, 1)
            for n, e in enumerate(gr[3]):
                acc(c, e)
                a.activation(zs[:, n, :], G[e[0]][:, 0:TOK], ACT.Silu).then_inc(acc_free[e[0]], 1)

        def branch_high(c, l, part):
            if part == 0:
                act.wait_ge(pv_done, c.head)
                act.wait_ge(kdm_ready, c.head)
                act.wait_ge(ka_out, c.head * 32)
                act.wait_ge(va_out, l * 32 + 32)
            if part == 3:
                act.wait_ge(orT_ev, c.head * 2)
            if part == 5:
                act.wait_ge(oaT_ev, c.head)
            for n in range(4 * part, 4 * part + 4):
                src = y_ret[:, n, :] if n < 2 * HEADS else y_att[:, n - 2 * HEADS, :]
                copy(yhi[:, n, :], src).then_inc(yhi_ready, 1)

        def merge(c, l, i, first):
            for j in range(20):
                high(c, j + 1)
                if first and j == 0:
                    squares(c)
                if first and j == 1:
                    attended(c, HEADS - 1)
                if first and j < 6:
                    branch_high(c, l, j)
                g, r = j // 10, j % 10
                if r in (1, 7):
                    for e in (S_MERGE.groups[4 * g + 1] if r == 7 else S_MERGE.groups[3] if g else []):
                        act.wait_ge(acc_free[e[0]], c.now[f"bank{e[0]}"] + (e[1] + 1))
                    if r == 1 and not g:
                        for b in (2, 3):
                            act.wait_ge(acc_free[b], c.now[f"bank{b}"])
                    for n, e in enumerate(S_MERGE.groups[4 * g + (2 if r == 7 else 0)]):
                        acc(c, e)
                        a.activation(gate[:, n, :], G[e[0]][:, 0:TOK], ACT.Sigmoid).then_inc(acc_free[e[0]], 1)
                if r == 9:
                    for n in range(2):
                        act.wait_ge(mix_ready, c.mix + (2 * g + n + 1))
                        copy(mhi[:, bass.ds(i * 4 + (2 * g + n), 1), :].rearrange("p a t -> p (a t)"),
                             mix[:, n, :]).then_inc(mhi_ready, 1)

        def up(c, i):
            for j in range(4):
                if not (isinstance(i, int) and i == j == 0):
                    high(c, j + 1)
                if j % 2:
                    for n, e in enumerate(S_UP.groups[j // 2]):
                        q = j // 2 * 2 + n
                        acc(c, e)
                        act.wait_ge(f_ready, c.ff + (q - 1 + F0))
                        a.activation(frelu[:, n, :], G[e[0]][:, 0:TOK], ACT.Relu).then_inc(acc_free[e[0]], 1)
                        act.wait_ge(acc_free[e[0]], c.now[f"bank{e[0]}"] + (e[1] + 1))
                        a.activation(fhi[:, bass.ds(i * 4 + q, 1), :].rearrange("p a t -> p (a t)"),
                                     frelu[:, n, :], ACT.Square).then_inc(f_hi, 1)

        def down(c, k0):
            for j in range(8):
                high(c, j + 1)
                if j == 0 and k0 is not None:
                    square(c, k0)

        act.wait_ge(pre_d, 5)
        act.wait_ge(consts, 1)
        with cnt.turn({}, use=("norm",)) as c:
            for k in (0, 2, 4):
                square(c, k)

        with cnt.turn({}, use=("blk", "round")) as c:
            high(c, 0)
        with act.Fori(0, DEPTH) as l:
            with cnt.turn({"norm": 1}, also=("blk", "round")) as c:
                norm(c, 0)
            for i in range(S_V.turns):
                with cnt.turn(S_V.adds) as c:
                    for j in range(4):
                        if i or j:
                            high(c, j + 1)
                        if j % 2:
                            for t, e in enumerate(S_V.groups[j // 2]):
                                acc(c, e)
                                copy(vaT[:, t, bass.ds(i * (2 * BC) + j // 2 * BC, BC)],
                                     G[e[0]][:, 0:BC]).then_inc(acc_free[e[0]], 1)
            with cnt.turn({}, use=("bank0", "bank1", "bank3")) as c:
                for b in (0, 1, 3):
                    act.wait_ge(acc_free[b], c.now[f"bank{b}"])
                act.dma_start(v_prompt[bass.ds(l, 1), 0].rearrange("l (t p) h d -> p (l t) (h d)", p=P),
                              vaT[:, 0:2, :]).then_inc(va_out, 16)
                act.dma_start(v_sample[bass.ds(l, 1)].rearrange("l b t h d -> (l b t) (h d)"),
                              vaT[:, 2, :]).then_inc(va_out, 16)
            with cnt.turn(S_HEAD.adds) as c:
                head(c, 0, None)
            with act.Fori(0, HEADS - 1) as h, cnt.turn(S_HEAD.adds) as c:
                head(c, h + 1, h)
            with cnt.turn(S_MERGE.adds, also=("head",)) as c:
                merge(c, l, 0, True)
            with act.Fori(0, S_MERGE.turns - 1) as i, cnt.turn(S_MERGE.adds) as c:
                merge(c, l, i + 1, False)
            for i in range(S_OUT.turns):
                with cnt.turn(S_OUT.adds, also=("norm",)) as c:
                    for j in range(4):
                        high(c, j + 1)
                        if i and j == 0:
                            square(c, 2)
                        if j == 2:
                            square(c, 4 * i)
            with cnt.turn({"norm": 1}, also=("blk", "round")) as c:
                norm(c, 3)
            with cnt.turn(S_UP.adds) as c:
                up(c, 0)
            with act.Fori(0, S_UP.turns - 1) as i, cnt.turn(S_UP.adds) as c:
                up(c, i + 1)
            with cnt.turn(S_DOWN.adds) as c:
                down(c, None)
            with act.Fori(0, S_DOWN.turns - 1) as i, cnt.turn(S_DOWN.adds, also=("norm",)) as c:
                down(c, i * 2)
        for n in (1, 3, 5):
            act.wait_ge(fin_pe, 4 + n // 2)
            copy(xtok[:, n // 2, 4 * P:8 * P], X[FIN_BANK[n]][:, :]).then_inc(fin_a, 1)
        act.wait_ge(va_out, DEPTH * 32)

    @block.vector
    def _(dve):
        v = nc.vector
        cnt = Counts(dve, dve_own, Counts.NAMES)
        dve.sem_inc(blk_split, RAW)
        dve.sem_inc(f_ready, F0)
        dve.sem_inc(pair_ev, P0)
        dve.sem_inc(h_ready, H0)
        dve.sem_inc(res_ready, R0)
        dve.sem_inc(m_ready, M0)

        def low(c, j):
            dve.wait_ge(blk_hi, c.blk + (j + 1))
            v.tensor_tensor(wlo[:, j % SPLIT, :, :], raw[:, j % RAW, :, :],
                            whi[:, j % SPLIT, :, :].bitcast(F32), ALU.subtract).then_inc(blk_split, 1)

        def acc(c, entry):
            _, _, kind, n = entry
            dve.wait_ge(acc_ready, c.ready + n) if kind == "ready" else dve.wait_ge(blk_used, c.blk + n)

        def copied(c, group):
            for b, use, _, _ in group:
                dve.wait_ge(acc_free[b], c.now[f"bank{b}"] + (use + 1))

        dve.wait_ge(ld_rb, 16)
        far = BAND_TOP - CLIP + 1
        v.tensor_copy(band[:, 0:far], rbrow[:, 2 * CLIP:2 * CLIP + 1].to_broadcast([DEPTH * HEADS, far])).then_inc(dve_own, 1)
        v.tensor_copy(band[:, far:BAND], rbrow[:, 0:2 * CLIP][:, ::-1]).then_inc(band_ready, 1)
        dve.reg_add(cnt.regs["own"], cnt.regs["own"], 1)
        dve.wait_ge(pre_pe, 1)
        v.tensor_copy(cT[:, :, 0:NSEQ], G[1][:, 0:KT * 16].rearrange("p (k b) -> p k b", k=KT)[:, :, 0:NSEQ]).then_inc(pre_d, 1)
        for n in (0, 2, 4):
            dve.wait_ge(pre_pe, n + 2)
            v.tensor_copy(xT[:, n % 2 * 4:n % 2 * 4 + 4, n // 2 * P:(n // 2 + 1) * P],
                          X[n % 4][:, :].rearrange("p (k t) -> p k t", k=4)).then_inc(pre_d, 1)
        dve.wait_ge(pre_pe, 8)
        v.tensor_copy(gT[:, :], G[0][:, 0:64]).then_inc(pre_d, 1)
        for k in (0, 2, 4):
            add_squares(dve, v, 0, k)
        dve.wait_ge(pre_a, 3)
        dve.wait_ge(ld_k, 80)

        def ada_rows(c, x):
            dve.wait_ge(ada_mm, c.ada + (ADA0 + 1))
            v.tensor_copy(ada_s[:, :], x[:, 0:P]).then_inc(ada_cp, 1)

        def ada_cols(c, s, x):
            dve.wait_ge(ada_tr, c.ada + (ADA0 + 1))
            v.tensor_copy(modT[:, bass.ds(s * 4, 4), :],
                          x[:, 0:P].rearrange("p (g b) -> p g b", g=4)[:, :, 0:NSEQ]).then_inc(mod_ready, 1)

        def norm(c, shift, gain):
            v.scalar_tensor_tensor(out=modA[:, :, :], in0=modT[:, (shift + 1) * KT:(shift + 2) * KT, :], scalar=1.0,
                                   in1=gT[:, gain].unsqueeze(2).to_broadcast([P, KT, NSEQ]), op0=ALU.add, op1=ALU.mult)\
                .then_inc(moda_ready, 1)
            low(c, 1)
            dve.wait_ge(std_ready, c.norm + 1)
            v.reciprocal(rstd[:, PR:TOK], std[:, PR:TOK]).then_inc(rstd_ready, 1)
            v.reciprocal(rstd[:, 0:PR], std[:, 0:PR]).then_inc(rstd_ready, 1)
            dve.wait_ge(rstd_ready, c.norm * 2 + 2)
            dve.wait_ge(moda_ready, c.norm + 1)
            for k in range(KT + 2):
                if k < KT:
                    if k >= NS:
                        dve.wait_ge(h_ready, c.norm * KT + (k - NS + 1 + H0))
                    v.scalar_tensor_tensor(out=hp[:, k % NS, :], in0=xT[:, k, 0:PR], scalar=modA[:, k, 0:1], in1=rstd[:, 0:PR],
                                           op0=ALU.mult, op1=ALU.mult).then_inc(hp_ready, 1)
                if k >= 2:
                    m = k - 2
                    dve.wait_ge(hhi_ready, c.norm * KT + (m + 1))
                    c.op(v.tensor_tensor(hlo[:, m, PR:TOK], hs[:, m, :], hhi[:, m, PR:TOK].bitcast(F32), ALU.subtract))
                    v.scalar_tensor_tensor(out=hlo[:, m, 0:PR], in0=hp[:, m % NS, :], scalar=modT[:, shift * KT + m, 0:1],
                                           in1=hhi[:, m, 0:PR].bitcast(F32), op0=ALU.add, op1=ALU.subtract).then_inc(h_ready, 1)

        def residual(c, x_tile, gate_of, e, t):
            acc(c, e)
            c.op(v.tensor_tensor(t[:, 0:PR], G[e[0]][:, 0:PR], gate_of[:, 0:1].to_broadcast([P, PR]), ALU.mult))
            v.tensor_tensor(seqs(t[:, PR:TOK]), seqs(G[e[0]][:, PR:TOK]),
                            gate_of[:, 1:NSEQ].unsqueeze(2).to_broadcast([P, SB, ST]), ALU.mult).then_inc(acc_free[e[0]], 1)
            dve.wait_ge(acc_free[e[0]], c.now[f"bank{e[0]}"] + (e[1] + 1))
            v.tensor_tensor(x_tile, x_tile, t, ALU.add).then_inc(res_ready, 1)

        def normed(c, l, h):
            dve.wait_ge(pv_done, c.head)
            c.op(v.tensor_copy(gcol[:, :], gT[:, bass.ds(l * 32 + h * 2 + 16, 2)]))
            c.settle()
            v.tensor_tensor(oa[:, :, :], X[3][:, 0:TOK].rearrange("p (t d) -> p t d", t=NT),
                            rinv.unsqueeze(2).to_broadcast([P, NT, DH]), ALU.mult).then_inc(oa_ready, 1)
            dve.wait_ge(oss_ready, c.head * 3)
            v.tensor_scalar(o_ms, o_ss, 1.0 / DV, EPS, ALU.mult, ALU.add).then_inc(o_msr, 1)
            dve.wait_ge(o_pow, c.head)
            c.op(v.tensor_tensor(onorm[:, 0:2, :], X[2][:, :].rearrange("p (t v) -> p t v", t=2),
                                 o_rs[:, 0:2].unsqueeze(2).to_broadcast([P, 2, DV]), ALU.mult))
            v.tensor_scalar(onorm[:, 2, :], X[0][:, 0:DV], o_rs[:, 2:3], None, ALU.mult).then_inc(on_ready, 1)

        def pair(c, q):
            dve.wait_ge(pair_done, c.head * 4 + (q + 1))
            s2 = st[:, 2 * q:2 * q + 2, :].rearrange("p b v -> p (b v)")
            v.scalar_tensor_tensor(out=s2, in0=s2, scalar=dec[:, DC_S:DC_S + 1], in1=X[PAIR_BANK[q]][:, :],
                                   op0=ALU.mult, op1=ALU.add).then_inc(pair_ev, 1)

        def gated(c, h):
            for b in (1, 2):
                dve.wait_ge(acc_free[b], c.now[f"bank{b}"])
            dve.wait_ge(orT_done, c.head)
            for n in range(2):
                v.scalar_tensor_tensor(out=y_ret[:, bass.ds(h * 2 + n, 1), :].rearrange("p a t -> p (a t)"),
                                       in0=X[2 * n][:, 0:TOK], scalar=gcol[:, n:n + 1], in1=zs[:, n, :],
                                       op0=ALU.mult, op1=ALU.mult).then_inc(orT_ev, 1)

        def head(c, l, h, prev):
            H = c.head
            gr = S_HEAD.groups
            low(c, 1)
            if prev is not None:
                normed(c, l, prev)
            low(c, 2)
            if prev is not None:
                pair(c, 0)
            low(c, 3)
            copied(c, gr[0])
            qk = qkA[:, :, :].rearrange("p t (a d) -> p (t a) d", a=2)
            tq = tmp[:, :].rearrange("p (a d) -> p a d", d=DH)
            c.op(v.tensor_tensor(tq, qk, qk, ALU.mult))
            c.settle()
            c.op(v.tensor_reduce(qk_ss, tq, axis=AXX, op=ALU.add))
            c.settle()
            v.tensor_scalar(qk_ms, qk_ss, 1.0 / DH, EPS, ALU.mult, ALU.add).then_inc(qk_msr, 1)
            if prev is not None:
                gated(c, prev)
                pair(c, 1)
            dve.wait_ge(qk_pow, H + 1)
            c.op(v.tensor_tensor(qk, qk, qk_rs.unsqueeze(2).to_broadcast([P, 6, DH]), ALU.mult))
            c.settle()
            v.tensor_tensor(qkA[:, :, :], qkA[:, :, :], gqk[:, bass.ds(l, 1), :].to_broadcast([P, NT, 2 * DH]),
                            ALU.mult).then_inc(qk_norm, 1)
            low(c, 4)
            if prev is not None:
                pair(c, 2)
                pair(c, 3)
            ada_rows(c, X[3])
            ada_cols(c, h + ADA0, X[3])
            dve.wait_ge(ta_done, H + 1)
            v.tensor_copy(kaT[:, :], X[1][:, 0:TOK]).then_inc(ka_ev, 1)
            low(c, 5)
            dve.wait_ge(kt_done[0], H + 1)
            v.tensor_copy(kcT[:, :, 0:P], X[2][:, :].rearrange("p (g k) -> p g k", g=4)).then_inc(kt_d[0], 1)
            copied(c, gr[1])
            dve.wait_ge(kdm_ready, H)
            half = DH // 2
            rr = qkZ[:, :].rearrange("p (t a h d) -> p t a h d", t=NT, a=2, h=2)
            ro = qkR[:, :, :].rearrange("p t (a h d) -> p t a h d", a=2, h=2)
            rt = tmp[:, :].rearrange("p (t a h d) -> p t a h d", t=NT, a=2, h=2)
            for t in range(NT):
                c.op(v.tensor_tensor(ro[:, t], rr[:, t], rope_t[:, t:t + 1, 0:1, :].to_broadcast([P, 2, 2, half]), ALU.mult))
                c.op(v.tensor_tensor(rt[:, t], rr[:, t, :, ::-1, :],
                                     rope_t[:, t:t + 1, 1:3, :].to_broadcast([P, 2, 2, half]), ALU.mult))
            c.settle()
            v.tensor_tensor(qkR[:, :, :], qkR[:, :, :], tmp[:, :].rearrange("p (t c) -> p t c", t=NT), ALU.add)\
                .then_inc(rope_ready, 1)
            low(c, 6)
            dve.wait_ge(kt_done[1], H + 1)
            dve.wait_ge(sn_done, H + 1)
            v.tensor_copy(kcT[:, :, 0:P], X[0][:, :].rearrange("p (g k) -> p g k", g=4)).then_inc(kt_d[1], 1)
            dve.wait_ge(sp_done, H + 1)
            dve.wait_ge(bias_full, H * 16 + 16)
            dve.wait_ge(orT_done, H)
            v.scalar_tensor_tensor(out=prob[:, 0:B_C], in0=X[3][:, 0:B_C], scalar=DH ** -0.5, in1=bias[:, 0:B_C],
                                   op0=ALU.mult, op1=ALU.add).then_inc(sp_read, 1)
            dve.wait_ge(sp_read, H + 1)
            c.op(v.tensor_reduce(negmax[:, 0:1], prob[:, B_Q0:B_Q0 + P], axis=AXX, op=ALU.max, negate=True))
            v.tensor_reduce(negmax[:, 1:2], prob[:, B_Q1:B_Q1 + SEQ], axis=AXX, op=ALU.max, negate=True).then_inc(maxp_ready, 1)
            low(c, 7)
            dve.wait_ge(ss_done, H + 1)
            v.scalar_tensor_tensor(out=prob[:, B_C:W_BIAS], in0=X[2][:, 0:PAST + P], scalar=DH ** -0.5,
                                   in1=bias[:, B_C:W_BIAS], op0=ALU.mult, op1=ALU.add).then_inc(ss_read, 1)
            dve.wait_ge(ss_read, H + 1)
            v.tensor_reduce(negmax[:, 2:3], prob[:, B_C:W_BIAS], axis=AXX, op=ALU.max, negate=True).then_inc(maxs_ready, 1)
            dve.wait_ge(tr_done, H + 1)
            dve.wait_ge(dec_full, H * 16 + 16)
            c.op(v.tensor_copy(qrT[:, :], X[0][:, 0:TOK]))
            row = dec[:, DC_ROW:DC_ROW + 64].rearrange("p (g t) -> p g t", g=4)
            c.op(v.tensor_tensor(par(qr_par[:, 0, :], 0), par(X[0][:, PR:TOK], 0), row, ALU.mult))
            v.tensor_tensor(par(qr_par[:, 1, :], 1), par(X[0][:, PR:TOK], 1), row, ALU.mult).then_inc(qr_ev, 1)
            low(c, 8)
            dve.wait_ge(rs_done, H + 1)
            v.tensor_tensor(sdT[:, :], X[2][:, :], dec[:, 0:512], ALU.mult).then_inc(sd_ready, 1)
            dve.wait_ge(pt_done, H + 1)
            v.tensor_copy(pT[:, 2 * P:4 * P], X[1][:, 0:2 * P]).then_inc(pt_d, 1)
            dve.wait_ge(exp_done, H * 3 + 3)
            c.op(v.reciprocal(rinv, rowsum))

        def branch_low(c, l, part):
            if part == 0:
                dve.wait_ge(stp_done, c.head)
            if part == 2:
                dve.wait_ge(pair_ev, c.head * 4 + P0)
                dve.wait_ge(stp_out, c.head * 16)
            if part == 4:
                dve.wait_ge(st_out, c.head * 16)
            for n in range(4 * part, 4 * part + 4):
                src = y_ret[:, n, :] if n < 2 * HEADS else y_att[:, n - 2 * HEADS, :]
                dve.wait_ge(yhi_ready, l * (3 * HEADS) + (n + 1))
                v.tensor_tensor(ylo[:, n, :], src, yhi[:, n, :].bitcast(F32), ALU.subtract).then_inc(y_ready, 1)

        def merge(c, l, i, first):
            for j in range(20):
                low(c, j + 1)
                if first and j == 0:
                    normed(c, l, HEADS - 1)
                    branch_low(c, l, 0)
                if first and j == 1:
                    pair(c, 0)
                    branch_low(c, l, 1)
                if first and j == 2:
                    gated(c, HEADS - 1)
                    pair(c, 1)
                if first and j == 3:
                    pair(c, 2)
                    pair(c, 3)
                    branch_low(c, l, 2)
                if first and j == 4:
                    branch_low(c, l, 3)
                if first and j == 5:
                    branch_low(c, l, 4)
                    branch_low(c, l, 5)
                    dve.wait_ge(y_ready, l * (3 * HEADS) + 3 * HEADS)
                g, r = j // 10, j % 10
                if r == 5:
                    copied(c, S_MERGE.groups[4 * g])
                    for n, e in enumerate(S_MERGE.groups[4 * g + 1]):
                        acc(c, e)
                        v.tensor_tensor(part[:, n, :], G[e[0]][:, 0:TOK], gate[:, n, :], ALU.mult).then_inc(acc_free[e[0]], 1)
                if r == 9:
                    copied(c, S_MERGE.groups[4 * g + 2])
                    for n, e in enumerate(S_MERGE.groups[4 * g + 3]):
                        acc(c, e)
                        v.tensor_tensor(mix[:, n, :], G[e[0]][:, 0:TOK], gate[:, n, :], ALU.mult).then_inc(acc_free[e[0]], 1)
                        dve.wait_ge(acc_free[e[0]], c.now[f"bank{e[0]}"] + (e[1] + 1))
                        v.tensor_tensor(mix[:, n, :], mix[:, n, :], part[:, n, :], ALU.add).then_inc(mix_ready, 1)
                    for n in range(2):
                        dve.wait_ge(mhi_ready, c.mix + (2 * g + n + 1))
                        kt = bass.ds(i * 4 + (2 * g + n), 1)
                        v.tensor_tensor(mlo[:, kt, :].rearrange("p a t -> p (a t)"), mix[:, n, :],
                                        mhi[:, kt, :].rearrange("p a t -> p (a t)").bitcast(F32),
                                        ALU.subtract).then_inc(m_ready, 1)

        def up(c, i):
            for j in range(4):
                if not (isinstance(i, int) and i == j == 0):
                    low(c, j + 1)
                if j % 2:
                    for n, e in enumerate(S_UP.groups[j // 2]):
                        q = j // 2 * 2 + n
                        copied(c, [e])
                        c.op(v.tensor_tensor(fsq[:, n, :], frelu[:, n, :], frelu[:, n, :], ALU.mult))
                        c.settle()
                        dve.wait_ge(f_hi, c.ff + (q + 1))
                        kt = bass.ds(i * 4 + q, 1)
                        v.tensor_tensor(flo[:, kt, :].rearrange("p a t -> p (a t)"), fsq[:, n, :],
                                        fhi[:, kt, :].rearrange("p a t -> p (a t)").bitcast(F32),
                                        ALU.subtract).then_inc(f_ready, 1)

        for s in range(ADA0):
            dve.wait_ge(ada_mm, s + 1)
            if s:
                dve.wait_ge(ada_tr, s)
            v.tensor_copy(ada_s[:, :], G[s][:, 0:P]).then_inc(ada_cp, 1)
            dve.wait_ge(ada_tr, s + 1)
            v.tensor_copy(modT[:, s * 4:s * 4 + 4, :],
                          G[s][:, 0:P].rearrange("p (g b) -> p g b", g=4)[:, :, 0:NSEQ]).then_inc(mod_ready, 1)
        with cnt.turn({}, use=("blk",)) as c:
            low(c, 0)
        with dve.Fori(0, DEPTH) as l:
            with cnt.turn({"norm": 1}, also=("blk", "ada")) as c:
                dve.wait_ge(mod_ready, c.ada + ADA0)
                norm(c, 0, bass.ds(l * 32, KT))
            for i in range(S_V.turns):
                with cnt.turn(S_V.adds) as c:
                    for j in range(4):
                        if i or j:
                            low(c, j + 1)
            with cnt.turn(S_HEAD.adds) as c:
                head(c, l, 0, None)
            with dve.Fori(0, HEADS - 1) as h, cnt.turn(S_HEAD.adds) as c:
                head(c, l, h + 1, h)
            with cnt.turn(S_MERGE.adds, also=("head",)) as c:
                merge(c, l, 0, True)
            with dve.Fori(0, S_MERGE.turns - 1) as i, cnt.turn(S_MERGE.adds) as c:
                merge(c, l, i + 1, False)
            with dve.Fori(0, S_OUT.turns) as i, cnt.turn(S_OUT.adds) as c:
                for j in range(4):
                    low(c, j + 1)
                    if j % 2:
                        for n, e in enumerate(S_OUT.groups[j // 2]):
                            q = i * 4 + (j // 2 * 2 + n)
                            residual(c, xT[:, bass.ds(q, 1), :].rearrange("p a t -> p (a t)"),
                                     modT[:, bass.ds(q + 2 * KT, 1), :].rearrange("p a b -> p (a b)"), e, rtm[:, n, :])
            with cnt.turn({"norm": 1}, also=("blk",)) as c:
                dve.wait_ge(res_ready, c.norm * KT + R0)
                norm(c, 3, bass.ds(l * 32 + KT, KT))
            with cnt.turn(S_UP.adds) as c:
                up(c, 0)
            with dve.Fori(0, S_UP.turns - 1) as i, cnt.turn(S_UP.adds) as c:
                up(c, i + 1)
            with dve.Fori(0, S_DOWN.turns) as i, cnt.turn(S_DOWN.adds) as c:
                for j in range(8):
                    low(c, j + 1)
                    if j == 5:
                        ada_rows(c, X[3])
                    if j == 6:
                        ada_cols(c, i, X[3])
                for n, e in enumerate(S_DOWN.groups[0]):
                    q = i * 2 + n
                    residual(c, xT[:, bass.ds(q, 1), :].rearrange("p a t -> p (a t)"),
                             modT[:, bass.ds(q + 5 * KT, 1), :].rearrange("p a b -> p (a b)"), e, rtf[:, n, :])
        for n in (0, 2, 4):
            dve.wait_ge(fin_pe, n // 2 + 1)
            v.tensor_copy(xtok[:, n // 2, 0:4 * P], X[FIN_BANK[n]][:, :]).then_inc(fin_d, 1)

    @block.tensor
    def _(pe):
        t = nc.tensor
        cnt = Counts(pe, None, tuple(n for n in Counts.NAMES if n != "own"))
        pe.sem_inc(blk_used, SPLIT)
        pe.sem_inc(ada_used, 2)
        pe.sem_inc(pair_done, P0)

        def turned(out, in_, k=P):
            return t.transpose(out, in_, ident[0:k, 0:k])

        pe.wait_ge(consts, 1)
        pe.wait_ge(csil_ready, 1)
        for k in range(KT):
            ins = turned(G[1][:, k * 16:k * 16 + NSEQ], csil[:, k * P:(k + 1) * P], NSEQ)
        ins.then_inc(pre_pe, 1)
        pe.wait_ge(ld_x, 32)
        for n in range(6):
            if n >= 4:
                pe.wait_ge(pre_d, 2) if n == 4 else pe.wait_ge(pre_a, 1)
            for k in range(4):
                kt = n % 2 * 4 + k
                ins = turned(X[n % 4][:, k * P:(k + 1) * P], xtok[:, n // 2, kt * P:(kt + 1) * P])
            ins.then_inc(pre_pe, 1)
        pe.wait_ge(ld_g, 6 * 16)
        turned(G[0][:, 0:64], grow[:, :], 64).then_inc(pre_pe, 1)
        pe.wait_ge(pre_d, 5)
        pe.wait_ge(pre_a, 3)

        def products(c, stage, j, banks, hi, lo, k0, first, last, normed=False):
            tokens = len(banks) == 3
            pe.wait_ge(blk_split, c.blk + (j + 1 + RAW))
            s = j % SPLIT
            if first:
                for b, use, _, _ in banks if normed else banks[:1]:
                    pe.wait_ge(acc_free[b], c.now[f"bank{b}"] + use if use else c.now[f"bank{b}"])
            order = [(n, k) for k in range(BK) for n in range(len(banks))] if normed else \
                [(n, k) for n in range(len(banks)) for k in range(BK)]
            for n, k in order:
                b, use = banks[n][:2]
                if normed and n == 0:
                    pe.wait_ge(h_ready, c.norm * KT + (k0 + k + 1))
                if first and n and k == 0 and not normed:
                    pe.wait_ge(acc_free[b], c.now[f"bank{b}"] + use if use else c.now[f"bank{b}"])
                for x, w in ((hi, whi), (lo, whi), (hi, wlo)):
                    start = first and k == 0 and x is hi and w is whi
                    stop = last and k == BK - 1 and w is wlo
                    if tokens:
                        ins = t.matmul(G[b][:, 0:BC], x[:, k0 + k, n * P:(n + 1) * P], w[:, s, k, :],
                                       start=start, stop=stop)
                    else:
                        ins = t.matmul(G[b][:, 0:TOK], w[:, s, k, n * P:(n + 1) * P], x[:, k0 + k, :],
                                       start=start, stop=stop)
                if k == BK - 1:
                    if n == len(banks) - 1:
                        ins.then_inc(blk_used, 1)
                    elif last:
                        ins.then_inc(acc_ready, 1)

        def norm(c):
            pe.wait_ge(std_ready, c.norm)
            pe.wait_ge(orT_ev, c.head * 2)
            pe.wait_ge(pair_ev, c.head * 4 + P0)
            pe.wait_ge(sq_used, c.norm * KT + KT - 2)
            t.matmul(X[0][:, 0:TOK], ones[:, :], sq_sum[:, :], start=True, stop=False)
            for n in range(2):
                pe.wait_ge(sq_ready, c.norm * KT + (KT - 1 + n))
                t.matmul(X[0][:, 0:TOK], ones[:, :], sq[:, n, :], start=False, stop=(n == 1)).then_inc(sq_used, 1)

        def ada_products(c, half):
            if half == 0:
                pe.wait_ge(mod_ready, c.ada + ADA0)
            else:
                pe.wait_ge(ada_bfull, c.ada * 16 + 16)
            for q in (2 * half, 2 * half + 1):
                pe.wait_ge(ada_full[q % 2], c.ada * 32 + (q // 2 * 16 + 16))
                for k in range(2):
                    for g in range(4):
                        ins = t.matmul(X[3][32 * g:32 * g + 32, 0:P], cT[:, 2 * q + k, :], ada_w[:, q % 2, k, g * P:(g + 1) * P],
                                       start=(q == 0 and k == 0), stop=False, skip_group_check=True)
                ins.then_inc(ada_used, 1)
            if half == 1:
                for g in range(4):
                    ins = t.matmul(X[3][32 * g:32 * g + 32, 0:P], ones[0:1, 0:32], ada_b[0:1, g * P:(g + 1) * P],
                                   start=False, stop=True, skip_group_check=True)
                ins.then_inc(ada_mm, 1)

        def ada_turned(c):
            pe.wait_ge(ada_cp, c.ada + (ADA0 + 1))
            turned(X[3][:, 0:P], ada_s[:, :]).then_inc(ada_tr, 1)

        def pair(c, q):
            x = X[PAIR_BANK[q]]
            mm(x[:, 0:DV], kdm[:, 2 * q, :], vR[:, 2, :])
            mm(x[:, DV:2 * DV], kdm[:, 2 * q + 1, :], vR[:, 2, :]).then_inc(pair_done, 1)

        def attended(c):
            pe.wait_ge(stp_ev, c.head)
            pe.wait_ge(kdm_ready, c.head)
            pair(c, 0)
            pe.wait_ge(oa_ready, c.head)
            for n in range(NT):
                ins = turned(X[3][:, n * P:(n + 1) * P], oa[:, n, :])
            ins.then_inc(oaT_done, 1)

        def retained(c):
            pe.wait_ge(pair_ev, c.head * 4 + 1)
            pair(c, 1)
            pe.wait_ge(on_ready, c.head)
            for r in range(2):
                for n in range(NT):
                    ins = turned(X[2 * r][:, n * P:(n + 1) * P], onorm[:, n, r * P:(r + 1) * P])
            ins.then_inc(orT_done, 1)

        def last_states(c):
            pe.wait_ge(orT_ev, c.head * 2)
            pair(c, 2)
            pair(c, 3)

        def mm(out, lhsT, rhs, start=True, stop=True):
            return t.matmul(out, lhsT, rhs, start=start, stop=stop, skip_group_check=True)

        def head(c, h, prev):
            H = c.head
            gr = S_HEAD.groups
            hd = bass.ds(h * DH, DH)

            def gemm(j):
                products(c, S_HEAD, j, gr[j // 2], hhi, hlo, j % 2 * BK, j % 2 == 0, j % 2 == 1)

            def cached_scores(e):
                for g in range(4):
                    ins = mm(X[2][32 * g:32 * g + 32, 0:PAST], qa_par[:, e, 32 * g:32 * g + 32], kcT[:, g, :],
                             start=(e == 0), stop=(e == 1))
                return ins

            def keys_turned(e, banks):
                pe.wait_ge(kc_full[e], H * 32 + 32)
                for kt in range(2):
                    for g in range(4):
                        ins = turned(X[banks[kt]][:, g * P:(g + 1) * P], kc[:, e, kt, g, :])
                ins.then_inc(kt_done[e], 1)

            gemm(0)
            if prev is not None:
                attended(c)
            gemm(1)
            if prev is not None:
                retained(c)
            pe.wait_ge(oaT_ev, H)
            ada_products(c, 0)
            gemm(2)
            if prev is not None:
                last_states(c)
            ada_products(c, 1)
            gemm(3)
            ada_turned(c)
            pe.wait_ge(qk_norm, H + 1)
            pe.wait_ge(pair_ev, H * 4 + P0)
            for n in range(NT):
                turned(X[0][:, n * P:(n + 1) * P], qkA[:, n, 0:DH])
            for n in range(NT):
                ins = turned(X[1][:, n * P:(n + 1) * P], qkA[:, n, DH:2 * DH])
            ins.then_inc(ta_done, 1)
            pe.wait_ge(mod_ready, c.ada + (ADA0 + 1))
            keys_turned(0, (2, 3))
            gemm(4)
            pe.wait_ge(qa_ev, H + 1)
            pe.wait_ge(ka_ev, H + 1)
            keys_turned(1, (0, 1))
            pe.wait_ge(kt_d[0], H + 1)
            pe.wait_ge(kt_a[0], H + 1)
            mm(X[2][:, PAST:PAST + P], qaT[:, PR:TOK], kaT[:, PR:TOK])
            cached_scores(0).then_inc(sn_done, 1)
            mm(X[3][:, 0:P], qaT[:, 0:P], kaT[:, 0:P])
            mm(X[3][:, P:3 * P], qaT[:, P:2 * P], kaT[:, 0:2 * P]).then_inc(sp_done, 1)
            gemm(5)
            pe.wait_ge(kt_d[1], H + 1)
            pe.wait_ge(kt_a[1], H + 1)
            cached_scores(1).then_inc(ss_done, 1)
            pe.wait_ge(rope_ready, H + 1)
            for n in range(NT):
                turned(X[0][:, n * P:(n + 1) * P], qkR[:, n, 0:DH])
            for n in range(NT):
                ins = turned(X[1][:, n * P:(n + 1) * P], qkR[:, n, DH:2 * DH])
            ins.then_inc(tr_done, 1)
            gemm(6)
            pe.wait_ge(ss_read, H + 1)
            pe.wait_ge(qr_ev, H + 1)
            pe.wait_ge(kr_ev, H + 1)
            mm(X[2][:, 0:256], krT[:, 0:P], qrT[:, 0:2 * P])
            mm(X[2][:, 256:384], krT[:, P:2 * P], qrT[:, P:2 * P])
            mm(X[2][:, 384:512], krT[:, PR:TOK], qrT[:, PR:TOK]).then_inc(rs_done, 1)
            pe.wait_ge(exp_done, H * 3 + 3)
            for n, at in enumerate((B_C, B_C + P, B_N, B_Q0)):
                turned(X[0][:, n * P:(n + 1) * P], prob[:, at:at + P])
            for n in range(2):
                ins = turned(X[1][:, n * P:(n + 1) * P], prob[:, B_Q1 + n * P:B_Q1 + (n + 1) * P])
            ins.then_inc(pt_done, 1)
            gemm(7)
            pe.wait_ge(pt_a, H + 1)
            pe.wait_ge(pt_d, H + 1)
            pe.wait_ge(sp_read, H + 1)
            pe.wait_ge(vc_full, H * 32 + 32)
            mm(X[3][:, 0:P], pT[:, P:2 * P], vaT[:, 0, hd])
            mm(X[3][:, P:2 * P], pT[:, 2 * P:3 * P], vaT[:, 0, hd], stop=False)
            mm(X[3][:, P:2 * P], pT[:, 3 * P:4 * P], vaT[:, 1, hd], start=False)
            mm(X[3][:, 2 * P:3 * P], pT[:, 0:P], vaT[:, 2, hd], stop=False)
            for kt in range(2):
                for e in range(2):
                    for g in range(4):
                        ins = mm(X[3][32 * g:32 * g + 32, 2 * P:3 * P], p_par[:, kt, e, 32 * g:32 * g + 32],
                                 vc[:, kt, 2 * g + e, :], start=False, stop=(kt == 1 and e == 1))
            ins.then_inc(pv_done, 1)
            pe.wait_ge(sd_ready, H + 1)
            for b in (0, 2, 3):
                pe.wait_ge(acc_free[b], c.now[f"bank{b}"] + ([e[1] for e in gr[2] if e[0] == b][0] + 1))
            mm(X[2][:, 0:DV], sdT[:, 0:P], vR[:, 0, :])
            mm(X[2][:, DV:2 * DV], sdT[:, P:2 * P], vR[:, 0, :], stop=False)
            mm(X[2][:, DV:2 * DV], sdT[:, 2 * P:3 * P], vR[:, 1, :], start=False)
            mm(X[0][:, 0:DV], sdT[:, 3 * P:4 * P], vR[:, 2, :], stop=False)
            pe.wait_ge(st_full, H * 32 + 32)
            for e in range(2):
                for g in range(4):
                    ins = mm(X[0][32 * g:32 * g + 32, 0:DV], qr_par[:, e, 32 * g:32 * g + 32], st[:, 2 * g + e, :],
                             start=False, stop=(e == 1))
            ins.then_inc(o_done, 1)
            pe.wait_ge(kdec_ready, H + 1)
            mm(X[1][:, 0:DV], kdec[:, 0, :], vR[:, 0, :], stop=False)
            mm(X[1][:, 0:DV], kdec[:, 1, :], vR[:, 1, :], start=False).then_inc(stp_done, 1)

        def merge(c, l, first):
            j = 0
            for g in range(2):
                for n, (hi, lo, k0, ks, y0) in enumerate(((hhi, hlo, 0, 2, None), (yhi, ylo, 0, 4, 0),
                                                          (hhi, hlo, 0, 2, None), (yhi, ylo, 2 * HEADS, 2, 2 * HEADS))):
                    for k in range(ks):
                        if y0 is not None:
                            pe.wait_ge(y_ready, l * (3 * HEADS) + (y0 + (k + 1) * BK))
                        products(c, S_MERGE, j, S_MERGE.groups[4 * g + n], hi, lo, k0 + k * BK, k == 0, k == ks - 1)
                        if first and j < 3:
                            (attended, retained, last_states)[j](c)
                        j += 1

        def up(c, first):
            for j in range(4):
                products(c, S_UP, j, S_UP.groups[j // 2], hhi, hlo, j % 2 * BK, j % 2 == 0, j % 2 == 1,
                         normed=first and j < 2)

        def down(c):
            for j in range(8):
                pe.wait_ge(f_ready, c.ff + (BK * j + 2))
                products(c, S_DOWN, j, S_DOWN.groups[0], fhi, flo, j * BK, j == 0, j == 7)
                if j in (2, 4):
                    ada_products(c, j // 4)
                if j == 5:
                    ada_turned(c)

        for s in range(ADA0 + 1):
            if s < ADA0:
                pe.wait_ge(ada0_full[s], 48)
                for k in range(KT + 1):
                    for g in range(4):
                        at = s * ADA_C + g * P
                        ins = mm(G[s][32 * g:32 * g + 32, 0:P], cT[:, k, :] if k < KT else ones[0:1, 0:32],
                                 ada0_w[:, s, k, g * P:(g + 1) * P] if k < KT else ada0_b[0:1, at:at + P],
                                 start=(k == 0), stop=(k == KT))
                ins.then_inc(ada_mm, 1)
            if s:
                pe.wait_ge(ada_cp, s)
                turned(G[s - 1][:, 0:P], ada_s[:, :]).then_inc(ada_tr, 1)
        with pe.Fori(0, DEPTH) as l:
            with cnt.turn({"norm": 1}, use=("norm", "head")) as c:
                norm(c)
            with pe.Fori(0, S_V.turns) as i, cnt.turn(S_V.adds, use=("blk", "bank0", "bank1", "bank2", "bank3", "norm")) as c:
                for j in range(4):
                    products(c, S_V, j, S_V.groups[j // 2], hhi, hlo, j % 2 * BK, j % 2 == 0, j % 2 == 1, normed=j < 2)
            with cnt.turn(S_HEAD.adds) as c:
                head(c, 0, None)
            with pe.Fori(0, HEADS - 1) as h, cnt.turn(S_HEAD.adds) as c:
                head(c, h + 1, h)
            with cnt.turn(S_MERGE.adds, also=("head",)) as c:
                merge(c, l, True)
            with pe.Fori(0, S_MERGE.turns - 1) as i, cnt.turn(S_MERGE.adds) as c:
                merge(c, l, False)
            with pe.Fori(0, S_OUT.turns) as i, cnt.turn(S_OUT.adds, also=("mix",)) as c:
                for j in range(4):
                    pe.wait_ge(m_ready, c.mix + j % 2 * BK)
                    products(c, S_OUT, j, S_OUT.groups[j // 2], mhi, mlo, j % 2 * BK, j % 2 == 0, j % 2 == 1)
            with cnt.turn({"norm": 1}, use=("norm", "head")) as c:
                norm(c)
            with cnt.turn(S_UP.adds, also=("norm",)) as c:
                up(c, True)
            with pe.Fori(0, S_UP.turns - 1) as i, cnt.turn(S_UP.adds, also=("norm",)) as c:
                up(c, False)
            with pe.Fori(0, S_DOWN.turns) as i, cnt.turn(S_DOWN.adds, also=("ff",)) as c:
                down(c)
        for n in (0, 2, 4, 1, 3, 5):
            pe.wait_ge(res_ready, 2 * DEPTH * KT + R0 - (0 if n % 2 else KT // 2))
            if n in (3, 5):
                pe.wait_ge(fin_d, 1 if n == 3 else 2)
            for k in range(4):
                ins = turned(X[FIN_BANK[n]][:, k * P:(k + 1) * P], xT[:, n % 2 * 4 + k, n // 2 * P:(n // 2 + 1) * P])
            ins.then_inc(fin_pe, 1)

    ctx.close()


_INS = ["x_prompt", "x_sample", "state_ret", "cache_attn_k", "cache_attn_v", "c_prompt", "c_sample", "w_ada", "b_ada",
        "norm_mix_g", "norm_ffn_g", "w_in", "ret_gn_g", "q_norm_g", "k_norm_g", "rel_bias", "w_br_ret", "w_br_att",
        "w_out", "w_up", "w_down"]
_OUTS = [(1, SEQ, DM), (SB, ST, DM), (DEPTH, 1, HEADS, DH, DV), (DEPTH, 1, SEQ, HEADS, DH), (DEPTH, 1, SEQ, HEADS, DH),
         (DEPTH, SB, HEADS, DH, DV), (DEPTH, SB, ST, HEADS, DH), (DEPTH, SB, ST, HEADS, DH)]


def kernel(**inputs):
    import numpy as _np
    import concourse.bacc as _bacc
    from concourse import mybir as _mybir
    from concourse.bass_utils import run_bass_kernel_spmd as _run

    nc = _bacc.Bacc("TRN2", target_bir_lowering=False, num_devices=1)
    rope, decay = tables()
    given = {**{n: inputs[n] for n in _INS}, "rope": rope, "decay": decay}
    arrays, args = {}, []
    for name, value in given.items():
        a = _np.ascontiguousarray(value)
        arrays[f"in_{name}_dram"] = a
        args.append(nc.dram_tensor(f"in_{name}_dram", a.shape, _mybir.dt.from_np(a.dtype), kind="ExternalInput").ap())
    for i, shape in enumerate(_OUTS):
        args.append(nc.dram_tensor(f"out_{i}_dram", shape, F32, kind="ExternalOutput").ap())
    trunk(nc, *args)
    r = _run(nc, [arrays], core_ids=[0])
    return tuple(r.results[0][f"out_{i}_dram"] for i in range(len(_OUTS)))
```
